# Optimizing a Trainium2 kernel written in Bass

```python
import math
import jax, jax.numpy as jnp
from jax import lax
import numpy as np

D_MODEL = 1024
BATCH = 1
SEQ = 256
DEPTH = 1

MEM_LEN = 256
EPS = 1e-6
S5_WIDTH = 512
S5_GROUP = 16
S5_GROUPS = S5_WIDTH // S5_GROUP
S5_STATE = 64
SGU_WIDTH = 1024
SGU_HEADS = 8
SGU_HEAD_DIM = SGU_WIDTH // SGU_HEADS
CHUNK = 128
XATTN_HEADS = 4
XATTN_HEAD_DIM = D_MODEL // XATTN_HEADS
D_FF = ((8 * D_MODEL // 3 + 255) // 256) * 256
OFF_U = S5_WIDTH
OFF_V = OFF_U + SGU_WIDTH
OFF_GA = OFF_V + SGU_WIDTH
OFF_GB = OFF_GA + D_MODEL
IN_COLS = OFF_GB + D_MODEL


def rms_norm(x, g):
    xf = x.astype(jnp.float32)
    y = xf * lax.rsqrt(jnp.mean(xf * xf, axis=-1, keepdims=True) + EPS)
    return (y * g.astype(jnp.float32)).astype(x.dtype)

def layer_norm(x, g, b):
    xf = x.astype(jnp.float32)
    mu = jnp.mean(xf, axis=-1, keepdims=True)
    xc = xf - mu
    y = xc * lax.rsqrt(jnp.mean(xc * xc, axis=-1, keepdims=True) + EPS)
    return (y * g.astype(jnp.float32) + b.astype(jnp.float32)).astype(x.dtype)

def _linear_recurrence(e1, e2):
    a1, b1 = e1
    a2, b2 = e2
    return a1 * a2, a2 * b1 + b2

def s5_scan(u, lam_re, lam_im, log_step, b_re, b_im, c_re, c_im, reverse):
    f32 = jnp.float32
    seq = u.shape[0]
    lam = lax.complex(lam_re.astype(f32), lam_im.astype(f32))
    step = jnp.exp(log_step.astype(f32))[:, None]
    lam_bar = jnp.exp(lam * step)
    b = lax.complex(b_re.astype(f32), b_im.astype(f32))
    b_bar = ((lam_bar - 1.0) / lam)[..., None] * b
    bu = jnp.einsum('gpc,lbgc->lbgp', b_bar, u.astype(jnp.complex64))
    a = jnp.broadcast_to(lam_bar[None, None], (seq, 1) + lam_bar.shape)
    _, states = lax.associative_scan(_linear_recurrence, (a, bu), axis=0, reverse=reverse)
    c = lax.complex(c_re.astype(f32), c_im.astype(f32))
    return jnp.einsum('gcp,lbgp->lbgc', c, states).real

def s5_branch(xa, lam_re, lam_im, log_step, b_re, b_im, c_re, c_im, d, w_glu):
    f32 = jnp.float32
    bsz, seq, _ = xa.shape
    u = xa.astype(f32).reshape(bsz, seq, S5_GROUPS, S5_GROUP).transpose(1, 0, 2, 3)
    y = d.astype(f32).reshape(S5_GROUPS, S5_GROUP) * u
    for direction, reverse in ((0, False), (1, True)):
        y = y + s5_scan(u, lam_re[direction], lam_im[direction], log_step[direction],
                        b_re[direction], b_im[direction], c_re[direction], c_im[direction],
                        reverse)
    y = jax.nn.gelu(y.transpose(1, 0, 2, 3).reshape(bsz, seq, S5_WIDTH))
    y = y * jax.nn.sigmoid(y @ w_glu.astype(f32))
    return y.astype(xa.dtype)

def sgu_branch(zu, zv, ln_g, ln_b, w_s, bias):
    bsz, seq, _ = zu.shape
    zu = jax.nn.gelu(zu)
    zv = layer_norm(jax.nn.gelu(zv), ln_g, ln_b)
    zv = zv.reshape(bsz, seq // CHUNK, CHUNK, SGU_HEADS, SGU_HEAD_DIM)
    sv = jnp.einsum('hts,bnshd->bnthd', w_s, zv) + bias.T[None, None, :, :, None]
    return zu * sv.reshape(bsz, seq, SGU_WIDTH)

def memory_cross_attention(hn, memn, w_q, w_k, w_v, w_o):
    bsz, seq, _ = hn.shape
    q = (hn @ w_q).reshape(bsz, seq, XATTN_HEADS, XATTN_HEAD_DIM)
    k = (memn @ w_k).reshape(bsz, MEM_LEN, XATTN_HEADS, XATTN_HEAD_DIM)
    v = (memn @ w_v).reshape(bsz, MEM_LEN, XATTN_HEADS, XATTN_HEAD_DIM)
    s = jnp.einsum('blhd,bmhd->bhlm', q, k).astype(jnp.float32) * (XATTN_HEAD_DIM ** -0.5)
    p = jax.nn.softmax(s, axis=-1).astype(v.dtype)
    o = jnp.einsum('bhlm,bmhd->blhd', p, v).reshape(bsz, seq, D_MODEL)
    return o @ w_o

def swiglu(hn, w_gate, w_up, w_down):
    return (jax.nn.silu(hn @ w_gate) * (hn @ w_up)) @ w_down

def first_inputs(seed: int = 0) -> dict:
    key = jax.random.key(seed)
    ks = iter(jax.random.split(key, 40))
    f32 = jnp.float32

    def nrm(shape, scale):
        return jax.random.normal(next(ks), shape, f32) * scale

    def gain(shape):
        return 1.0 + nrm(shape, 0.02)

    L, G, P, C, H = DEPTH, S5_GROUPS, S5_STATE, S5_GROUP, SGU_HEADS
    n_idx = jnp.arange(P, dtype=f32)
    lam_re = -0.5 + nrm((L, 2, G, P), 0.01)
    lam_im = math.pi * n_idx + nrm((L, 2, G, P), 0.01)
    log_step = jax.random.uniform(next(ks), (L, 2, G), f32, math.log(1e-3), math.log(1e-1))
    return {
        "x": nrm((BATCH, SEQ, D_MODEL), 1.0),
        "mem": nrm((BATCH, MEM_LEN, D_MODEL), 1.0),
        "mix_norm_g": gain((L, D_MODEL)),
        "w_in": nrm((L, D_MODEL, IN_COLS), D_MODEL ** -0.5),
        "s5_lam_re": lam_re,
        "s5_lam_im": lam_im,
        "s5_log_step": log_step,
        "s5_b_re": nrm((L, 2, G, P, C), (2 * C) ** -0.5),
        "s5_b_im": nrm((L, 2, G, P, C), (2 * C) ** -0.5),
        "s5_c_re": nrm((L, 2, G, C, P), (2 * P) ** -0.5),
        "s5_c_im": nrm((L, 2, G, C, P), (2 * P) ** -0.5),
        "s5_d": nrm((L, S5_WIDTH), 1.0),
        "s5_w_glu": nrm((L, S5_WIDTH, S5_WIDTH), S5_WIDTH ** -0.5),
        "sgu_ln_g": gain((L, SGU_WIDTH)),
        "sgu_ln_b": nrm((L, SGU_WIDTH), 0.02),
        "sgu_w": nrm((L, H, CHUNK, CHUNK), 0.5 * CHUNK ** -0.5),
        "sgu_bias": 1.0 + nrm((L, H, CHUNK), 0.02),
        "w_proj_a": nrm((L, S5_WIDTH, D_MODEL), S5_WIDTH ** -0.5),
        "w_proj_b": nrm((L, SGU_WIDTH, D_MODEL), SGU_WIDTH ** -0.5),
        "w_out": nrm((L, D_MODEL, D_MODEL), D_MODEL ** -0.5),
        "xattn_norm_g": gain((L, D_MODEL)),
        "mem_norm_g": gain((D_MODEL,)),
        "w_q": nrm((L, D_MODEL, D_MODEL), D_MODEL ** -0.5),
        "w_k": nrm((L, D_MODEL, D_MODEL), D_MODEL ** -0.5),
        "w_v": nrm((L, D_MODEL, D_MODEL), D_MODEL ** -0.5),
        "w_xo": nrm((L, D_MODEL, D_MODEL), D_MODEL ** -0.5),
        "ffn_norm_g": gain((L, D_MODEL)),
        "w_gate": nrm((L, D_MODEL, D_FF), D_MODEL ** -0.5),
        "w_up": nrm((L, D_MODEL, D_FF), D_MODEL ** -0.5),
        "w_down": nrm((L, D_FF, D_MODEL), D_FF ** -0.5),
        "final_norm_g": gain((D_MODEL,)),
    }

def first_block(x, mem, mix_norm_g, w_in, s5_lam_re, s5_lam_im, s5_log_step, s5_b_re, s5_b_im,
              s5_c_re, s5_c_im, s5_d, s5_w_glu, sgu_ln_g, sgu_ln_b, sgu_w, sgu_bias,
              w_proj_a, w_proj_b, w_out, xattn_norm_g, mem_norm_g, w_q, w_k, w_v, w_xo,
              ffn_norm_g, w_gate, w_up, w_down, final_norm_g):
    memn = rms_norm(mem, mem_norm_g)
    h = x
    for i in range(DEPTH):
        n = rms_norm(h, mix_norm_g[i])
        proj = n @ w_in[i]
        xa = proj[..., :OFF_U]
        zu = proj[..., OFF_U:OFF_V]
        zv = proj[..., OFF_V:OFF_GA]
        gate_a = jax.nn.sigmoid(proj[..., OFF_GA:OFF_GB])
        gate_b = jax.nn.sigmoid(proj[..., OFF_GB:])
        ya = s5_branch(xa, s5_lam_re[i], s5_lam_im[i], s5_log_step[i], s5_b_re[i], s5_b_im[i],
                       s5_c_re[i], s5_c_im[i], s5_d[i], s5_w_glu[i])
        yb = sgu_branch(zu, zv, sgu_ln_g[i], sgu_ln_b[i], sgu_w[i], sgu_bias[i])
        merged = gate_a * (ya @ w_proj_a[i]) + gate_b * (yb @ w_proj_b[i])
        h = h + merged @ w_out[i]
        h = h + memory_cross_attention(rms_norm(h, xattn_norm_g[i]), memn,
                                       w_q[i], w_k[i], w_v[i], w_xo[i])
        h = h + swiglu(rms_norm(h, ffn_norm_g[i]), w_gate[i], w_up[i], w_down[i])
    return rms_norm(h, final_norm_g)


DEPTH_2 = 2

HEAD_DIM = 64
NA_HEADS = 8
NA_WIDTH = NA_HEADS * HEAD_DIM
GRID_W = 64
NA_KH_MAX = 8
NA_KW = 16
NA_QCOLS = 16
NA_KCOLS = NA_QCOLS + NA_KW
SW_HEADS = 8
SW_KV_HEADS = 2
SW_GROUP = SW_HEADS // SW_KV_HEADS
SW_WIDTH = SW_HEADS * HEAD_DIM
SW_KV_WIDTH = SW_KV_HEADS * HEAD_DIM
SW_WINDOW = 128
SW_BLOCK = 128
ROT_DIM = HEAD_DIM // 4
ROPE_THETA = 500000.0
OFF_QNA = NA_WIDTH
OFF_KNA = 2 * NA_WIDTH
OFF_VNA = 3 * NA_WIDTH
OFF_QSW = OFF_VNA + SW_WIDTH
OFF_KSW = OFF_QSW + SW_KV_WIDTH
OFF_VSW = OFF_KSW + SW_KV_WIDTH
N_BRANCHES = 2
PROJ_COLS = OFF_VSW + N_BRANCHES * D_MODEL
D_FF_DENSE = 2816
N_EXPERTS = 8
TOP_K = 2
D_FF_EXPERT = 3584
N_DENSE_LAYERS = (DEPTH_2 + 1) // 2
N_MOE_LAYERS = DEPTH_2 // 2
DEEPNORM_ALPHA = (2 * DEPTH_2) ** 0.25
DEEPNORM_BETA = (8 * DEPTH_2) ** -0.25
LN_EPS = 1e-5
NEG_INF = -1e30


def layer_norm_2(x, g, b):
    xf = x.astype(jnp.float32)
    mu = jnp.mean(xf, axis=-1, keepdims=True)
    var = jnp.mean(jnp.square(xf - mu), axis=-1, keepdims=True)
    return ((xf - mu) * lax.rsqrt(var + LN_EPS)).astype(x.dtype) * g + b

def partial_rotary(x, pos):
    half = ROT_DIM // 2
    inv_freq = 1.0 / (ROPE_THETA ** (jnp.arange(0, ROT_DIM, 2, dtype=jnp.float32) / ROT_DIM))
    ang = pos.astype(jnp.float32)[:, None] * inv_freq[None, :]
    cos = jnp.cos(ang)[None, :, None, :]
    sin = jnp.sin(ang)[None, :, None, :]
    x1 = x[..., :half].astype(jnp.float32)
    x2 = x[..., half:ROT_DIM].astype(jnp.float32)
    rot = jnp.concatenate([x1 * cos - x2 * sin, x2 * cos + x1 * sin], axis=-1).astype(x.dtype)
    return jnp.concatenate([rot, x[..., ROT_DIM:]], axis=-1)

def neighbourhood_attention(q, k, v, rpb):
    B, S, H, D = q.shape
    rows = S // GRID_W
    kh = min(NA_KH_MAX, rows)
    n_cb = GRID_W // NA_QCOLS
    r = np.arange(rows)
    row_start = np.clip(r - kh // 2, 0, rows - kh)
    key_rows = row_start[:, None] + np.arange(kh)[None, :]
    cb_start = np.clip(np.arange(n_cb) * NA_QCOLS - NA_KW // 2, 0, GRID_W - NA_KCOLS)
    key_cols = cb_start[:, None] + np.arange(NA_KCOLS)[None, :]
    key_tok = (key_rows[:, None, :, None] * GRID_W + key_cols[None, :, None, :])
    key_tok = key_tok.reshape(rows, n_cb, kh * NA_KCOLS)
    kg = jnp.take(k, key_tok, axis=1)
    vg = jnp.take(v, key_tok, axis=1)
    qb = q.reshape(B, rows, n_cb, NA_QCOLS, H, D)
    s = jnp.einsum('brjqhd,brjkhd->brjhqk', qb, kg,
                   preferred_element_type=jnp.float32) * (D ** -0.5)
    qcol = np.arange(n_cb)[:, None] * NA_QCOLS + np.arange(NA_QCOLS)[None, :]
    qcs = np.clip(qcol - NA_KW // 2, 0, GRID_W - NA_KW)
    kcol = key_cols[:, None, :]
    valid = (kcol >= qcs[..., None]) & (kcol < qcs[..., None] + NA_KW)
    dr = key_rows - r[:, None] + (NA_KH_MAX - 1)
    dc = np.clip(kcol - qcol[..., None] + (NA_KW - 1), 0, 2 * NA_KW - 2)
    dri = dr[:, None, None, :, None]
    dci = dc[None, :, :, None, :]
    bias = rpb[:, dri, dci].astype(jnp.float32)
    mask = np.broadcast_to(valid[None, :, :, None, :], (rows, n_cb, NA_QCOLS, kh, NA_KCOLS))
    bias = jnp.where(mask[None], bias, NEG_INF)
    bias = bias.reshape(H, rows, n_cb, NA_QCOLS, kh * NA_KCOLS).transpose(1, 2, 0, 3, 4)
    p = jax.nn.softmax(s + bias[None], axis=-1)
    o = jnp.einsum('brjhqk,brjkhd->brjqhd', p.astype(v.dtype), vg)
    return o.reshape(B, S, H * D)

def sliding_window_attention(q, k, v, sink):
    B, S, HQ, D = q.shape
    nb = S // SW_BLOCK
    pad = ((0, 0), (SW_BLOCK, SW_BLOCK), (0, 0), (0, 0))
    kp = jnp.pad(k, pad).reshape(B, nb + 2, SW_BLOCK, SW_KV_HEADS, D)
    vp = jnp.pad(v, pad).reshape(B, nb + 2, SW_BLOCK, SW_KV_HEADS, D)
    kb = jnp.concatenate([kp[:, :-2], kp[:, 1:-1], kp[:, 2:]], axis=2)
    vb = jnp.concatenate([vp[:, :-2], vp[:, 1:-1], vp[:, 2:]], axis=2)
    qb = q.reshape(B, nb, SW_BLOCK, SW_KV_HEADS, SW_GROUP, D)
    s = jnp.einsum('bnqkgd,bnskd->bnkgqs', qb, kb,
                   preferred_element_type=jnp.float32) * (D ** -0.5)
    qpos = np.arange(SW_BLOCK)[:, None] + SW_BLOCK
    kpos = np.arange(3 * SW_BLOCK)[None, :]
    band = np.abs(qpos - kpos) <= SW_WINDOW
    kabs = np.arange(nb)[:, None, None] * SW_BLOCK + kpos[None] - SW_BLOCK
    valid = band[None] & (kabs >= 0) & (kabs < S)
    s = jnp.where(valid[None, :, None, None], s, NEG_INF)
    sink_logit = sink.astype(jnp.float32).reshape(SW_KV_HEADS, SW_GROUP)[None, None, :, :, None, None]
    m = jnp.maximum(jnp.max(s, axis=-1, keepdims=True), sink_logit)
    p = jnp.exp(s - m)
    denom = jnp.sum(p, axis=-1, keepdims=True) + jnp.exp(sink_logit - m)
    o = jnp.einsum('bnkgqs,bnskd->bnqkgd', (p / denom).astype(v.dtype), vb)
    return o.reshape(B, S, HQ * D)

def mixer_block(x, w_in, b_gate, rpb, sink, w_branch_na, w_branch_sw, w_out):
    B, S, _ = x.shape
    proj = x @ w_in
    q_na, k_na, v_na, q_sw, k_sw, v_sw, gate_logits = jnp.split(
        proj, [OFF_QNA, OFF_KNA, OFF_VNA, OFF_QSW, OFF_KSW, OFF_VSW], axis=-1)
    hs = lambda t, h: t.reshape(B, S, h, HEAD_DIM)
    y_na = neighbourhood_attention(hs(q_na, NA_HEADS), hs(k_na, NA_HEADS), hs(v_na, NA_HEADS), rpb)
    pos = jnp.arange(S, dtype=jnp.int32)
    qs = partial_rotary(hs(q_sw, SW_HEADS), pos)
    ks = partial_rotary(hs(k_sw, SW_KV_HEADS), pos)
    y_sw = sliding_window_attention(qs, ks, hs(v_sw, SW_KV_HEADS), sink)
    y_na = y_na @ w_branch_na
    y_sw = y_sw @ w_branch_sw
    gates = jax.nn.sigmoid((gate_logits + b_gate).astype(jnp.float32)).astype(x.dtype)
    g_na, g_sw = jnp.split(gates, N_BRANCHES, axis=-1)
    return (g_na * y_na + g_sw * y_sw) @ w_out

def swiglu_2(x, w_gate, w_up, w_down):
    return (jax.nn.silu(x @ w_gate) * (x @ w_up)) @ w_down

def moe_swiglu(x, w_router, w_gate, w_up, w_down):
    B, S, D = x.shape
    xt = x.reshape(B * S, D)
    logits = (xt @ w_router).astype(jnp.float32)
    top_vals, top_idx = lax.top_k(logits, TOP_K)
    top_w = jax.nn.softmax(top_vals, axis=-1)
    combine = jnp.sum(jax.nn.one_hot(top_idx, N_EXPERTS, dtype=jnp.float32) * top_w[..., None], axis=1)
    combine = combine.astype(x.dtype)
    y = jnp.zeros_like(xt)
    for e in range(N_EXPERTS):
        y = y + combine[:, e:e + 1] * swiglu_2(xt, w_gate[e], w_up[e], w_down[e])
    return y.reshape(B, S, D)

def second_inputs(seed: int = 0) -> dict:
    key = jax.random.key(seed)
    ks = jax.random.split(key, 24)
    f32 = jnp.float32
    nrm = lambda k, shape, scale: jax.random.normal(k, shape, f32) * scale
    beta = DEEPNORM_BETA
    col_scale = np.ones((PROJ_COLS,), np.float32)
    col_scale[OFF_KNA:OFF_VNA] = beta
    col_scale[OFF_KSW:OFF_VSW] = beta
    w_in = nrm(ks[1], (DEPTH_2, D_MODEL, PROJ_COLS), D_MODEL ** -0.5) * jnp.asarray(col_scale)
    return {
        "x": nrm(ks[0], (BATCH, SEQ, D_MODEL), 1.0),
        "emb_ln_g": 1.0 + nrm(ks[2], (D_MODEL,), 0.02),
        "emb_ln_b": nrm(ks[3], (D_MODEL,), 0.02),
        "w_in": w_in,
        "b_gate": nrm(ks[4], (DEPTH_2, N_BRANCHES * D_MODEL), 0.1),
        "na_rpb": nrm(ks[5], (DEPTH_2, NA_HEADS, 2 * NA_KH_MAX - 1, 2 * NA_KW - 1), 0.2),
        "sw_sink": nrm(ks[6], (DEPTH_2, SW_HEADS), 0.5),
        "w_branch_na": nrm(ks[7], (DEPTH_2, NA_WIDTH, D_MODEL), beta * NA_WIDTH ** -0.5),
        "w_branch_sw": nrm(ks[8], (DEPTH_2, SW_WIDTH, D_MODEL), beta * SW_WIDTH ** -0.5),
        "w_out": nrm(ks[9], (DEPTH_2, D_MODEL, D_MODEL), beta * D_MODEL ** -0.5),
        "ln1_g": 1.0 + nrm(ks[10], (DEPTH_2, D_MODEL), 0.02),
        "ln1_b": nrm(ks[11], (DEPTH_2, D_MODEL), 0.02),
        "ffn_w_gate": nrm(ks[12], (N_DENSE_LAYERS, D_MODEL, D_FF_DENSE), beta * D_MODEL ** -0.5),
        "ffn_w_up": nrm(ks[13], (N_DENSE_LAYERS, D_MODEL, D_FF_DENSE), beta * D_MODEL ** -0.5),
        "ffn_w_down": nrm(ks[14], (N_DENSE_LAYERS, D_FF_DENSE, D_MODEL), beta * D_FF_DENSE ** -0.5),
        "moe_router": nrm(ks[15], (N_MOE_LAYERS, D_MODEL, N_EXPERTS), D_MODEL ** -0.5),
        "moe_w_gate": nrm(ks[16], (N_MOE_LAYERS, N_EXPERTS, D_MODEL, D_FF_EXPERT), beta * D_MODEL ** -0.5),
        "moe_w_up": nrm(ks[17], (N_MOE_LAYERS, N_EXPERTS, D_MODEL, D_FF_EXPERT), beta * D_MODEL ** -0.5),
        "moe_w_down": nrm(ks[18], (N_MOE_LAYERS, N_EXPERTS, D_FF_EXPERT, D_MODEL), beta * D_FF_EXPERT ** -0.5),
        "ln2_g": 1.0 + nrm(ks[19], (DEPTH_2, D_MODEL), 0.02),
        "ln2_b": nrm(ks[20], (DEPTH_2, D_MODEL), 0.02),
    }

def second_block(x, emb_ln_g, emb_ln_b, w_in, b_gate, na_rpb, sw_sink, w_branch_na, w_branch_sw,
              w_out, ln1_g, ln1_b, ffn_w_gate, ffn_w_up, ffn_w_down, moe_router, moe_w_gate,
              moe_w_up, moe_w_down, ln2_g, ln2_b):
    x = layer_norm_2(x, emb_ln_g, emb_ln_b)
    for layer in range(DEPTH_2):
        m = mixer_block(x, w_in[layer], b_gate[layer], na_rpb[layer], sw_sink[layer],
                        w_branch_na[layer], w_branch_sw[layer], w_out[layer])
        x = layer_norm_2(DEEPNORM_ALPHA * x + m, ln1_g[layer], ln1_b[layer])
        i = layer // 2
        if layer % 2 == 0:
            f = swiglu_2(x, ffn_w_gate[i], ffn_w_up[i], ffn_w_down[i])
        else:
            f = moe_swiglu(x, moe_router[i], moe_w_gate[i], moe_w_up[i], moe_w_down[i])
        x = layer_norm_2(DEEPNORM_ALPHA * x + f, ln2_g[layer], ln2_b[layer])
    return x


def setup_inputs(seed=0):
    out = dict(first_inputs(seed))
    for name, value in second_inputs(seed + 1).items():
        if name != "x":
            out[name + "_2"] = value
    return out


def reference(
    x, mem, mix_norm_g, w_in, s5_lam_re, s5_lam_im, s5_log_step, s5_b_re, s5_b_im, s5_c_re,
    s5_c_im, s5_d, s5_w_glu, sgu_ln_g, sgu_ln_b, sgu_w, sgu_bias, w_proj_a, w_proj_b, w_out,
    xattn_norm_g, mem_norm_g, w_q, w_k, w_v, w_xo, ffn_norm_g, w_gate, w_up, w_down,
    final_norm_g, emb_ln_g_2, emb_ln_b_2, w_in_2, b_gate_2, na_rpb_2, sw_sink_2, w_branch_na_2,
    w_branch_sw_2, w_out_2, ln1_g_2, ln1_b_2, ffn_w_gate_2, ffn_w_up_2, ffn_w_down_2,
    moe_router_2, moe_w_gate_2, moe_w_up_2, moe_w_down_2, ln2_g_2, ln2_b_2,
):
    x = first_block(
        x, mem, mix_norm_g, w_in, s5_lam_re, s5_lam_im, s5_log_step, s5_b_re, s5_b_im, s5_c_re,
        s5_c_im, s5_d, s5_w_glu, sgu_ln_g, sgu_ln_b, sgu_w, sgu_bias, w_proj_a, w_proj_b, w_out,
        xattn_norm_g, mem_norm_g, w_q, w_k, w_v, w_xo, ffn_norm_g, w_gate, w_up, w_down,
        final_norm_g,
    )
    return second_block(
        x, emb_ln_g_2, emb_ln_b_2, w_in_2, b_gate_2, na_rpb_2, sw_sink_2, w_branch_na_2,
        w_branch_sw_2, w_out_2, ln1_g_2, ln1_b_2, ffn_w_gate_2, ffn_w_up_2, ffn_w_down_2,
        moe_router_2, moe_w_gate_2, moe_w_up_2, moe_w_down_2, ln2_g_2, ln2_b_2,
    )


_drawn_inputs = setup_inputs


def setup_inputs(seed=0):
    import zlib

    import numpy as np

    out = dict(_drawn_inputs(seed))
    spreads = {}
    factors = {'mix_norm_g': 4.813,
     's5_lam_re': 64.0,
     's5_lam_im': 25.248,
     's5_log_step': 28.939,
     's5_b_re': 40.496,
     's5_b_im': 40.928,
     's5_c_re': 40.96,
     's5_c_im': 40.208,
     'sgu_ln_g': 8.0,
     'sgu_ln_b': 8.0,
     'sgu_bias': 7.67,
     'xattn_norm_g': 8.0,
     'mem_norm_g': 8.0,
     'ffn_norm_g': 4.039,
     'final_norm_g': 2.759,
     'emb_ln_g_2': 2.87,
     'emb_ln_b_2': 2.811,
     'b_gate_2': 8.0,
     'na_rpb_2': 8.0,
     'sw_sink_2': 8.0,
     'w_branch_na_2': 3.361,
     'w_branch_sw_2': 4.879,
     'w_out_2': 2.759}
    for name, (base, spread) in spreads.items():
        noise = np.random.default_rng([zlib.crc32(name.encode()), seed]).standard_normal(out[name].shape)
        drawn = base * np.exp(spread * noise) if base else spread * noise
        out[name] = __import__('jax').numpy.asarray(drawn.astype(out[name].dtype))
    for name, factor in factors.items():
        out[name] = (out[name] * factor).astype(out[name].dtype)
    return out
```

```python
from contextlib import ExitStack

import numpy as np

import concourse.bass as bass
from concourse import mybir

P = 128
TOK = 256
TB = TOK // P
D = 1024
KD = D // P
SLOTS = 7
CHUNK_F = 2048
BANKS = 8
BF = 512

ALU = mybir.AluOpType
ACT = mybir.ActivationFunctionType
F32 = mybir.dt.float32
I32 = mybir.dt.int32
AX_X = mybir.AxisListType.X

S5_G, S5_P, S5_C = 32, 64, 16
PAIRS = S5_G // 2
BLK = 2 * PAIRS
FF_STEPS = 2816 // 256
MOE_E = 8
MOE_PER = 3584 // 256
MOE_STEPS = MOE_E * MOE_PER
ALPHA = 4.0 ** 0.25
EPS = 1e-6
LN_EPS = 1e-5
XSCALE = 256.0 ** -0.5
HSCALE = 64.0 ** -0.5
NORMS = ("x", "mem", "zv", "xattn", "ffn", "final", "emb", "ln1_0", "ln2_0", "ln1_1", "ln2_1")


def ffn_chunks(name, steps):
    out = [("k8", name + "_gate", 0), ("k8", name + "_up", 0)]
    for s in range(1, steps):
        out += [("k8", name + "_gate", s), ("k8", name + "_up", s), ("k2", name + "_down", s - 1)]
    return out + [("k2", name + "_down", steps - 1)]


def plan_chunks():
    c = [("k8", "w_in", i) for i in range(18)]
    c += [("k8", "w_k", i) for i in range(4)] + [("k8", "w_v", i) for i in range(4)]
    c += [("k8", "w_proj_b", i) for i in range(4)]
    c += [("k4", "s5_w_glu", 0)] + [("k4", "w_proj_a", i) for i in range(2)]
    c += [("k8", w, i) for w in ("w_out", "w_q", "w_xo") for i in range(4)]
    c += ffn_chunks("ffn", FF_STEPS)
    for layer in range(2):
        c += [("k8", f"w_in_{layer}", i) for i in range(17)]
        c += [("k4", f"w_na_{layer}", i) for i in range(2)] + [("k4", f"w_sw_{layer}", i) for i in range(2)]
        c += [("k8", f"w_out_{layer}", i) for i in range(4)]
        c += ffn_chunks("dense", FF_STEPS) if layer == 0 else ffn_chunks("moe", MOE_STEPS)
    return c


def plan_units():
    u = []

    def add(name, n):
        u.extend((name, i) for i in range(n))

    add("t_x", 4)
    add("t_mem", 4)
    add("xa", 2)
    add("zv", 4)
    add("t_b", 4)
    add("bu", BLK)
    add("zu", 4)
    add("ga", 4)
    add("gb", 4)
    add("k", 4)
    add("v", 4)
    add("sgu", 4)
    add("pb", 4)
    add("y", 4)
    add("glu", 2)
    add("pa", 4)
    add("out", 4)
    add("t_xattn", 4)
    add("q", 4)
    attention_units(u, "x", 4)
    add("xo", 4)
    add("t_ffn", 4)
    for m in range(2):
        add(f"t_in{m}", 4)
        add(f"projb{m}", 5)
        add(f"qk{m}", 4)
        add(f"ga{m}", 4)
        add(f"t_sw{m}", 3)
        add(f"gb{m}", 4)
        attention_units(u, f"na{m}", 8)
        attention_units(u, f"sw{m}", 8)
        add(f"bna{m}", 4)
        add(f"bsw{m}", 4)
        add(f"out{m}", 4)
        add(f"t_mid{m}", 4)
    add("router", 1)
    add("cb", 4)
    return u


def attention_units(u, name, heads):
    for i in range(heads + 2):
        if i < heads:
            u.append((name + "_s", i))
        if 0 <= i - 1 < heads:
            u.append((name + "_t", i - 1))
        if 0 <= i - 2 < heads:
            u.append((name + "_o", i - 2))


CHUNKS = plan_chunks()
CHUNK_AT = {c: n for n, c in enumerate(CHUNKS)}
UNITS = plan_units()
UNIT_AT = {u: n for n, u in enumerate(UNITS)}
assert len(CHUNKS) % SLOTS == 0 and len(CHUNK_AT) == len(CHUNKS) and len(UNIT_AT) == len(UNITS)


def build(nc, a, out, stop=None):
    with ExitStack() as ctx:
        def sb(name, shape, dt=F32):
            return ctx.enter_context(nc.sbuf_tensor(name, shape, dt))

        def sem(name):
            return ctx.enter_context(nc.semaphore(name))

        ring = sb("ring", [P, SLOTS, CHUNK_F])
        big = sb("big", [P, 16384])
        h = sb("h", [P, TB, D])
        xT = sb("xT", [P, KD, TOK])
        memT = sb("memT", [P, KD, TOK])
        r_zu = sb("r_zu", [P, 2048])
        r_zv = sb("r_zv", [P, 2048])
        r_ga = sb("r_ga", [P, 2048])
        r_gb = sb("r_gb", [P, 2048])
        r_k = sb("r_k", [P, 2048])
        r_v = sb("r_v", [P, 2048])
        uT = sb("uT", [P, 4, TOK])
        sguT = sb("sguT", [P, 8, P])
        ident = sb("ident", [P, P])
        gains = sb("gains", [P, 4, KD])
        s5d = sb("s5d", [P, 4])
        bgate = sb("bgate", [P, 2, 16])
        sink = sb("sink", [P, 2, 8])
        st = sb("st", [P, TB, 2, 6])
        mv = sb("mv", [P, TB, 2])
        ve = sb("ve", [P, TB])
        sd = sb("sd", [P, TB])
        rstd = sb("rstd", [P, TB])
        msq = sb("msq", [P, TB])
        lam_a = sb("lam_a", [P, 2, 2, BLK])
        scan_t = sb("scan_t", [P, 3, 2, BLK])
        mx = sb("mx", [P, 2, TB])
        negm = sb("negm", [P, 2, TB])
        ssum = sb("ssum", [P, 2, TB])
        rsum = sb("rsum", [P, 2, TB])
        esink = sb("esink", [P, 2, TB])
        rt = sb("rt", [P, 12, TB, 8])
        ones = sb("ones", [P, P])
        psum = ctx.enter_context(nc.psum_tensor("psum", [P, BANKS, BF], F32))

        def view(region, lo, size, pat, **kw):
            return region[:, lo:lo + size].rearrange(pat, **kw)

        x_mem = view(big, 0, 2048, "p (b d) -> p b d", b=TB)
        n_mem = view(big, 2048, 2048, "p (b d) -> p b d", b=TB)
        states = big[:, :].rearrange("p (t r k) -> p t r k", r=2, k=BLK)
        xn = view(r_gb, 0, 2048, "p (b d) -> p b d", b=TB)
        ln_v = view(r_k, 0, 2048, "p (a d) -> p a d", a=2)
        b_raw = view(r_zu, 0, 1024, "p (r k c) -> p r k c", r=2, k=BLK)
        pt = view(r_zu, 1024, 1024, "p (n k) -> p n k", k=BLK)
        b_tmp = view(r_v, 0, 1024, "p (r k c) -> p r k c", r=2, k=BLK)
        b_wide = view(r_ga, 0, 2048, "p (r k g c) -> p r k g c", r=2, k=BLK, g=2)
        b_wide_f = r_ga
        bT = view(r_v, 0, 2048, "p (n m) -> p n m", m=P)
        cw = xT[:, :, :].rearrange("p a t -> p (a t)").rearrange("p (r k m) -> p r k m", r=2, k=BLK)
        zuT = view(r_zu, 0, 2048, "p (k t) -> p k t", t=TOK)
        zv = view(r_zv, 0, 2048, "p (b d) -> p b d", b=TB)
        gaT = view(r_ga, 0, 2048, "p (k t) -> p k t", t=TOK)
        gbT = view(r_gb, 0, 2048, "p (k t) -> p k t", t=TOK)
        kT = view(r_k, 0, 2048, "p (k t) -> p k t", t=TOK)
        v_t = view(r_v, 0, 2048, "p (b d) -> p b d", b=TB)
        ygT = memT[:, 0:4, :]
        yaT = memT[:, 4:8, :]
        sbias = sb("sbias", [1, 8 * P])
        prob = view(r_zv, 0, 1024, "p (n b m) -> p n b m", n=2, b=TB)
        probT = view(r_zv, 1024, 1024, "p (n b l) -> p n b l", n=2, b=TB)
        logit = uT[:, :, :].rearrange("p a t -> p (a t)").rearrange("p (n b m) -> p n b m", n=2, b=TB)
        qT = zuT
        oT = xT
        silu = view(r_zu, 0, 1024, "p (n m) -> p n m", n=2)
        hT = view(r_zu, 1024, 1024, "p (n j t) -> p n j t", n=2, j=2)
        comb = view(r_ga, 0, 2048, "p (e t) -> p e t", e=MOE_E)
        cdiag = view(r_v, 0, 2048, "p (n m) -> p n m", m=P)
        nabias = [view(big, 4096 * m, 4096, "p (h b m) -> p h b m", h=8, b=TB) for m in range(2)]
        bc = view(big, 8192, 7168, "p (n d) -> p n d", d=D)
        swmask = big[:, 15360:15872].rearrange("p (b m) -> p b m", b=TB)
        rope = big[:, 15872:15904].rearrange("p (b c f) -> p b c f", b=TB, c=2)
        wr = big[:, 15904:15968].rearrange("p (k e) -> p k e", e=8)
        qk_t = view(r_gb, 0, 1536, "p (b d) -> p b d", b=TB)
        rtmp = view(r_zv, 0, 2048, "p (n b m) -> p n b m", n=8, b=TB)
        qnT = view(r_zu, 0, 1024, "p (k t) -> p k t", t=TOK)
        knT = view(r_zu, 1024, 1024, "p (k t) -> p k t", t=TOK)
        v_na = view(r_v, 0, 1024, "p (b d) -> p b d", b=TB)
        onT = view(r_v, 1024, 1024, "p (k t) -> p k t", t=TOK)
        qsT = view(r_k, 0, 1024, "p (k t) -> p k t", t=TOK)
        ksT = r_k[:, 1024:1280]
        v_sw = view(r_k, 1280, 256, "p (b d) -> p b d", b=TB)
        osT = view(memT[:, :, :].rearrange("p a t -> p (a t)"), 0, 1024, "p (k t) -> p k t", t=TOK)

        slot_full = [sem(f"slot_full{i}") for i in range(SLOTS)]
        chunk_used = sem("chunk_used")
        bank_full = [sem(f"bank_full{i}") for i in range(BANKS)]
        bank_free = [sem(f"bank_free{i}") for i in range(BANKS)]
        loads = {n: sem("ld_" + n) for n in (
            "x", "mem", "ident", "gains", "prm", "b", "lnv", "sgu", "sbias", "s5d", "cw", "bgate", "sink",
            "nab", "bc0", "bcn", "consts")}
        dve_step = sem("dve_step")
        scan_step = sem("scan_step")
        var_ready = sem("var_ready")
        std_ready = sem("std_ready")
        xn_ready = sem("xn_ready")
        memn_ready = sem("memn_ready")
        bwide_ready = sem("bwide_ready")
        prm_exp = sem("prm_ready")
        sin_ready = sem("sin_ready")
        zvn_ready = sem("zvn_ready")
        scan_done = sem("scan_done")
        cneg_ready = sem("cneg_ready")
        yg_ready = sem("yg_ready")
        ya_ready = sem("ya_ready")
        m_ready = sem("m_ready")
        negm_ready = sem("negm_ready")
        exp_ready = sem("exp_ready")
        prob_ready = sem("prob_ready")
        g_full = sem("gate_full")
        u_full = sem("up_full")
        silu_ready = sem("silu_ready")
        hT_ready = sem("hT_ready")
        moe_scaled = sem("moe_scaled")
        down_done = sem("down_done")
        acc_free = sem("acc_free")
        qk_roped = sem("qk_roped")
        rexp_in = sem("rexp_in")
        rexp_out = sem("rexp_out")
        diag_ready = sem("diag_ready")
        ones_ready = sem("ones_ready")
        out_ready = sem("out_ready")
        stored = sem("stored")

        def bank(u):
            return psum[:, UNIT_AT[u] % BANKS, :]

        def open_unit(pe, u):
            n = UNIT_AT[u]
            if n >= BANKS:
                pe.wait_ge(bank_free[n % BANKS], n // BANKS)

        def close_unit(last, u):
            last.then_inc(bank_full[UNIT_AT[u] % BANKS], 1)

        def take_unit(eng, u):
            n = UNIT_AT[u]
            eng.wait_ge(bank_full[n % BANKS], n // BANKS + 1)

        def free_unit(last, u):
            last.then_inc(bank_free[UNIT_AT[u] % BANKS], 1)

        def evacuated(eng, u):
            n = UNIT_AT[u]
            eng.wait_ge(bank_free[n % BANKS], n // BANKS + 1)

        def halves(ap):
            return ap.rearrange("p (b c) -> p b c", b=2)

        passes = [("x", 4)] + [(f"{k}{m}", 8) for m in range(2) for k in ("na", "sw")]
        head0 = {}
        n = 0
        for name, heads in passes:
            head0[name] = n
            n += heads
        ff0 = {"ffn": 0, "dense": FF_STEPS, "moe": 2 * FF_STEPS}
        ffn_no = {"ffn": 1, "dense": 2, "moe": 3}

        def sink_col(m, i):
            head = i // 2 + 4 * (i % 2)
            return sink[:, m, head:head + 1]

        block = ctx.enter_context(nc.Block())

        @block.sync
        def _(sp):
            for j in range(SLOTS):
                sp.dma_start(ring[:, j, :], a["stream"][j, :, :]).then_inc(slot_full[j], 16)
            with sp.Fori(1, len(CHUNKS) // SLOTS) as r:
                for j in range(SLOTS):
                    sp.wait_ge(chunk_used, r * SLOTS - SLOTS + j + 1)
                    sp.dma_start(ring[:, j, :], a["stream"][bass.ds(r * SLOTS + j, 1), :, :]
                                 .rearrange("a p f -> (a p) f")).then_inc(slot_full[j], 16)

        @block.gpsimd
        def _(pool):
            for q in range(4):
                take_unit(pool, ("y", q))
            for m in range(2):
                pool.dma_start(nabias[m], a["na_bias"][m]).then_inc(loads["nab"], 16)
            for n in range(7):
                pool.dma_start(bc[:, n, :], a["bc"][n:n + 1, :].to_broadcast([P, D])).then_inc(loads["bc0"], 16)
            pool.dma_start(swmask, a["sw_mask"]).then_inc(loads["consts"], 16)
            pool.dma_start(rope, a["rope"]).then_inc(loads["consts"], 16)
            pool.dma_start(wr, a["router"]).then_inc(loads["consts"], 16)
            for n in range(4):
                pool.wait_ge(xn_ready, 5 + n // 2)
                pool.dma_start(bc[:, 3 + n, :], a["bc"][7 + n:8 + n, :].to_broadcast([P, D])
                               ).then_inc(loads["bcn"], 16)

        @block.tensor
        def _(pe):
            def weights(c):
                n = CHUNK_AT[c]
                pe.wait_ge(slot_full[n % SLOTS], 16 * (n // SLOTS + 1))
                k = {"k8": KD, "k4": 4, "k2": 2}[c[0]]
                return ring[:, n % SLOTS, :].rearrange("p (k c) -> p k c", k=k)

            def release(first, chunk):
                if CHUNK_AT[chunk] > 0:
                    first.then_inc(chunk_used, 1)

            def transposes(u0, src, n_units=4):
                for u in range(n_units):
                    open_unit(pe, (u0, u))
                    for j in range(2):
                        for b in range(TB):
                            last = nc.tensor.transpose(
                                bank((u0, u))[:, (2 * j + b) * P:(2 * j + b + 1) * P],
                                src[:, b, (2 * u + j) * P:(2 * u + j + 1) * P], ident[:, :])
                    close_unit(last, (u0, u))

            def form_a(unit, chunk, act_T):
                open_unit(pe, unit)
                w = weights(chunk)
                for j in range(2):
                    for k in range(KD):
                        last = nc.tensor.matmul(bank(unit)[:, j * TOK:(j + 1) * TOK], w[:, k, j * P:(j + 1) * P],
                                                act_T[:, k, :], start=(k == 0), stop=(k == KD - 1))
                        if j == k == 0:
                            release(last, chunk)
                close_unit(last, unit)

            def form_a4(name, chunk, act_T, u0):
                w = weights(chunk)
                for u in range(2):
                    open_unit(pe, (name, u0 + u))
                    for j in range(2):
                        for k in range(4):
                            last = nc.tensor.matmul(
                                bank((name, u0 + u))[:, j * TOK:(j + 1) * TOK],
                                w[:, k, (2 * u + j) * P:(2 * u + j + 1) * P],
                                act_T[:, k, :], start=(k == 0), stop=(k == 3))
                            if u == j == k == 0:
                                release(last, chunk)
                    close_unit(last, (name, u0 + u))

            def form_b(unit, chunk, act_T):
                open_unit(pe, unit)
                w = weights(chunk)
                for b in range(TB):
                    for k in range(KD):
                        last = nc.tensor.matmul(bank(unit)[:, b * 256:(b + 1) * 256],
                                                act_T[:, k, b * P:(b + 1) * P], w[:, k, :],
                                                start=(k == 0), stop=(k == KD - 1))
                        if b == k == 0:
                            release(last, chunk)
                close_unit(last, unit)

            def attention(name, heads, kd, q_of, k_of, v_of, o_rows, dblocks):
                g0 = head0[name]
                for i in range(heads + 2):
                    if i < heads:
                        u = (name + "_s", i)
                        open_unit(pe, u)
                        for b in range(TB):
                            for k in range(kd):
                                last = nc.tensor.matmul(bank(u)[:, b * 256:(b + 1) * 256],
                                                        q_of(i, k)[:, b * P:(b + 1) * P], k_of(i, k),
                                                        start=(k == 0), stop=(k == kd - 1))
                        close_unit(last, u)
                    if 0 <= i - 1 < heads:
                        u = (name + "_t", i - 1)
                        g = g0 + i - 1
                        pe.wait_ge(prob_ready, g + 1)
                        open_unit(pe, u)
                        for m in range(TB):
                            for b in range(TB):
                                last = nc.tensor.transpose(
                                    bank(u)[:, (2 * m + b) * P:(2 * m + b + 1) * P],
                                    prob[:, g % 2, b, m * P:(m + 1) * P], ident[:, :])
                        close_unit(last, u)
                    if 0 <= i - 2 < heads:
                        u = (name + "_o", i - 2)
                        g = g0 + i - 2
                        evacuated(pe, (name + "_t", i - 2))
                        open_unit(pe, u)
                        r0, rn = o_rows(i - 2)
                        for j in range(dblocks):
                            for m in range(TB):
                                last = nc.tensor.matmul(bank(u)[r0:r0 + rn, j * TOK:(j + 1) * TOK],
                                                        v_of(i - 2, j, m), probT[:, g % 2, m, :],
                                                        start=(m == 0), stop=(m == TB - 1))
                        close_unit(last, u)

            def gate_up(name, s):
                for o, part, full in ((0, "_gate", g_full), (1, "_up", u_full)):
                    product_gu(2 * (s % 2) + o, weights(("k8", name + part, s)), full)

            def product_gu(b, w, full):
                for j in range(2):
                    for k in range(KD):
                        last = nc.tensor.matmul(psum[:, b, j * TOK:(j + 1) * TOK], w[:, k, j * P:(j + 1) * P],
                                                xT[:, k, :], start=(k == 0), stop=(k == KD - 1))
                        if j == k == 0:
                            last.then_inc(chunk_used, 1)
                last.then_inc(full, 1)

            def down(s, w, first, final):
                for k in range(2):
                    for b in range(TB):
                        for c in range(2):
                            last = nc.tensor.matmul(psum[:, 4 + 2 * b + c, :], hT[:, s % 2, k, b * P:(b + 1) * P],
                                                    w[:, k, c * 512:(c + 1) * 512],
                                                    start=(first and k == 0), stop=(final and k == 1),
                                                    skip_group_check=True)
                            if k == b == c == 0:
                                last.then_inc(chunk_used, 1)
                last.then_inc(down_done, 1)

            def all_banks_free(next_unit):
                n = next_unit
                for b in range(BANKS):
                    used = (n - b + BANKS - 1) // BANKS
                    if used > 0:
                        pe.wait_ge(bank_free[b], used)

            def ffn(name, steps, next_unit):
                f0 = ff0[name]
                all_banks_free(next_unit)
                for s in range(steps + 1):
                    if s < steps:
                        if s >= 2:
                            pe.wait_ge(hT_ready, f0 + s - 1)
                        gate_up(name, s)
                    if s >= 1:
                        pe.wait_ge(hT_ready, f0 + s)
                        down(s - 1, weights(("k2", name + "_down", s - 1)), s == 1, s == steps)

            pe.wait_ge(loads["ident"], 16)
            pe.wait_ge(xn_ready, 1)
            transposes("t_x", xn)
            pe.wait_ge(memn_ready, 1)
            transposes("t_mem", n_mem)
            evacuated(pe, ("t_x", 3))
            for i in range(2):
                form_a(("xa", i), ("k8", "w_in", i), xT)
            for i in range(4):
                form_b(("zv", i), ("k8", "w_in", 2 + i), xT)
            pe.wait_ge(bwide_ready, 1)
            for u in range(4):
                open_unit(pe, ("t_b", u))
                for j in range(4):
                    last = nc.tensor.transpose(bank(("t_b", u))[:, j * P:(j + 1) * P],
                                               b_wide_f[:, (4 * u + j) * P:(4 * u + j + 1) * P], ident[:, :])
                close_unit(last, ("t_b", u))
            evacuated(pe, ("t_b", 3))
            evacuated(pe, ("xa", 1))
            for blk in range(BLK):
                pair = blk % PAIRS
                r0 = 32 * (pair % 4)
                open_unit(pe, ("bu", blk))
                for r in range(2):
                    last = nc.tensor.matmul(bank(("bu", blk))[:, r * TOK:(r + 1) * TOK],
                                            bT[r0:r0 + 32, r * 8 + blk // 4, :],
                                            uT[r0:r0 + 32, pair // 4, :], start=True, stop=True)
                close_unit(last, ("bu", blk))
            for i in range(4):
                form_a(("zu", i), ("k8", "w_in", 6 + i), xT)
            for i in range(4):
                form_a(("ga", i), ("k8", "w_in", 10 + i), xT)
            for i in range(4):
                form_a(("gb", i), ("k8", "w_in", 14 + i), xT)
            evacuated(pe, ("t_mem", 3))
            for i in range(4):
                form_a(("k", i), ("k8", "w_k", i), memT)
            for i in range(4):
                form_b(("v", i), ("k8", "w_v", i), memT)
            pe.wait_ge(zvn_ready, 1)
            pe.wait_ge(loads["sgu"], 16)
            pe.wait_ge(loads["sbias"], 16)
            pe.wait_ge(ones_ready, 1)
            for u in range(4):
                open_unit(pe, ("sgu", u))
                for j in range(2):
                    hd = 2 * u + j
                    for b in range(TB):
                        o = bank(("sgu", u))[:, j * TOK + b * P:j * TOK + (b + 1) * P]
                        nc.tensor.matmul(o, zv[:, b, hd * P:(hd + 1) * P], sguT[:, hd, :], start=True, stop=False)
                        last = nc.tensor.matmul(o, ones[0:1, :], sbias[0:1, hd * P:(hd + 1) * P],
                                                start=False, stop=True)
                close_unit(last, ("sgu", u))
            evacuated(pe, ("sgu", 3))
            for i in range(4):
                form_a(("pb", i), ("k8", "w_proj_b", i), zuT)
            pe.wait_ge(scan_done, 1)
            pe.wait_ge(cneg_ready, 1)
            for q in range(4):
                open_unit(pe, ("y", q))
                for i in range(4):
                    pair = 4 * q + i
                    for n in range(4):
                        d, r = n // 2, n % 2
                        blk = d * PAIRS + pair
                        rhs = states[:, :, r, blk] if d == 0 else states[:, ::-1, r, blk]
                        last = nc.tensor.matmul(bank(("y", q))[32 * i:32 * i + 32, 0:TOK],
                                                cw[:, r, blk, :], rhs, start=(n == 0), stop=(n == 3))
                close_unit(last, ("y", q))
            pe.wait_ge(yg_ready, 4)
            form_a4("glu", ("k4", "s5_w_glu", 0), ygT, 0)
            pe.wait_ge(ya_ready, 2)
            for c in range(2):
                form_a4("pa", ("k4", "w_proj_a", c), yaT, 2 * c)
            pe.wait_ge(m_ready, 4)
            for i in range(4):
                form_b(("out", i), ("k8", "w_out", i), gaT)
            pe.wait_ge(xn_ready, 2)
            transposes("t_xattn", xn)
            evacuated(pe, ("t_xattn", 3))
            for i in range(4):
                form_a(("q", i), ("k8", "w_q", i), xT)
            evacuated(pe, ("q", 3))
            evacuated(pe, ("v", 3))
            attention("x", 4, 2, lambda i, k: qT[:, 2 * i + k, :], lambda i, k: kT[:, 2 * i + k, :],
                      lambda i, j, m: v_t[:, m, (2 * i + j) * P:(2 * i + j + 1) * P], lambda i: (0, P), 2)
            evacuated(pe, ("x_o", 3))
            for i in range(4):
                form_b(("xo", i), ("k8", "w_xo", i), oT)
            pe.wait_ge(xn_ready, 3)
            transposes("t_ffn", xn)
            evacuated(pe, ("t_ffn", 3))
            ffn("ffn", FF_STEPS, UNIT_AT[("t_in0", 0)])

            for m in range(2):
                pe.wait_ge(acc_free, 1 + m)
                pe.wait_ge(xn_ready, 4 + 2 * m)
                transposes(f"t_in{m}", h)
                evacuated(pe, (f"t_in{m}", 3))
                for i in range(5):
                    form_b((f"projb{m}", i), ("k8", f"w_in_{m}", i), xT)
                for i in range(4):
                    form_a((f"qk{m}", i), ("k8", f"w_in_{m}", 5 + i), xT)
                for i in range(4):
                    form_a((f"ga{m}", i), ("k8", f"w_in_{m}", 9 + i), xT)
                pe.wait_ge(qk_roped, m + 1)
                for u in range(3):
                    open_unit(pe, (f"t_sw{m}", u))
                    for j in range(2 if u < 2 else 1):
                        for b in range(TB):
                            last = nc.tensor.transpose(
                                bank((f"t_sw{m}", u))[:, (2 * j + b) * P:(2 * j + b + 1) * P],
                                qk_t[:, b, (2 * u + j) * P:(2 * u + j + 1) * P], ident[:, :])
                    close_unit(last, (f"t_sw{m}", u))
                for i in range(4):
                    form_a((f"gb{m}", i), ("k8", f"w_in_{m}", 13 + i), xT)
                evacuated(pe, (f"qk{m}", 3))
                evacuated(pe, (f"t_sw{m}", 2))
                attention(f"na{m}", 8, 1,
                          lambda i, k: qnT[64 * (i % 2):64 * (i % 2) + 64, i // 2, :],
                          lambda i, k: knT[64 * (i % 2):64 * (i % 2) + 64, i // 2, :],
                          lambda i, j, mb: v_na[:, mb, i * 64:(i + 1) * 64], lambda i: (64 * (i % 2), 64), 1)
                attention(f"sw{m}", 8, 1,
                          lambda i, k: qsT[64 * (i % 2):64 * (i % 2) + 64, i // 2, :],
                          lambda i, k: ksT[64 * (i % 2):64 * (i % 2) + 64, :],
                          lambda i, j, mb: v_sw[:, mb, (i % 2) * 64:(i % 2) * 64 + 64],
                          lambda i: (64 * (i % 2), 64), 1)
                evacuated(pe, (f"na{m}_o", 7))
                for c in range(2):
                    form_a4(f"bna{m}", ("k4", f"w_na_{m}", c), onT, 2 * c)
                evacuated(pe, (f"sw{m}_o", 7))
                for c in range(2):
                    form_a4(f"bsw{m}", ("k4", f"w_sw_{m}", c), osT, 2 * c)
                pe.wait_ge(m_ready, 4 + 4 * (m + 1))
                for i in range(4):
                    form_b((f"out{m}", i), ("k8", f"w_out_{m}", i), gaT)
                pe.wait_ge(xn_ready, 5 + 2 * m)
                transposes(f"t_mid{m}", h)
                evacuated(pe, (f"t_mid{m}", 3))
                if m == 0:
                    ffn("dense", FF_STEPS, UNIT_AT[("t_in1", 0)])

            pe.wait_ge(loads["consts"], 48)
            open_unit(pe, ("router", 0))
            for b in range(TB):
                for k in range(KD):
                    last = nc.tensor.matmul(bank(("router", 0))[:, b * 8:(b + 1) * 8], xT[:, k, b * P:(b + 1) * P],
                                            wr[:, k, :], start=(k == 0), stop=(k == KD - 1))
            close_unit(last, ("router", 0))
            pe.wait_ge(diag_ready, 1)
            for u in range(4):
                open_unit(pe, ("cb", u))
                for n in range(4):
                    last = nc.tensor.matmul(bank(("cb", u))[:, n * P:(n + 1) * P], ones[:, :],
                                            cdiag[:, 4 * u + n, :], start=True, stop=True)
                close_unit(last, ("cb", u))
            all_banks_free(len(UNITS))
            f0 = ff0["moe"]
            c0 = CHUNK_AT[("k8", "moe_gate", 0)]
            assert c0 % SLOTS == 0

            gate_up("moe", 0)

            def moe_step(par, n, rnd, hr, first):
                if not first:
                    pe.wait_ge(hT_ready, hr - 1)
                for o, full in ((0, g_full), (1, u_full)):
                    pe.wait_ge(slot_full[(n + o) % SLOTS], rnd(n + o))
                    product_gu(2 * par + o, ring[:, (n + o) % SLOTS, :].rearrange("p (k c) -> p k c", k=KD), full)
                pe.wait_ge(hT_ready, hr)
                pe.wait_ge(slot_full[(n + 2) % SLOTS], rnd(n + 2))
                down(1 - par, ring[:, (n + 2) % SLOTS, :].rearrange("p (k c) -> p k c", k=2), first, False)

            r0 = c0 // SLOTS
            moe_step(1, 2, lambda n: 16 * (r0 + n // SLOTS + 1), f0 + 1, True)
            turns = (MOE_STEPS - 2) // 14
            with pe.Fori(0, turns) as t:
                for i in range(14):
                    moe_step(i % 2, 5 + 3 * i, lambda n: t * (16 * 6) + 16 * (r0 + n // SLOTS + 1),
                             t * 14 + (f0 + 2 + i), False)
            for s in range(2 + 14 * turns, MOE_STEPS):
                moe_step(s % 2, 3 * s - 1, lambda n: 16 * (r0 + n // SLOTS + 1), f0 + s, False)
            pe.wait_ge(hT_ready, f0 + MOE_STEPS)
            down(MOE_STEPS - 1, weights(("k2", "moe_down", MOE_STEPS - 1)), False, True)

        @block.scalar
        def _(act):
            def load(dst, src, name):
                act.dma_start(dst, src).then_inc(loads[name], 16)

            load(h[:, :, :], a["x"].rearrange("a (b p) d -> p (a b) d", p=P), "x")
            load(x_mem, a["mem"].rearrange("a (b p) d -> p (a b) d", p=P), "mem")
            load(ident[:, :], a["ident"], "ident")
            load(gains[:, :, :], a["gains"], "gains")
            load(pt[:, 0:3, :], a["s5_prm"], "prm")
            load(b_raw, a["s5_b"], "b")
            load(ln_v, a["sgu_ln"].rearrange("(o a) d -> o a d", o=1).to_broadcast([P, 2, D]), "lnv")
            load(sguT[:, :, :], a["sgu_w"], "sgu")
            load(sbias[:, :], a["sgu_bias"], "sbias")
            load(s5d[:, :], a["s5_d"], "s5d")
            load(bgate[:, :, :], a["b_gate"], "bgate")
            load(sink[:, :, :], a["sink"].rearrange("(o a) d -> o a d", o=1).to_broadcast([P, 2, 8]), "sink")

            stds = [0]

            def std():
                stds[0] += 1
                act.wait_ge(var_ready, stds[0])
                nc.scalar.activation(sd[:, :], ve[:, :], ACT.Sqrt).then_inc(std_ready, 1)

            def copy_T(u0, dst, gain=None):
                for u in range(4):
                    take_unit(act, (u0, u))
                    for j in range(2):
                        src = bank((u0, u))[:, j * TOK:(j + 1) * TOK]
                        k = 2 * u + j
                        if gain is None:
                            last = nc.scalar.activation(dst[:, k, :], src, ACT.Copy)
                        else:
                            last = nc.scalar.activation(dst[:, k, :], src, ACT.Identity,
                                                        scale=gains[:, gain, k:k + 1])
                    free_unit(last, (u0, u))

            def out_of(u, dst, func):
                take_unit(act, u)
                free_unit(nc.scalar.activation(dst, halves(bank(u)), func), u)

            def attention(name, heads, direct, dst_of, rows_of, dblocks, sink_of=None):
                g0 = head0[name]
                for i in range(heads + 2):
                    if i < heads:
                        g = g0 + i
                        act.wait_ge(negm_ready, g + 1)
                        if sink_of is not None:
                            nc.scalar.activation(esink[:, g % 2, :], negm[:, g % 2, :], ACT.Exp, bias=sink_of(i))
                        for b in range(TB):
                            src = bank((name + "_s", i))[:, b * 256:(b + 1) * 256] if direct else logit[:, g % 2, b, :]
                            last = nc.scalar.activation(prob[:, g % 2, b, :], src, ACT.Exp,
                                                        bias=negm[:, g % 2, b:b + 1],
                                                        scale=XSCALE if direct else 1.0,
                                                        accum_out=ssum[:, g % 2, b:b + 1])
                        last.then_inc(exp_ready, 1)
                    if 0 <= i - 1 < heads:
                        u, g = (name + "_t", i - 1), g0 + i - 1
                        take_unit(act, u)
                        last = nc.scalar.activation(probT[:, g % 2, :, :], halves(bank(u)), ACT.Copy)
                        free_unit(last, u)
                    if 0 <= i - 2 < heads:
                        u = (name + "_o", i - 2)
                        take_unit(act, u)
                        r0, rn = rows_of(i - 2)
                        src = bank(u)[r0:r0 + rn, 0:dblocks * TOK]
                        last = nc.scalar.activation(dst_of(i - 2), src if dblocks == 1 else halves(src), ACT.Copy)
                        free_unit(last, u)

            def ffn_silu(name, steps):
                f0 = ff0[name]
                for s in range(steps):
                    act.wait_ge(g_full, f0 + s + 1)
                    if s >= 2:
                        act.wait_ge(hT_ready, f0 + s - 1)
                    nc.scalar.activation(silu[:, s % 2, :], psum[:, 2 * (s % 2), :], ACT.Silu).then_inc(silu_ready, 1)

            std()
            act.wait_ge(loads["gains"], 16)
            copy_T("t_x", xT, 0)
            std()
            copy_T("t_mem", memT, 1)
            for i in range(2):
                out_of(("xa", i), uT[:, 2 * i:2 * i + 2, :], ACT.Copy)
            act.wait_ge(prm_exp, 1)
            nc.scalar.activation(pt[:, 20, :], pt[:, 12, :], ACT.Sin)
            nc.scalar.activation(pt[:, 21, :], pt[:, 12, :], ACT.Sin, scale=0.5).then_inc(sin_ready, 1)
            for i in range(4):
                out_of(("zv", i), zv[:, :, i * 256:(i + 1) * 256], ACT.Gelu_apprx_tanh)
            std()
            for u in range(4):
                take_unit(act, ("t_b", u))
                last = nc.scalar.activation(bT[:, 4 * u:4 * u + 4, :],
                                            bank(("t_b", u)).rearrange("p (n m) -> p n m", m=P), ACT.Copy)
                free_unit(last, ("t_b", u))
            for blk in range(0, BLK, 2):
                take_unit(act, ("bu", blk))
                dst = states[:, :, :, blk] if blk < PAIRS else states[:, ::-1, :, blk]
                last = nc.scalar.activation(dst.rearrange("p t r -> p r t"), halves(bank(("bu", blk))), ACT.Copy)
                free_unit(last, ("bu", blk))
            for i in range(4):
                out_of(("zu", i), zuT[:, 2 * i:2 * i + 2, :], ACT.Gelu_apprx_tanh)
            for i in range(4):
                out_of(("ga", i), gaT[:, 2 * i:2 * i + 2, :], ACT.Sigmoid)
            for i in range(4):
                out_of(("gb", i), gbT[:, 2 * i:2 * i + 2, :], ACT.Sigmoid)
            act.dma_start(cw, a["s5_c"]).then_inc(loads["cw"], 16)
            act.wait_ge(zvn_ready, 1)
            for i in range(4):
                out_of(("k", i), kT[:, 2 * i:2 * i + 2, :], ACT.Copy)
            for i in range(4):
                out_of(("v", i), v_t[:, :, i * 256:(i + 1) * 256], ACT.Copy)
            for q in range(4):
                evacuated(act, ("y", q))
                nc.scalar.activation(ygT[:, q, :], ygT[:, q, :], ACT.Gelu_apprx_tanh).then_inc(yg_ready, 1)
            for i in range(2):
                take_unit(act, ("glu", i))
                last = nc.scalar.activation(yaT[:, 2 * i:2 * i + 2, :], halves(bank(("glu", i))), ACT.Sigmoid)
                free_unit(last, ("glu", i))
            std()
            copy_T("t_xattn", xT, 2)
            for i in range(4):
                out_of(("q", i), qT[:, 2 * i:2 * i + 2, :], ACT.Copy)
            attention("x", 4, True, lambda i: oT[:, 2 * i:2 * i + 2, :], lambda i: (0, P), 2)
            std()
            copy_T("t_ffn", xT, 3)
            ffn_silu("ffn", FF_STEPS)
            std()
            std()
            act.wait_ge(loads["bgate"], 16)
            for m in range(2):
                copy_T(f"t_in{m}", xT)
                for i in range(2):
                    out_of((f"projb{m}", i), v_na[:, :, i * 256:(i + 1) * 256], ACT.Copy)
                for i in range(2):
                    out_of((f"projb{m}", 2 + i), qk_t[:, :, i * 256:(i + 1) * 256], ACT.Copy)
                u = (f"projb{m}", 4)
                take_unit(act, u)
                nc.scalar.activation(qk_t[:, :, 512:640], halves(bank(u))[:, :, 0:128], ACT.Copy)
                last = nc.scalar.activation(v_sw, halves(bank(u))[:, :, 128:256], ACT.Copy)
                free_unit(last, u)
                for i in range(2):
                    out_of((f"qk{m}", i), qnT[:, 2 * i:2 * i + 2, :], ACT.Copy)
                for i in range(2):
                    out_of((f"qk{m}", 2 + i), knT[:, 2 * i:2 * i + 2, :], ACT.Copy)

                def gates(name, dst, col0):
                    for i in range(4):
                        take_unit(act, (name, i))
                        for j in range(2):
                            k = 2 * i + j
                            last = nc.scalar.activation(dst[:, k, :], bank((name, i))[:, j * TOK:(j + 1) * TOK],
                                                        ACT.Sigmoid, bias=bgate[:, m, col0 + k:col0 + k + 1])
                        free_unit(last, (name, i))

                gates(f"ga{m}", gaT, 0)
                for u in range(3):
                    take_unit(act, (f"t_sw{m}", u))
                    if u < 2:
                        last = nc.scalar.activation(qsT[:, 2 * u:2 * u + 2, :], halves(bank((f"t_sw{m}", u))), ACT.Copy)
                    else:
                        last = nc.scalar.activation(ksT, bank((f"t_sw{m}", u))[:, 0:TOK], ACT.Copy)
                    free_unit(last, (f"t_sw{m}", u))
                gates(f"gb{m}", gbT, 8)
                attention(f"na{m}", 8, False, lambda i: onT[64 * (i % 2):64 * (i % 2) + 64, i // 2, :],
                          lambda i: (64 * (i % 2), 64), 1)
                attention(f"sw{m}", 8, False, lambda i: osT[64 * (i % 2):64 * (i % 2) + 64, i // 2, :],
                          lambda i: (64 * (i % 2), 64), 1, lambda i: sink_col(m, i))
                std()
                copy_T(f"t_mid{m}", xT)
                if m == 0:
                    ffn_silu("dense", FF_STEPS)
                    std()
            act.wait_ge(rexp_in, 1)
            nc.scalar.activation(rt[:, 8, :, 0], rt[:, 7, :, 0], ACT.Exp).then_inc(rexp_out, 1)
            for u in range(4):
                out_of(("cb", u), comb[:, 2 * u:2 * u + 2, :], ACT.Copy)
            f0 = ff0["moe"]
            for s in range(2):
                act.wait_ge(g_full, f0 + s + 1)
                nc.scalar.activation(silu[:, s, :], psum[:, 2 * s, :], ACT.Silu).then_inc(silu_ready, 1)
            with act.Fori(1, MOE_STEPS // 2) as t:
                for s in range(2):
                    act.wait_ge(g_full, t * 2 + (f0 + s + 1))
                    act.wait_ge(hT_ready, t * 2 + (f0 + s - 1))
                    nc.scalar.activation(silu[:, s, :], psum[:, 2 * s, :], ACT.Silu).then_inc(silu_ready, 1)
            std()
            act.wait_ge(out_ready, 1)
            act.dma_start(out.rearrange("a (b p) d -> p (a b) d", p=P), h[:, :, :]).then_inc(stored, 16)
            act.wait_ge(stored, 16)

        @block.vector
        def _(dve):
            V = nc.vector
            steps = [0]

            def link(ins):
                steps[0] += 1
                ins.then_inc(dve_step, 1)
                dve.wait_ge(dve_step, steps[0])

            norms = [0]

            def stats(src, rms, eps):
                norms[0] += 1
                for b in range(TB):
                    for c in range(2):
                        last = V.bn_stats(st[:, b, c, :], src[:, b, c * 512:(c + 1) * 512])
                link(last)
                for b in range(TB):
                    last = V.bn_aggr(mv[:, b, :], st[:, b, :, :])
                link(last)
                if rms:
                    link(V.tensor_tensor(msq[:, :], mv[:, :, 0], mv[:, :, 0], ALU.mult))
                    link(V.tensor_tensor(msq[:, :], msq[:, :], mv[:, :, 1], ALU.add))
                    V.tensor_scalar(ve[:, :], msq[:, :], eps, None, ALU.add).then_inc(var_ready, 1)
                else:
                    V.tensor_scalar(ve[:, :], mv[:, :, 1], eps, None, ALU.add).then_inc(var_ready, 1)
                dve.wait_ge(std_ready, norms[0])
                link(V.reciprocal(rstd[:, :], sd[:, :]))

            def scaled(dst, src, ready):
                for b in range(TB):
                    last = V.tensor_scalar(dst[:, b, :], src[:, b, :], rstd[:, b:b + 1], None, ALU.mult)
                last.then_inc(ready, 1)

            def layer_norm(x, g, b_, eps):
                stats(x, False, eps)
                for b in range(TB):
                    last = V.tensor_scalar(x[:, b, :], x[:, b, :], mv[:, b, 0:1], rstd[:, b:b + 1],
                                           ALU.subtract, ALU.mult)
                link(last)
                for b in range(TB):
                    last = V.tensor_tensor(x[:, b, :], x[:, b, :], g, ALU.mult)
                link(last)
                for b in range(TB):
                    last = V.tensor_tensor(x[:, b, :], x[:, b, :], b_, ALU.add)
                return last

            def residual(unit, i, alpha=None):
                take_unit(dve, unit)
                hs = h[:, :, i * 256:(i + 1) * 256]
                if alpha is None:
                    last = V.tensor_tensor(hs, hs, halves(bank(unit)), ALU.add)
                else:
                    last = V.scalar_tensor_tensor(hs, hs, alpha, halves(bank(unit)), ALU.mult, ALU.add)
                free_unit(last, unit)
                return last

            def attention(name, heads, bias_of, sink_of):
                g0 = head0[name]
                for i in range(heads + 1):
                    if i < heads:
                        g = g0 + i
                        u = (name + "_s", i)
                        take_unit(dve, u)
                        if bias_of is None:
                            link(V.reduce_max(mx[:, g % 2, :], halves(bank(u)), AX_X))
                            V.tensor_scalar(negm[:, g % 2, :], mx[:, g % 2, :], -XSCALE, None,
                                            ALU.mult).then_inc(negm_ready, 1)
                        else:
                            last = V.scalar_tensor_tensor(logit[:, g % 2, :, :], halves(bank(u)), HSCALE,
                                                          bias_of(i), ALU.mult, ALU.add)
                            free_unit(last, u)
                            evacuated(dve, u)
                            link(V.reduce_max(mx[:, g % 2, :], logit[:, g % 2, :, :], AX_X))
                            if sink_of is not None:
                                link(V.tensor_scalar(mx[:, g % 2, :], mx[:, g % 2, :], sink_of(i), None, ALU.max))
                            V.tensor_scalar(negm[:, g % 2, :], mx[:, g % 2, :], -1.0, None,
                                            ALU.mult).then_inc(negm_ready, 1)
                    if i >= 1:
                        g = g0 + i - 1
                        dve.wait_ge(exp_ready, g + 1)
                        if sink_of is not None:
                            link(V.tensor_tensor(ssum[:, g % 2, :], ssum[:, g % 2, :], esink[:, g % 2, :], ALU.add))
                        link(V.reciprocal(rsum[:, g % 2, :], ssum[:, g % 2, :]))
                        for b in range(TB):
                            last = V.tensor_scalar(prob[:, g % 2, b, :], prob[:, g % 2, b, :],
                                                   rsum[:, g % 2, b:b + 1], None, ALU.mult)
                            if b == 0 and bias_of is None:
                                free_unit(last, (name + "_s", i - 1))
                        last.then_inc(prob_ready, 1)

            def ffn_mul(name, steps_):
                f0 = ff0[name]
                for s in range(steps_):
                    dve.wait_ge(silu_ready, f0 + s + 1)
                    dve.wait_ge(u_full, f0 + s + 1)
                    if s >= 2:
                        dve.wait_ge(down_done, f0 + s - 1)
                    V.tensor_tensor(hT[:, s % 2, :, :], halves(silu[:, s % 2, :]), halves(psum[:, 2 * (s % 2) + 1, :]),
                                    ALU.mult).then_inc(hT_ready, 1)

            def add_sums(n, alpha=None):
                dve.wait_ge(down_done, (FF_STEPS, 2 * FF_STEPS, 2 * FF_STEPS + MOE_STEPS)[n - 1])
                for b in range(TB):
                    for c in range(2):
                        hs = h[:, b, c * 512:(c + 1) * 512]
                        acc = psum[:, 4 + 2 * b + c, :]
                        if alpha is None:
                            last = V.tensor_tensor(hs, hs, acc, ALU.add)
                        else:
                            last = V.scalar_tensor_tensor(hs, hs, alpha, acc, ALU.mult, ALU.add)
                last.then_inc(acc_free, 1)
                dve.wait_ge(acc_free, n)

            V.memset(ones[:, :], 1.0).then_inc(ones_ready, 1)
            dve.wait_ge(loads["x"], 16)
            stats(h, True, EPS)
            scaled(xn, h, xn_ready)
            dve.wait_ge(loads["mem"], 16)
            stats(x_mem, True, EPS)
            scaled(n_mem, x_mem, memn_ready)

            row = lambda n: pt[:, n, :]
            LR, LI, LS, STEP, X, KF, R, H, KI, ER = range(10)
            ANG, KA, MAG, NR, ARE, AIM, CRE, CIM, T1, T2 = 12, 10, 11, 13, 14, 15, 16, 17, 18, 19
            SN, SH = 20, 21
            magic = 1.5 * 2.0 ** 23

            def exp_of(dst, src):
                link(V.tensor_scalar(row(X), row(src), -87.0, 88.0, ALU.max, ALU.min))
                link(V.tensor_scalar(row(KF), row(X), 1.4426950408889634, magic, ALU.mult, ALU.add))
                link(V.tensor_scalar(row(KF), row(KF), magic, None, ALU.subtract))
                link(V.scalar_tensor_tensor(row(R), row(KF), -0.693359375, row(X), ALU.mult, ALU.add))
                link(V.scalar_tensor_tensor(row(R), row(KF), 2.12194440e-4, row(R), ALU.mult, ALU.add))
                link(V.tensor_scalar(row(H), row(R), 1.0 / 5040, None, ALU.mult))
                for c in (1.0 / 720, 1.0 / 120, 1.0 / 24, 1.0 / 6, 0.5, 1.0):
                    link(V.scalar_tensor_tensor(row(H), row(H), c, row(R), ALU.add, ALU.mult))
                link(V.tensor_scalar(row(KI).bitcast(I32), row(KF), 127.0, 2.0 ** 23, ALU.add, ALU.mult))
                link(V.scalar_tensor_tensor(row(dst), row(H), 1.0, row(KI), ALU.add, ALU.mult))

            dve.wait_ge(loads["prm"], 16)
            exp_of(STEP, LS)
            link(V.tensor_tensor(row(MAG), row(LR), row(STEP), ALU.mult))
            exp_of(ER, MAG)
            link(V.tensor_tensor(row(ANG), row(LI), row(STEP), ALU.mult))
            link(V.tensor_scalar(row(KA), row(ANG), 1.0 / (2 * np.pi), magic, ALU.mult, ALU.add))
            link(V.tensor_scalar(row(KA), row(KA), magic, None, ALU.subtract))
            c1 = 6.28125
            c2 = float(np.float32(np.floor((2 * np.pi - c1) * 2 ** 21) / 2 ** 21))
            c3 = float(2 * np.pi - c1 - c2)
            for c in (c1, c2, c3):
                link(V.scalar_tensor_tensor(row(ANG), row(KA), -c, row(ANG), ALU.mult, ALU.add))
            V.tensor_scalar(row(ANG), row(ANG), -3.1415925, 3.1415925, ALU.max, ALU.min).then_inc(prm_exp, 1)
            link(V.memset(b_wide_f[:, :], 0.0))
            dve.wait_ge(sin_ready, 1)
            link(V.tensor_tensor(row(SH), row(SH), row(SH), ALU.mult))
            link(V.tensor_scalar(row(SH), row(SH), -2.0, 1.0, ALU.mult, ALU.add))
            V.tensor_tensor(row(ARE), row(ER), row(SH), ALU.mult)
            link(V.tensor_tensor(row(AIM), row(ER), row(SN), ALU.mult))
            for r in range(2):
                V.tensor_copy(lam_a[:, 0, r, :], row(ARE))
            V.tensor_scalar(lam_a[:, 1, 1, :], row(AIM), -1.0, None, ALU.mult)
            V.tensor_copy(lam_a[:, 1, 0, :], row(AIM))
            link(V.tensor_scalar(row(NR), row(ARE), -1.0, None, ALU.add))
            V.tensor_tensor(row(T1), row(LR), row(LR), ALU.mult)
            link(V.tensor_tensor(row(T2), row(LI), row(LI), ALU.mult))
            link(V.tensor_tensor(row(MAG), row(T1), row(T2), ALU.add))
            link(V.reciprocal(row(MAG), row(MAG)))
            V.tensor_tensor(row(T1), row(NR), row(LR), ALU.mult)
            V.tensor_tensor(row(T2), row(AIM), row(LI), ALU.mult)
            V.tensor_tensor(row(CRE), row(AIM), row(LR), ALU.mult)
            link(V.tensor_tensor(row(CIM), row(NR), row(LI), ALU.mult))
            V.tensor_tensor(row(T1), row(T1), row(T2), ALU.add)
            link(V.tensor_tensor(row(CIM), row(CRE), row(CIM), ALU.subtract))
            V.tensor_tensor(row(CRE), row(T1), row(MAG), ALU.mult)
            link(V.tensor_tensor(row(CIM), row(CIM), row(MAG), ALU.mult))
            dve.wait_ge(loads["b"], 16)
            cre = row(CRE).unsqueeze(2).to_broadcast([P, BLK, S5_C])
            cim = row(CIM).unsqueeze(2).to_broadcast([P, BLK, S5_C])
            for out_r, (r0, r1, op) in enumerate(((0, 1, ALU.subtract), (1, 0, ALU.add))):
                V.tensor_tensor(b_tmp[:, 0], b_raw[:, r0], cre, ALU.mult)
                link(V.tensor_tensor(b_tmp[:, 1], b_raw[:, r1], cim, ALU.mult))
                for g in range(2):
                    rows = slice(64 * g, 64 * g + 64)
                    last = V.tensor_tensor(b_wide[rows, out_r, :, g, :], b_tmp[rows, 0], b_tmp[rows, 1], op)
                link(last)
            V.memset(msq[:, :], 0.0).then_inc(bwide_ready, 1)

            evacuated(dve, ("zv", 3))
            stats(zv, False, EPS)
            dve.wait_ge(loads["lnv"], 16)
            for b in range(TB):
                last = V.tensor_scalar(zv[:, b, :], zv[:, b, :], mv[:, b, 0:1], rstd[:, b:b + 1],
                                       ALU.subtract, ALU.mult)
            link(last)
            for b in range(TB):
                last = V.tensor_tensor(zv[:, b, :], zv[:, b, :], ln_v[:, 0, :], ALU.mult)
            link(last)
            for b in range(TB):
                last = V.tensor_tensor(zv[:, b, :], zv[:, b, :], ln_v[:, 1, :], ALU.add)
            last.then_inc(zvn_ready, 1)

            for blk in range(1, BLK, 2):
                take_unit(dve, ("bu", blk))
                dst = states[:, :, :, blk] if blk < PAIRS else states[:, ::-1, :, blk]
                last = V.tensor_copy(dst.rearrange("p t r -> p r t"), halves(bank(("bu", blk))))
                free_unit(last, ("bu", blk))
            evacuated(dve, ("bu", BLK - 1))
            evacuated(dve, ("bu", BLK - 2))
            per = 5
            ops = 4
            with dve.Fori(0, (TOK - 1) // per) as t:
                for j in range(per):
                    def at(o):
                        return states[:, bass.ds(t * per + (j + o), 1), :, :].rearrange("p a r k -> p (a r) k")
                    prev, cur = at(0), at(1)
                    done = t * (ops * per) + ops * j
                    V.tensor_tensor(scan_t[:, 0], prev, lam_a[:, 0], ALU.mult).then_inc(scan_step, 1)
                    V.tensor_tensor(scan_t[:, 1, ::-1, :], prev, lam_a[:, 1], ALU.mult).then_inc(scan_step, 1)
                    dve.wait_ge(scan_step, done + 1)
                    V.tensor_tensor(scan_t[:, 2], scan_t[:, 0], cur, ALU.add).then_inc(scan_step, 1)
                    dve.wait_ge(scan_step, done + 3)
                    V.tensor_tensor(cur, scan_t[:, 2], scan_t[:, 1], ALU.add).then_inc(scan_step, 1)
                    dve.wait_ge(scan_step, done + 4)
            V.memset(msq[:, :], 0.0).then_inc(scan_done, 1)
            dve.wait_ge(loads["cw"], 16)
            V.tensor_scalar(cw[:, 1], cw[:, 1], -1.0, None, ALU.mult).then_inc(cneg_ready, 1)

            evacuated(dve, ("zu", 3))
            for u in range(4):
                take_unit(dve, ("sgu", u))
                zs = zuT[:, 2 * u:2 * u + 2, :]
                last = V.tensor_tensor(zs, zs, halves(bank(("sgu", u))), ALU.mult)
                free_unit(last, ("sgu", u))
            evacuated(dve, ("gb", 3))
            for i in range(4):
                take_unit(dve, ("pb", i))
                gs = gbT[:, 2 * i:2 * i + 2, :]
                last = V.tensor_tensor(gs, gs, halves(bank(("pb", i))), ALU.mult)
                free_unit(last, ("pb", i))
            dve.wait_ge(loads["s5d"], 16)
            for q in range(4):
                take_unit(dve, ("y", q))
                last = V.scalar_tensor_tensor(ygT[:, q, :], uT[:, q, :], s5d[:, q:q + 1],
                                              bank(("y", q))[:, 0:TOK], ALU.mult, ALU.add)
                free_unit(last, ("y", q))
            for i in range(2):
                evacuated(dve, ("glu", i))
                ys = yaT[:, 2 * i:2 * i + 2, :]
                V.tensor_tensor(ys, ys, ygT[:, 2 * i:2 * i + 2, :], ALU.mult).then_inc(ya_ready, 1)

            def merge(name, first):
                for i in range(4):
                    take_unit(dve, (name, i))
                    gs = gaT[:, 2 * i:2 * i + 2, :]
                    last = V.tensor_tensor(gs, gs, halves(bank((name, i))), ALU.mult)
                    free_unit(last, (name, i))
                    evacuated(dve, (name, i))
                    V.tensor_tensor(gs, gs, gbT[:, 2 * i:2 * i + 2, :], ALU.add).then_inc(m_ready, 1)

            merge("pa", True)
            for i in range(4):
                residual(("out", i), i)
            evacuated(dve, ("out", 3))
            stats(h, True, EPS)
            scaled(xn, h, xn_ready)
            attention("x", 4, None, None)
            for i in range(4):
                residual(("xo", i), i)
            evacuated(dve, ("xo", 3))
            stats(h, True, EPS)
            scaled(xn, h, xn_ready)
            ffn_mul("ffn", FF_STEPS)
            add_sums(1)
            dve.wait_ge(loads["bc0"], 16 * 7)
            stats(h, True, EPS)
            for b in range(TB):
                last = V.scalar_tensor_tensor(h[:, b, :], h[:, b, :], rstd[:, b:b + 1], bc[:, 0, :],
                                              ALU.mult, ALU.mult)
            link(last)
            layer_norm(h, bc[:, 1, :], bc[:, 2, :], LN_EPS).then_inc(xn_ready, 1)
            dve.wait_ge(xn_ready, 4)
            dve.wait_ge(loads["nab"], 32)
            dve.wait_ge(loads["consts"], 48)
            dve.wait_ge(loads["sink"], 16)
            for m in range(2):
                evacuated(dve, (f"projb{m}", 4))
                heads = qk_t[:, :, 0:640].rearrange("p b (h d) -> p b h d", d=64)
                tmp = rtmp[:, :, :, 0:80]
                for b in range(TB):
                    x1, x2 = heads[:, b, :, 0:8], heads[:, b, :, 8:16]
                    cos = rope[:, b, 0, :].unsqueeze(1).to_broadcast([P, 10, 8])
                    sin = rope[:, b, 1, :].unsqueeze(1).to_broadcast([P, 10, 8])
                    t = [rtmp[:, n, b, 0:80].rearrange("p (h f) -> p h f", f=8) for n in range(4)]
                    V.tensor_tensor(t[0], x1, cos, ALU.mult)
                    V.tensor_tensor(t[1], x2, sin, ALU.mult)
                    V.tensor_tensor(t[2], x2, cos, ALU.mult)
                    link(V.tensor_tensor(t[3], x1, sin, ALU.mult))
                    V.tensor_tensor(x1, t[0], t[1], ALU.subtract)
                    last = V.tensor_tensor(x2, t[2], t[3], ALU.add)
                last.then_inc(qk_roped, 1)
                attention(f"na{m}", 8, lambda i: nabias[m][:, i, :, :], None)
                attention(f"sw{m}", 8, lambda i: swmask, lambda i: sink_col(m, i))
                evacuated(dve, (f"gb{m}", 3))
                for i in range(4):
                    take_unit(dve, (f"bna{m}", i))
                    gs = gaT[:, 2 * i:2 * i + 2, :]
                    last = V.tensor_tensor(gs, gs, halves(bank((f"bna{m}", i))), ALU.mult)
                    free_unit(last, (f"bna{m}", i))
                for i in range(4):
                    take_unit(dve, (f"bsw{m}", i))
                    gs = gbT[:, 2 * i:2 * i + 2, :]
                    last = V.tensor_tensor(gs, gs, halves(bank((f"bsw{m}", i))), ALU.mult)
                    free_unit(last, (f"bsw{m}", i))
                    evacuated(dve, (f"bsw{m}", i))
                    ms = gaT[:, 2 * i:2 * i + 2, :]
                    V.tensor_tensor(ms, ms, gs, ALU.add).then_inc(m_ready, 1)
                for i in range(4):
                    residual((f"out{m}", i), i, ALPHA)
                evacuated(dve, (f"out{m}", 3))
                if m == 1:
                    dve.wait_ge(loads["bcn"], 16 * 4)
                layer_norm(h, bc[:, 3, :], bc[:, 4, :], LN_EPS).then_inc(xn_ready, 1)
                dve.wait_ge(xn_ready, 5 + 2 * m)
                if m == 0:
                    ffn_mul("dense", FF_STEPS)
                    add_sums(2, ALPHA)
                    layer_norm(h, bc[:, 5, :], bc[:, 6, :], LN_EPS).then_inc(xn_ready, 1)
                    dve.wait_ge(xn_ready, 6)

            lg, m1, c1_, f1, l2, m2, f2 = (rt[:, n, :, :] for n in range(7))
            v1, v2 = rt[:, 9, :, 0:1], rt[:, 9, :, 1:2]
            take_unit(dve, ("router", 0))
            last = V.tensor_copy(lg, bank(("router", 0))[:, 0:16].rearrange("p (b e) -> p b e", e=8))
            free_unit(last, ("router", 0))
            evacuated(dve, ("router", 0))

            def first_max(val, src, dst, tmp, top):
                link(V.reduce_max(top, src, AX_X))
                link(V.tensor_tensor(tmp, src, top.to_broadcast([P, TB, 8]), ALU.is_equal))
                for b in range(TB):
                    last = V.tensor_tensor_scan(c1_[:, b, :], ones[:, 0:8], tmp[:, b, :], 0.0, ALU.mult, ALU.add)
                link(last)
                link(V.tensor_scalar(c1_, c1_, 1.0, None, ALU.is_le))
                link(V.tensor_tensor(dst, tmp, c1_, ALU.mult))

            first_max(None, lg, f1, m1, v1)
            link(V.scalar_tensor_tensor(l2, f1, -3.0e38, lg, ALU.mult, ALU.add))
            first_max(None, l2, f2, m2, v2)
            V.tensor_tensor(rt[:, 7, :, 0:1], v2, v1, ALU.subtract).then_inc(rexp_in, 1)
            dve.wait_ge(rexp_out, 1)
            ex, den, w1, w2 = rt[:, 8, :, 0:1], rt[:, 10, :, 0:1], rt[:, 10, :, 1:2], rt[:, 10, :, 2:3]
            link(V.tensor_scalar(den, ex, 1.0, None, ALU.add))
            link(V.reciprocal(w1, den))
            link(V.tensor_tensor(w2, ex, w1, ALU.mult))
            V.tensor_tensor(f1, f1, w1.to_broadcast([P, TB, 8]), ALU.mult)
            link(V.tensor_tensor(f2, f2, w2.to_broadcast([P, TB, 8]), ALU.mult))
            link(V.tensor_tensor(f1, f1, f2, ALU.add))
            for e in range(MOE_E):
                for b in range(TB):
                    last = V.tensor_scalar(cdiag[:, 2 * e + b, :], ident[:, :], f1[:, b, e:e + 1], None, ALU.mult)
            last.then_inc(diag_ready, 1)

            f0 = ff0["moe"]
            evacuated(dve, ("cb", 3))

            def moe_mul(s, n, e_comb, first):
                dve.wait_ge(silu_ready, n + 1)
                sl = halves(silu[:, s % 2, :])
                V.tensor_tensor(sl, sl, e_comb, ALU.mult).then_inc(moe_scaled, 1)
                dve.wait_ge(u_full, n + 1)
                if not first:
                    dve.wait_ge(down_done, n - 1)
                dve.wait_ge(moe_scaled, n - f0 + 1)
                V.tensor_tensor(hT[:, s % 2, :, :], sl, halves(psum[:, 2 * (s % 2) + 1, :]),
                                ALU.mult).then_inc(hT_ready, 1)

            with dve.Fori(0, MOE_E) as e:
                for s in range(MOE_PER):
                    cb = comb[:, bass.ds(e, 1), :].to_broadcast([P, 2, TOK])
                    moe_mul(s, e * MOE_PER + (f0 + s), cb, False)
            add_sums(3, ALPHA)
            last = layer_norm(h, bc[:, 5, :], bc[:, 6, :], LN_EPS)
            last.then_inc(out_ready, 1)


def weight_stream(w):
    out = np.empty((len(CHUNKS), P, CHUNK_F), np.float32)
    for n, (kind, name, i) in enumerate(CHUNKS):
        m = w[name]
        if m.ndim == 3:
            per = MOE_PER
            m, i = m[i // per], i % per
        if kind == "k2":
            out[n] = m[256 * i:256 * i + 256].reshape(2, P, D).transpose(1, 0, 2).reshape(P, CHUNK_F)
        else:
            k, cols = (KD, 256) if kind == "k8" else (4, 512)
            part = m[:, cols * i:cols * (i + 1)]
            out[n] = part.reshape(k, P, cols).transpose(1, 0, 2).reshape(P, CHUNK_F)
    return out


def pair_heads():
    return np.concatenate([np.arange(64) + 64 * hd for i in range(4) for hd in (i, i + 4)])


def na_bias_layout(rpb):
    q, k = np.arange(TOK)[:, None], np.arange(TOK)[None, :]
    qr, qc, kr, kc = q // 64, q % 64, k // 64, k % 64
    start = np.clip(qc - 8, 0, 48)
    valid = (kc >= start) & (kc < start + 16)
    dr, dc = kr - qr + 7, np.clip(kc - qc + 15, 0, 30)
    out = np.where(valid[None], rpb[:, dr, dc], np.float32(-1e30))
    return out.reshape(8, TB, P, TOK).transpose(2, 0, 1, 3)


def layout(i):
    f = {k: np.asarray(v) for k, v in i.items()}
    per = pair_heads()
    w = {"w_in": np.concatenate([f["w_in"][0][:, :512], f["w_in"][0][:, 1536:2560],
                                 f["w_in"][0][:, 512:1536], f["w_in"][0][:, 2560:]], 1)}
    for n in ("w_k", "w_v", "w_q", "w_xo", "w_out", "w_proj_a", "w_proj_b", "s5_w_glu"):
        w[n] = f[n][0]
    w["ffn_gate"], w["ffn_up"], w["ffn_down"] = f["w_gate"][0], f["w_up"][0], f["w_down"][0]
    w["dense_gate"], w["dense_up"], w["dense_down"] = (f[f"ffn_w_{n}_2"][0] for n in ("gate", "up", "down"))
    w["moe_gate"], w["moe_up"], w["moe_down"] = (f[f"moe_w_{n}_2"][0] for n in ("gate", "up", "down"))
    for m in range(2):
        x = f["w_in_2"][m]
        w[f"w_in_{m}"] = np.concatenate([x[:, 1024:1536], x[:, 1536:2048][:, per], x[:, 2048:2304],
                                         x[:, 0:1024], x[:, 2304:]], 1)
        w[f"w_na_{m}"] = f["w_branch_na_2"][m]
        w[f"w_sw_{m}"] = f["w_branch_sw_2"][m][per]
        w[f"w_out_{m}"] = f["w_out_2"][m]

    def col(v):
        return v.reshape(-1, P).T

    def states(v):
        v = v.reshape(2, PAIRS, 2, S5_P, *v.shape[3:])
        return np.moveaxis(v, (2, 3), (0, 1)).reshape(P, BLK, *v.shape[4:])

    step = np.broadcast_to(f["s5_log_step"][0][:, :, None], (2, S5_G, S5_P))
    s5_c = np.zeros((P, 2, BLK, 2, S5_C), np.float32)
    for r, n in enumerate(("s5_c_re", "s5_c_im")):
        c = states(f[n][0].transpose(0, 1, 3, 2))
        for g in range(2):
            s5_c[64 * g:64 * g + 64, r, :, g, :] = c[64 * g:64 * g + 64]
    pos = np.arange(TOK, dtype=np.float32)
    inv = (1.0 / (500000.0 ** (np.arange(0, 16, 2, dtype=np.float32) / 16))).astype(np.float32)
    ang = pos[:, None] * inv[None, :]
    rope = np.stack([np.cos(ang), np.sin(ang)], 1).astype(np.float32).reshape(TB, P, 2, 8).transpose(1, 0, 2, 3)
    q, k = np.arange(TOK)[:, None], np.arange(TOK)[None, :]
    band = np.where(np.abs(q - k) <= 128, 0.0, -1e30).astype(np.float32).reshape(TB, P, TOK).transpose(1, 0, 2)
    return {
        "x": f["x"], "mem": f["mem"], "stream": weight_stream(w),
        "ident": np.eye(P, dtype=np.float32),
        "gains": np.stack([col(f["mix_norm_g"][0]), col(f["mem_norm_g"]), col(f["xattn_norm_g"][0]),
                           col(f["ffn_norm_g"][0])], 1),
        "s5_prm": np.stack([states(f["s5_lam_re"][0]), states(f["s5_lam_im"][0]), states(step)], 1),
        "s5_b": np.stack([states(f["s5_b_re"][0]), states(f["s5_b_im"][0])], 1),
        "s5_c": s5_c.reshape(P, 2, BLK, 32),
        "s5_d": col(f["s5_d"][0]),
        "sgu_ln": np.concatenate([f["sgu_ln_g"], f["sgu_ln_b"]], 0),
        "sgu_w": f["sgu_w"][0].transpose(2, 0, 1),
        "sgu_bias": f["sgu_bias"][0].reshape(1, -1),
        "b_gate": np.stack([col(f["b_gate_2"][m]) for m in range(2)], 1),
        "sink": f["sw_sink_2"],
        "na_bias": np.stack([na_bias_layout(f["na_rpb_2"][m]) for m in range(2)]),
        "sw_mask": band, "rope": rope,
        "router": f["moe_router_2"][0].reshape(KD, P, 8).transpose(1, 0, 2),
        "bc": np.stack([f["final_norm_g"], f["emb_ln_g_2"], f["emb_ln_b_2"]]
                       + [f[n][m] for m in range(2) for n in ("ln1_g_2", "ln1_b_2", "ln2_g_2", "ln2_b_2")]),
    }


def kernel(**inputs):
    import concourse.bacc as _bacc
    from concourse.bass_utils import run_bass_kernel_spmd as _run

    nc = _bacc.Bacc("TRN2", target_bir_lowering=False, num_devices=1)
    arrays, aps = {}, {}
    for name, v in layout(inputs).items():
        arrays["in_" + name] = np.ascontiguousarray(v)
        aps[name] = nc.dram_tensor("in_" + name, v.shape, mybir.dt.from_np(v.dtype), kind="ExternalInput").ap()
    out = nc.dram_tensor("out_dram", (1, TOK, D), F32, kind="ExternalOutput").ap()
    build(nc, aps, out)
    r = _run(nc, [arrays], core_ids=[0])
    return r.results[0]["out_dram"]
```

```python
from contextlib import ExitStack

import numpy as np

import concourse.bass as bass
from concourse import mybir

P = 128
TOK = 256
TB = TOK // P
D = 1024
KD = D // P
SLOTS = 7
CHUNK_F = 2048
BANKS = 8
BF = 512

ALU = mybir.AluOpType
ACT = mybir.ActivationFunctionType
F32 = mybir.dt.float32
F32R = mybir.dt.float32r
I32 = mybir.dt.int32
AX_X = mybir.AxisListType.X

S5_G, S5_P, S5_C = 32, 64, 16
PAIRS = S5_G // 2
BLK = 2 * PAIRS
FF_STEPS = 2816 // 256
MOE_E = 8
MOE_PER = 3584 // 256
MOE_CHUNKS = 3 * MOE_PER
CAP = P
OVER = (2 * TOK) // (CAP + 1)
PASSES = MOE_E + OVER + 1
SPLITS = 3
AHEAD = 2
ALPHA = 4.0 ** 0.25
EPS = 1e-6
LN_EPS = 1e-5
XSCALE = 256.0 ** -0.5
HSCALE = 64.0 ** -0.5
NORMS = ("x", "mem", "zv", "xattn", "ffn", "final", "emb", "ln1_0", "ln2_0", "ln1_1", "ln2_1")


def ffn_chunks(name, steps):
    out = [("k8", name + "_gate", 0), ("k8", name + "_up", 0)]
    for s in range(1, steps):
        out += [("k8", name + "_gate", s), ("k8", name + "_up", s), ("k2", name + "_down", s - 1)]
    return out + [("k2", name + "_down", steps - 1)]


def moe_chunks(e):
    out = []
    for s in range(MOE_PER + 2):
        if s < MOE_PER:
            out += [("k8", "moe_gate", e * MOE_PER + s), ("k8", "moe_up", e * MOE_PER + s)]
        if s >= 2:
            out.append(("k2", "moe_down", e * MOE_PER + s - 2))
    return out


def moe_events():
    chunks, after = [], {}
    for s in range(MOE_PER + 2):
        if s < MOE_PER:
            chunks += [("gate", s), ("up", s)]
            after[len(chunks) - 1] = [("prod", s)]
        if s >= 2:
            chunks.append(("down", s - 2))
        if 1 <= s <= MOE_PER:
            after.setdefault(len(chunks) - 1, []).append(("move", s - 1))
    return chunks, after


def plan_chunks():
    c = [("k8", "w_in", i) for i in range(18)]
    c += [("k8", "w_k", i) for i in range(4)] + [("k8", "w_v", i) for i in range(4)]
    c += [("k8", "w_proj_b", i) for i in range(4)]
    c += [("k4", "s5_w_glu", 0)] + [("k4", "w_proj_a", i) for i in range(2)]
    c += [("k8", w, i) for w in ("w_out", "w_q", "w_xo") for i in range(4)]
    c += ffn_chunks("ffn", FF_STEPS)
    for layer in range(2):
        c += [("k8", f"w_in_{layer}", i) for i in range(17)]
        c += [("k4", f"w_na_{layer}", i) for i in range(2)] + [("k4", f"w_sw_{layer}", i) for i in range(2)]
        c += [("k8", f"w_out_{layer}", i) for i in range(4)]
        if layer == 0:
            c += ffn_chunks("dense", FF_STEPS)
    for e in range(MOE_E):
        c += moe_chunks(e)
    return c


def plan_units():
    u = []

    def add(name, n):
        u.extend((name, i) for i in range(n))

    add("t_x", 4)
    add("t_mem", 4)
    add("xa", 2)
    add("zv", 4)
    add("t_b", 4)
    add("bu", BLK)
    add("zu", 4)
    add("ga", 4)
    add("gb", 4)
    add("k", 4)
    add("v", 4)
    add("sgu", 4)
    add("pb", 4)
    add("y", 4)
    add("glu", 2)
    add("pa", 4)
    add("out", 4)
    add("t_xattn", 4)
    add("q", 4)
    attention_units(u, "x", 4)
    add("xo", 4)
    add("t_ffn", 4)
    for m in range(2):
        add(f"t_in{m}", 4)
        add(f"projb{m}", 5)
        add(f"qk{m}", 4)
        add(f"ga{m}", 4)
        add(f"t_sw{m}", 3)
        add(f"gb{m}", 4)
        attention_units(u, f"na{m}", 8)
        attention_units(u, f"sw{m}", 8)
        add(f"bna{m}", 4)
        add(f"bsw{m}", 4)
        add(f"out{m}", 4)
        add(f"t_mid{m}", 4)
    add("router", 1)
    add("pos", 1)
    return u


def attention_units(u, name, heads):
    for i in range(heads + 2):
        if i < heads:
            u.append((name + "_s", i))
        if 0 <= i - 1 < heads:
            u.append((name + "_t", i - 1))
        if 0 <= i - 2 < heads:
            u.append((name + "_o", i - 2))


CHUNKS = plan_chunks()
CHUNK_AT = {c: n for n, c in enumerate(CHUNKS)}
UNITS = plan_units()
UNIT_AT = {u: n for n, u in enumerate(UNITS)}
MOE_C0 = CHUNK_AT[("k8", "moe_gate", 0)]
assert len(CHUNKS) % SLOTS == 0 and MOE_C0 % SLOTS == 0 and MOE_CHUNKS % SLOTS == 0 and len(CHUNK_AT) == len(CHUNKS) and len(UNIT_AT) == len(UNITS)


def build(nc, a, out, stop=None):
    with ExitStack() as ctx:
        def sb(name, shape, dt=F32):
            return ctx.enter_context(nc.sbuf_tensor(name, shape, dt))

        def sem(name):
            return ctx.enter_context(nc.semaphore(name))

        ring = sb("ring", [P, SLOTS, CHUNK_F])
        h = sb("h", [P, TB, D])
        ident = sb("ident", [P, P])
        gains = sb("gains", [P, 4, KD])
        s5d = sb("s5d", [P, 4])
        bgate = sb("bgate", [P, 2, 16])
        sink = sb("sink", [P, 2, 8])
        st = sb("st", [P, TB, 2, 6])
        mv = sb("mv", [P, TB, 2])
        ve = sb("ve", [P, TB])
        sd = sb("sd", [P, TB])
        rstd = sb("rstd", [P, TB])
        msq = sb("msq", [P, TB])
        lam_a = sb("lam_a", [P, 2, 2, BLK])
        scan_t = sb("scan_t", [P, 3, 2, BLK])
        mx = sb("mx", [P, 2, TB])
        negm = sb("negm", [P, 2, TB])
        ssum = sb("ssum", [P, 2, TB])
        rsum = sb("rsum", [P, 2, TB])
        esink = sb("esink", [P, 2, TB])
        rt = sb("rt", [P, 12, TB, 8])
        mask = rt[:, 11, :, :]
        ones = sb("ones", [P, P])
        pass_pos = sb("pass_pos", [P, TB, PASSES])
        pass_w = sb("pass_w", [P, TB, PASSES])
        over = sb("over", [P, 4, PASSES - MOE_E, 8])
        table = sb("table", [P, 8], I32)
        psum = ctx.enter_context(nc.psum_tensor("psum", [P, BANKS, BF], F32))
        with ExitStack() as early:
            def region(name, shape, dt=F32):
                return early.enter_context(nc.sbuf_tensor(name, shape, dt))

            big = region("big", [P, 16384])
            xT = region("xT", [P, KD, TOK])
            memT = region("memT", [P, KD, TOK])
            r_zu = region("r_zu", [P, 2048])
            r_zv = region("r_zv", [P, 2048])
            r_ga = region("r_ga", [P, 2048])
            r_gb = region("r_gb", [P, 2048])
            r_k = region("r_k", [P, 2048])
            r_v = region("r_v", [P, 2048])
            uT = region("uT", [P, 4, TOK])
            sguT = region("sguT", [P, 8, P])
        w_l = sb("w_l", [P, SPLITS, CHUNK_F], F32R)
        h_l = sb("h_l", [P, TB, D], F32R)
        sb("constants_stay", [P, 8192])
        w_h = sb("w_h", [P, SPLITS, CHUNK_F], F32R)
        h_h = sb("h_h", [P, TB, D], F32R)
        ysum = sb("ysum", [P, TB, D])
        xe_h = sb("xe_h", [P, KD, P], F32R)
        xe_l = sb("xe_l", [P, KD, P], F32R)
        o_h = sb("o_h", [P, 2, BF], F32R)
        o_l = sb("o_l", [P, 2, BF], F32R)
        pick = sb("pick", [P, TB, P], F32R)
        pickT = sb("pickT", [P, TB, P], F32R)
        e_silu = sb("e_silu", [P, 2, 256])
        e_h = sb("e_h", [P, 2, 256])
        eT_h = sb("eT_h", [P, 2, 2, P], F32R)
        eT_l = sb("eT_l", [P, 2, 2, P], F32R)

        def view(region, lo, size, pat, **kw):
            return region[:, lo:lo + size].rearrange(pat, **kw)

        x_mem = view(big, 0, 2048, "p (b d) -> p b d", b=TB)
        n_mem = view(big, 2048, 2048, "p (b d) -> p b d", b=TB)
        states = big[:, :].rearrange("p (t r k) -> p t r k", r=2, k=BLK)
        xn = view(r_gb, 0, 2048, "p (b d) -> p b d", b=TB)
        ln_v = view(r_k, 0, 2048, "p (a d) -> p a d", a=2)
        b_raw = view(r_zu, 0, 1024, "p (r k c) -> p r k c", r=2, k=BLK)
        pt = view(r_zu, 1024, 1024, "p (n k) -> p n k", k=BLK)
        b_tmp = view(r_v, 0, 1024, "p (r k c) -> p r k c", r=2, k=BLK)
        b_wide = view(r_ga, 0, 2048, "p (r k g c) -> p r k g c", r=2, k=BLK, g=2)
        b_wide_f = r_ga
        bT = view(r_v, 0, 2048, "p (n m) -> p n m", m=P)
        cw = xT[:, :, :].rearrange("p a t -> p (a t)").rearrange("p (r k m) -> p r k m", r=2, k=BLK)
        zuT = view(r_zu, 0, 2048, "p (k t) -> p k t", t=TOK)
        zv = view(r_zv, 0, 2048, "p (b d) -> p b d", b=TB)
        gaT = view(r_ga, 0, 2048, "p (k t) -> p k t", t=TOK)
        gbT = view(r_gb, 0, 2048, "p (k t) -> p k t", t=TOK)
        kT = view(r_k, 0, 2048, "p (k t) -> p k t", t=TOK)
        v_t = view(r_v, 0, 2048, "p (b d) -> p b d", b=TB)
        ygT = memT[:, 0:4, :]
        yaT = memT[:, 4:8, :]
        sbias = yaT.rearrange("p a t -> p (a t)")
        prob = view(r_zv, 0, 1024, "p (n b m) -> p n b m", n=2, b=TB)
        probT = view(r_zv, 1024, 1024, "p (n b l) -> p n b l", n=2, b=TB)
        logit = uT[:, :, :].rearrange("p a t -> p (a t)").rearrange("p (n b m) -> p n b m", n=2, b=TB)
        qT = zuT
        oT = xT
        silu = view(r_zu, 0, 1024, "p (n m) -> p n m", n=2)
        hT = view(r_zu, 1024, 1024, "p (n j t) -> p n j t", n=2, j=2)
        nabias = [view(big, 4096 * m, 4096, "p (h b m) -> p h b m", h=8, b=TB) for m in range(2)]
        bc = view(big, 8192, 7168, "p (n d) -> p n d", d=D)
        swmask = big[:, 15360:15872].rearrange("p (b m) -> p b m", b=TB)
        rope = big[:, 15872:15904].rearrange("p (b c f) -> p b c f", b=TB, c=2)
        wr = big[:, 15904:15968].rearrange("p (k e) -> p k e", e=8)
        before = big[:, 15968:16096]
        iota = big[:, 16096:16224]
        qk_t = view(r_gb, 0, 1536, "p (b d) -> p b d", b=TB)
        rtmp = view(r_zv, 0, 2048, "p (n b m) -> p n b m", n=8, b=TB)
        qnT = view(r_zu, 0, 1024, "p (k t) -> p k t", t=TOK)
        knT = view(r_zu, 1024, 1024, "p (k t) -> p k t", t=TOK)
        v_na = view(r_v, 0, 1024, "p (b d) -> p b d", b=TB)
        onT = view(r_v, 1024, 1024, "p (k t) -> p k t", t=TOK)
        qsT = view(r_k, 0, 1024, "p (k t) -> p k t", t=TOK)
        ksT = r_k[:, 1024:1280]
        v_sw = view(r_k, 1280, 256, "p (b d) -> p b d", b=TB)
        osT = view(memT[:, :, :].rearrange("p a t -> p (a t)"), 0, 1024, "p (k t) -> p k t", t=TOK)

        slot_full = [sem(f"slot_full{i}") for i in range(SLOTS)]
        chunk_used = sem("chunk_used")
        bank_full = [sem(f"bank_full{i}") for i in range(BANKS)]
        bank_free = [sem(f"bank_free{i}") for i in range(BANKS)]
        loads = {n: sem("ld_" + n) for n in (
            "x", "mem", "ident", "gains", "prm", "b", "lnv", "sgu", "sbias", "s5d", "cw", "bgate", "sink",
            "nab", "bc0", "bcn", "consts")}
        dve_step = sem("dve_step")
        scan_step = sem("scan_step")
        var_ready = sem("var_ready")
        std_ready = sem("std_ready")
        xn_ready = sem("xn_ready")
        memn_ready = sem("memn_ready")
        bwide_ready = sem("bwide_ready")
        prm_exp = sem("prm_ready")
        sin_ready = sem("sin_ready")
        zvn_ready = sem("zvn_ready")
        scan_done = sem("scan_done")
        cneg_ready = sem("cneg_ready")
        yg_ready = sem("yg_ready")
        ya_ready = sem("ya_ready")
        m_ready = sem("m_ready")
        negm_ready = sem("negm_ready")
        exp_ready = sem("exp_ready")
        prob_ready = sem("prob_ready")
        g_full = sem("gate_full")
        u_full = sem("up_full")
        silu_ready = sem("silu_ready")
        hT_ready = sem("hT_ready")
        down_done = sem("down_done")
        acc_free = sem("acc_free")
        qk_roped = sem("qk_roped")
        rexp_in = sem("rexp_in")
        rexp_out = sem("rexp_out")
        mask_ready = sem("mask_ready")
        table_ready = sem("table_ready")
        pick_ready = sem("pick_ready")
        gathered = sem("gathered")
        w_high = sem("w_high")
        w_split = sem("w_split")
        w_used = sem("w_used")
        h_high = sem("h_high")
        h_split = sem("h_split")
        xe_high = sem("xe_high")
        xe_split = sem("xe_split")
        hT_high = sem("hT_high")
        hT_full = sem("hT_full")
        hT_moved = sem("hT_moved")
        oe_full = sem("oe_full")
        oe_high = sem("oe_high")
        oe_split = sem("oe_split")
        pickT_full = sem("pickT_full")
        pickT_ready = sem("pickT_ready")
        scattered = sem("scattered")
        y_added = sem("y_added")
        ones_ready = sem("ones_ready")
        out_ready = sem("out_ready")
        stored = sem("stored")

        def bank(u):
            return psum[:, UNIT_AT[u] % BANKS, :]

        def open_unit(pe, u):
            n = UNIT_AT[u]
            if n >= BANKS:
                pe.wait_ge(bank_free[n % BANKS], n // BANKS)

        def close_unit(last, u):
            last.then_inc(bank_full[UNIT_AT[u] % BANKS], 1)

        def take_unit(eng, u):
            n = UNIT_AT[u]
            eng.wait_ge(bank_full[n % BANKS], n // BANKS + 1)

        def free_unit(last, u):
            last.then_inc(bank_free[UNIT_AT[u] % BANKS], 1)

        def evacuated(eng, u):
            n = UNIT_AT[u]
            eng.wait_ge(bank_free[n % BANKS], n // BANKS + 1)

        def halves(ap):
            return ap.rearrange("p (b c) -> p b c", b=2)

        passes = [("x", 4)] + [(f"{k}{m}", 8) for m in range(2) for k in ("na", "sw")]
        head0 = {}
        n = 0
        for name, heads in passes:
            head0[name] = n
            n += heads
        ff0 = {"ffn": 0, "dense": FF_STEPS, "moe": 2 * FF_STEPS}
        ffn_no = {"ffn": 1, "dense": 2, "moe": 3}

        def sink_col(m, i):
            head = i // 2 + 4 * (i % 2)
            return sink[:, m, head:head + 1]

        block = ctx.enter_context(nc.Block())

        @block.sync
        def _(sp):
            for j in range(SLOTS):
                sp.dma_start(ring[:, j, :], a["stream"][j, :, :]).then_inc(slot_full[j], 16)
            with sp.Fori(1, MOE_C0 // SLOTS + 1) as r:
                for j in range(SLOTS):
                    sp.wait_ge(chunk_used, r * SLOTS - SLOTS + j + 1)
                    sp.dma_start(ring[:, j, :], a["stream"][bass.ds(r * SLOTS + j, 1), :, :]
                                 .rearrange("a p f -> (a p) f")).then_inc(slot_full[j], 16)
            with sp.Fori(MOE_C0 // SLOTS + 1, len(CHUNKS) // SLOTS) as r:
                for j in range(SLOTS):
                    sp.wait_ge(w_split, r * SLOTS + (j + 1 - SLOTS - MOE_C0))
                    sp.dma_start(ring[:, j, :], a["stream"][bass.ds(r * SLOTS + j, 1), :, :]
                                 .rearrange("a p f -> (a p) f")).then_inc(slot_full[j], 16)
            sp.wait_ge(table_ready, 1)
            n_over = sp.value_load(table[0:1, 1:2], min_val=0, max_val=OVER)
            with sp.If(n_over > 0):
                with sp.Fori(0, n_over) as p:
                    e = sp.value_load(table[0:1, bass.ds(p + 2, 1)], min_val=0, max_val=MOE_E - 1)
                    with sp.Fori(0, MOE_CHUNKS // SLOTS) as r:
                        for j in range(SLOTS):
                            sp.wait_ge(w_split, p * MOE_CHUNKS + r * SLOTS + (len(CHUNKS) - MOE_C0 - SLOTS + j + 1))
                            sp.dma_start(ring[:, j, :], a["stream"][bass.ds(e * MOE_CHUNKS + r * SLOTS + (MOE_C0 + j), 1), :, :]
                                         .rearrange("a p f -> (a p) f")).then_inc(slot_full[j], 16)
            for j in range(AHEAD):
                sp.wait_ge(w_split, n_over * MOE_CHUNKS + (len(CHUNKS) - MOE_C0 - SLOTS + j + 1))
                sp.dma_start(ring[:, j, :], a["stream"][MOE_C0 + j, :, :]).then_inc(slot_full[j], 16)

        @block.gpsimd
        def _(pool):
            for q in range(4):
                take_unit(pool, ("y", q))
            for m in range(2):
                pool.dma_start(nabias[m], a["na_bias"][m]).then_inc(loads["nab"], 16)
            for n in range(7):
                pool.dma_start(bc[:, n, :], a["bc"][n:n + 1, :].to_broadcast([P, D])).then_inc(loads["bc0"], 16)
            pool.dma_start(swmask, a["sw_mask"]).then_inc(loads["consts"], 16)
            pool.dma_start(rope, a["rope"]).then_inc(loads["consts"], 16)
            pool.dma_start(wr, a["router"]).then_inc(loads["consts"], 16)
            pool.dma_start(before, a["before"]).then_inc(loads["consts"], 16)
            pool.dma_start(iota, a["iota"]).then_inc(loads["consts"], 16)
            for n in range(4):
                pool.wait_ge(xn_ready, 5 + n // 2)
                pool.dma_start(bc[:, 3 + n, :], a["bc"][7 + n:8 + n, :].to_broadcast([P, D])
                               ).then_inc(loads["bcn"], 16)

        @block.tensor
        def _(pe):
            def weights(c):
                n = CHUNK_AT[c]
                pe.wait_ge(slot_full[n % SLOTS], 16 * (n // SLOTS + 1))
                k = {"k8": KD, "k4": 4, "k2": 2}[c[0]]
                return ring[:, n % SLOTS, :].rearrange("p (k c) -> p k c", k=k)

            def release(first, chunk):
                if CHUNK_AT[chunk] > 0:
                    first.then_inc(chunk_used, 1)

            def transposes(u0, src, n_units=4):
                for u in range(n_units):
                    open_unit(pe, (u0, u))
                    for j in range(2):
                        for b in range(TB):
                            last = nc.tensor.transpose(
                                bank((u0, u))[:, (2 * j + b) * P:(2 * j + b + 1) * P],
                                src[:, b, (2 * u + j) * P:(2 * u + j + 1) * P], ident[:, :])
                    close_unit(last, (u0, u))

            def form_a(unit, chunk, act_T):
                open_unit(pe, unit)
                w = weights(chunk)
                for j in range(2):
                    for k in range(KD):
                        last = nc.tensor.matmul(bank(unit)[:, j * TOK:(j + 1) * TOK], w[:, k, j * P:(j + 1) * P],
                                                act_T[:, k, :], start=(k == 0), stop=(k == KD - 1))
                        if j == k == 0:
                            release(last, chunk)
                close_unit(last, unit)

            def form_a4(name, chunk, act_T, u0):
                w = weights(chunk)
                for u in range(2):
                    open_unit(pe, (name, u0 + u))
                    for j in range(2):
                        for k in range(4):
                            last = nc.tensor.matmul(
                                bank((name, u0 + u))[:, j * TOK:(j + 1) * TOK],
                                w[:, k, (2 * u + j) * P:(2 * u + j + 1) * P],
                                act_T[:, k, :], start=(k == 0), stop=(k == 3))
                            if u == j == k == 0:
                                release(last, chunk)
                    close_unit(last, (name, u0 + u))

            def form_b(unit, chunk, act_T):
                open_unit(pe, unit)
                w = weights(chunk)
                for b in range(TB):
                    for k in range(KD):
                        last = nc.tensor.matmul(bank(unit)[:, b * 256:(b + 1) * 256],
                                                act_T[:, k, b * P:(b + 1) * P], w[:, k, :],
                                                start=(k == 0), stop=(k == KD - 1))
                        if b == k == 0:
                            release(last, chunk)
                close_unit(last, unit)

            def attention(name, heads, kd, q_of, k_of, v_of, o_rows, dblocks):
                g0 = head0[name]
                for i in range(heads + 2):
                    if i < heads:
                        u = (name + "_s", i)
                        open_unit(pe, u)
                        for b in range(TB):
                            for k in range(kd):
                                last = nc.tensor.matmul(bank(u)[:, b * 256:(b + 1) * 256],
                                                        q_of(i, k)[:, b * P:(b + 1) * P], k_of(i, k),
                                                        start=(k == 0), stop=(k == kd - 1))
                        close_unit(last, u)
                    if 0 <= i - 1 < heads:
                        u = (name + "_t", i - 1)
                        g = g0 + i - 1
                        pe.wait_ge(prob_ready, g + 1)
                        open_unit(pe, u)
                        for m in range(TB):
                            for b in range(TB):
                                last = nc.tensor.transpose(
                                    bank(u)[:, (2 * m + b) * P:(2 * m + b + 1) * P],
                                    prob[:, g % 2, b, m * P:(m + 1) * P], ident[:, :])
                        close_unit(last, u)
                    if 0 <= i - 2 < heads:
                        u = (name + "_o", i - 2)
                        g = g0 + i - 2
                        evacuated(pe, (name + "_t", i - 2))
                        open_unit(pe, u)
                        r0, rn = o_rows(i - 2)
                        for j in range(dblocks):
                            for m in range(TB):
                                last = nc.tensor.matmul(bank(u)[r0:r0 + rn, j * TOK:(j + 1) * TOK],
                                                        v_of(i - 2, j, m), probT[:, g % 2, m, :],
                                                        start=(m == 0), stop=(m == TB - 1))
                        close_unit(last, u)

            def gate_up(name, s):
                for o, part, full in ((0, "_gate", g_full), (1, "_up", u_full)):
                    product_gu(2 * (s % 2) + o, weights(("k8", name + part, s)), full)

            def product_gu(b, w, full):
                for j in range(2):
                    for k in range(KD):
                        last = nc.tensor.matmul(psum[:, b, j * TOK:(j + 1) * TOK], w[:, k, j * P:(j + 1) * P],
                                                xT[:, k, :], start=(k == 0), stop=(k == KD - 1))
                        if j == k == 0:
                            last.then_inc(chunk_used, 1)
                last.then_inc(full, 1)

            def down(s, w, first, final):
                for k in range(2):
                    for b in range(TB):
                        for c in range(2):
                            last = nc.tensor.matmul(psum[:, 4 + 2 * b + c, :], hT[:, s % 2, k, b * P:(b + 1) * P],
                                                    w[:, k, c * 512:(c + 1) * 512],
                                                    start=(first and k == 0), stop=(final and k == 1),
                                                    skip_group_check=True)
                            if k == b == c == 0:
                                last.then_inc(chunk_used, 1)
                last.then_inc(down_done, 1)

            def all_banks_free(next_unit):
                n = next_unit
                for b in range(BANKS):
                    used = (n - b + BANKS - 1) // BANKS
                    if used > 0:
                        pe.wait_ge(bank_free[b], used)

            def ffn(name, steps, next_unit):
                f0 = ff0[name]
                all_banks_free(next_unit)
                for s in range(steps + 1):
                    if s < steps:
                        if s >= 2:
                            pe.wait_ge(hT_ready, f0 + s - 1)
                        gate_up(name, s)
                    if s >= 1:
                        pe.wait_ge(hT_ready, f0 + s)
                        down(s - 1, weights(("k2", name + "_down", s - 1)), s == 1, s == steps)

            pe.wait_ge(loads["ident"], 16)
            pe.wait_ge(xn_ready, 1)
            transposes("t_x", xn)
            pe.wait_ge(memn_ready, 1)
            transposes("t_mem", n_mem)
            evacuated(pe, ("t_x", 3))
            for i in range(2):
                form_a(("xa", i), ("k8", "w_in", i), xT)
            for i in range(4):
                form_b(("zv", i), ("k8", "w_in", 2 + i), xT)
            pe.wait_ge(bwide_ready, 1)
            for u in range(4):
                open_unit(pe, ("t_b", u))
                for j in range(4):
                    last = nc.tensor.transpose(bank(("t_b", u))[:, j * P:(j + 1) * P],
                                               b_wide_f[:, (4 * u + j) * P:(4 * u + j + 1) * P], ident[:, :])
                close_unit(last, ("t_b", u))
            evacuated(pe, ("t_b", 3))
            evacuated(pe, ("xa", 1))
            for blk in range(BLK):
                pair = blk % PAIRS
                r0 = 32 * (pair % 4)
                open_unit(pe, ("bu", blk))
                for r in range(2):
                    last = nc.tensor.matmul(bank(("bu", blk))[:, r * TOK:(r + 1) * TOK],
                                            bT[r0:r0 + 32, r * 8 + blk // 4, :],
                                            uT[r0:r0 + 32, pair // 4, :], start=True, stop=True)
                close_unit(last, ("bu", blk))
            for i in range(4):
                form_a(("zu", i), ("k8", "w_in", 6 + i), xT)
            for i in range(4):
                form_a(("ga", i), ("k8", "w_in", 10 + i), xT)
            for i in range(4):
                form_a(("gb", i), ("k8", "w_in", 14 + i), xT)
            evacuated(pe, ("t_mem", 3))
            for i in range(4):
                form_a(("k", i), ("k8", "w_k", i), memT)
            for i in range(4):
                form_b(("v", i), ("k8", "w_v", i), memT)
            pe.wait_ge(zvn_ready, 1)
            pe.wait_ge(loads["sgu"], 16)
            pe.wait_ge(loads["sbias"], 16)
            pe.wait_ge(ones_ready, 1)
            for u in range(4):
                open_unit(pe, ("sgu", u))
                for j in range(2):
                    hd = 2 * u + j
                    for b in range(TB):
                        o = bank(("sgu", u))[:, j * TOK + b * P:j * TOK + (b + 1) * P]
                        nc.tensor.matmul(o, zv[:, b, hd * P:(hd + 1) * P], sguT[:, hd, :], start=True, stop=False)
                        last = nc.tensor.matmul(o, ones[0:1, :], sbias[0:1, hd * P:(hd + 1) * P],
                                                start=False, stop=True)
                close_unit(last, ("sgu", u))
            evacuated(pe, ("sgu", 3))
            for i in range(4):
                form_a(("pb", i), ("k8", "w_proj_b", i), zuT)
            pe.wait_ge(scan_done, 1)
            pe.wait_ge(cneg_ready, 1)
            for q in range(4):
                open_unit(pe, ("y", q))
                for i in range(4):
                    pair = 4 * q + i
                    for n in range(4):
                        d, r = n // 2, n % 2
                        blk = d * PAIRS + pair
                        rhs = states[:, :, r, blk] if d == 0 else states[:, ::-1, r, blk]
                        last = nc.tensor.matmul(bank(("y", q))[32 * i:32 * i + 32, 0:TOK],
                                                cw[:, r, blk, :], rhs, start=(n == 0), stop=(n == 3))
                close_unit(last, ("y", q))
            pe.wait_ge(yg_ready, 4)
            form_a4("glu", ("k4", "s5_w_glu", 0), ygT, 0)
            pe.wait_ge(ya_ready, 2)
            for c in range(2):
                form_a4("pa", ("k4", "w_proj_a", c), yaT, 2 * c)
            pe.wait_ge(m_ready, 4)
            for i in range(4):
                form_b(("out", i), ("k8", "w_out", i), gaT)
            pe.wait_ge(xn_ready, 2)
            transposes("t_xattn", xn)
            evacuated(pe, ("t_xattn", 3))
            for i in range(4):
                form_a(("q", i), ("k8", "w_q", i), xT)
            evacuated(pe, ("q", 3))
            evacuated(pe, ("v", 3))
            attention("x", 4, 2, lambda i, k: qT[:, 2 * i + k, :], lambda i, k: kT[:, 2 * i + k, :],
                      lambda i, j, m: v_t[:, m, (2 * i + j) * P:(2 * i + j + 1) * P], lambda i: (0, P), 2)
            evacuated(pe, ("x_o", 3))
            for i in range(4):
                form_b(("xo", i), ("k8", "w_xo", i), oT)
            pe.wait_ge(xn_ready, 3)
            transposes("t_ffn", xn)
            evacuated(pe, ("t_ffn", 3))
            ffn("ffn", FF_STEPS, UNIT_AT[("t_in0", 0)])

            for m in range(2):
                pe.wait_ge(acc_free, 1 + m)
                pe.wait_ge(xn_ready, 4 + 2 * m)
                transposes(f"t_in{m}", h)
                evacuated(pe, (f"t_in{m}", 3))
                for i in range(5):
                    form_b((f"projb{m}", i), ("k8", f"w_in_{m}", i), xT)
                for i in range(4):
                    form_a((f"qk{m}", i), ("k8", f"w_in_{m}", 5 + i), xT)
                for i in range(4):
                    form_a((f"ga{m}", i), ("k8", f"w_in_{m}", 9 + i), xT)
                pe.wait_ge(qk_roped, m + 1)
                for u in range(3):
                    open_unit(pe, (f"t_sw{m}", u))
                    for j in range(2 if u < 2 else 1):
                        for b in range(TB):
                            last = nc.tensor.transpose(
                                bank((f"t_sw{m}", u))[:, (2 * j + b) * P:(2 * j + b + 1) * P],
                                qk_t[:, b, (2 * u + j) * P:(2 * u + j + 1) * P], ident[:, :])
                    close_unit(last, (f"t_sw{m}", u))
                for i in range(4):
                    form_a((f"gb{m}", i), ("k8", f"w_in_{m}", 13 + i), xT)
                evacuated(pe, (f"qk{m}", 3))
                evacuated(pe, (f"t_sw{m}", 2))
                attention(f"na{m}", 8, 1,
                          lambda i, k: qnT[64 * (i % 2):64 * (i % 2) + 64, i // 2, :],
                          lambda i, k: knT[64 * (i % 2):64 * (i % 2) + 64, i // 2, :],
                          lambda i, j, mb: v_na[:, mb, i * 64:(i + 1) * 64], lambda i: (64 * (i % 2), 64), 1)
                attention(f"sw{m}", 8, 1,
                          lambda i, k: qsT[64 * (i % 2):64 * (i % 2) + 64, i // 2, :],
                          lambda i, k: ksT[64 * (i % 2):64 * (i % 2) + 64, :],
                          lambda i, j, mb: v_sw[:, mb, (i % 2) * 64:(i % 2) * 64 + 64],
                          lambda i: (64 * (i % 2), 64), 1)
                evacuated(pe, (f"na{m}_o", 7))
                for c in range(2):
                    form_a4(f"bna{m}", ("k4", f"w_na_{m}", c), onT, 2 * c)
                evacuated(pe, (f"sw{m}_o", 7))
                for c in range(2):
                    form_a4(f"bsw{m}", ("k4", f"w_sw_{m}", c), osT, 2 * c)
                pe.wait_ge(m_ready, 4 + 4 * (m + 1))
                for i in range(4):
                    form_b((f"out{m}", i), ("k8", f"w_out_{m}", i), gaT)
                pe.wait_ge(xn_ready, 5 + 2 * m)
                transposes(f"t_mid{m}", h)
                evacuated(pe, (f"t_mid{m}", 3))
                if m == 0:
                    ffn("dense", FF_STEPS, UNIT_AT[("t_in1", 0)])

            pe.wait_ge(loads["consts"], 80)
            open_unit(pe, ("router", 0))
            for b in range(TB):
                for k in range(KD):
                    last = nc.tensor.matmul(bank(("router", 0))[:, b * 8:(b + 1) * 8], xT[:, k, b * P:(b + 1) * P],
                                            wr[:, k, :], start=(k == 0), stop=(k == KD - 1))
                    if b == k == 0:
                        last.then_inc(chunk_used, 1)
            close_unit(last, ("router", 0))
            pe.wait_ge(mask_ready, 1)
            open_unit(pe, ("pos", 0))
            pos = bank(("pos", 0))
            nc.tensor.matmul(pos[:, 0:8], before, mask[:, 0, :], start=True, stop=True)
            nc.tensor.matmul(pos[:, 8:16], ones[:, :], mask[:, 0, :], start=True, stop=False)
            nc.tensor.matmul(pos[:, 8:16], before, mask[:, 1, :], start=False, stop=True)
            nc.tensor.matmul(pos[:, 16:24], ones[:, :], mask[:, 0, :], start=True, stop=False)
            close_unit(nc.tensor.matmul(pos[:, 16:24], ones[:, :], mask[:, 1, :], start=False, stop=True),
                       ("pos", 0))
            all_banks_free(len(UNITS))

            def gather():
                for k in range(KD):
                    for b in range(TB):
                        for part in (h_h, h_l):
                            last = nc.tensor.matmul(psum[:, 6 + k // 4, (k % 4) * P:(k % 4 + 1) * P],
                                                    part[:, b, k * P:(k + 1) * P], pick[:, b, :],
                                                    start=(b == 0 and part is h_h), stop=(b == 1 and part is h_l))
                last.then_inc(gathered, 1)

            def transpose_pick():
                for b in range(TB):
                    last = nc.tensor.transpose(psum[:, 3, b * P:(b + 1) * P], pick[:, b, :].bitcast(F32), ident[:, :])
                last.then_inc(pickT_full, 1)

            pe.wait_ge(h_split, 1)
            pe.wait_ge(pick_ready, 1)
            gather()
            transpose_pick()
            f0 = ff0["moe"]
            pe.wait_ge(table_ready, 1)
            n_pass = pe.value_load(table[0:1, 0:1], min_val=MOE_E, max_val=MOE_E + OVER)
            with pe.Fori(0, n_pass) as p:
                chunk = [0]

                def next_chunk(k):
                    n = chunk[0]
                    chunk[0] += 1
                    pe.wait_ge(w_split, p * MOE_CHUNKS + (n + 1))
                    return [w[:, n % SPLITS, :].rearrange("p (k c) -> p k c", k=k) for w in (w_h, w_l)]

                def half_product(s, o):
                    wh, wl = next_chunk(KD)
                    out = psum[:, s % 2, o * 256:(o + 1) * 256]
                    for k in range(KD):
                        first = nc.tensor.matmul(out, xe_h[:, k, :], wh[:, k, :], start=(k == 0), stop=False)
                        if k == 0:
                            first.then_inc(w_used, 1)
                        nc.tensor.matmul(out, xe_h[:, k, :], wl[:, k, :], start=False, stop=False)
                        last = nc.tensor.matmul(out, xe_l[:, k, :], wh[:, k, :], start=False, stop=(k == KD - 1))
                    if o == 1:
                        last.then_inc(u_full, 1)

                def transpose_h(s):
                    pe.wait_ge(hT_ready, p * MOE_PER + (f0 + s + 1))
                    for k in range(2):
                        last = nc.tensor.transpose(psum[:, 2, (2 * (s % 2) + k) * P:(2 * (s % 2) + k + 1) * P],
                                                   e_h[:, s % 2, k * P:(k + 1) * P], ident[:, :])
                    last.then_inc(hT_full, 1)

                def expert_down(s):
                    pe.wait_ge(hT_moved, p * MOE_PER + (s + 1))
                    wh, wl = next_chunk(2)
                    for k in range(2):
                        for n, (x, w) in enumerate(((eT_h, wh), (eT_h, wl), (eT_l, wh))):
                            for c in range(2):
                                last = nc.tensor.matmul(psum[:, 4 + c, :], x[:, s % 2, k, :],
                                                        w[:, k, c * 512:(c + 1) * 512],
                                                        start=(s == 0 and k == n == 0),
                                                        stop=(s == MOE_PER - 1 and k == 1 and n == 2),
                                                        skip_group_check=True)
                                if k == n == c == 0:
                                    last.then_inc(w_used, 1)
                    if s == MOE_PER - 1:
                        last.then_inc(oe_full, 1)

                pe.wait_ge(xe_split, p + 1)
                for s in range(MOE_PER):
                    if s < 2:
                        pe.wait_ge(y_added, p * 4 + (s + 1))
                    pe.wait_ge(hT_ready, p * MOE_PER + (f0 + s - 1))
                    half_product(s, 0)
                    half_product(s, 1)
                    if s == 2:
                        pe.wait_ge(y_added, p * 4 + 4)
                    if s >= 2:
                        expert_down(s - 2)
                    if s >= 1:
                        transpose_h(s - 1)
                expert_down(MOE_PER - 2)
                transpose_h(MOE_PER - 1)
                pe.wait_ge(pick_ready, p + 2)
                gather()
                expert_down(MOE_PER - 1)
                transpose_pick()
                pe.wait_ge(oe_split, p + 1)
                pe.wait_ge(pickT_ready, p + 1)
                for b in range(TB):
                    for c in range(2):
                        nc.tensor.matmul(psum[:, 4 * b + c, :], pickT[:, b, :], o_h[:, c, :], start=True, stop=False)
                        nc.tensor.matmul(psum[:, 4 * b + c, :], pickT[:, b, :], o_l[:, c, :],
                                         start=False, stop=True).then_inc(scattered, 1)

        @block.scalar
        def _(act):
            def load(dst, src, name):
                act.dma_start(dst, src).then_inc(loads[name], 16)

            load(h[:, :, :], a["x"].rearrange("a (b p) d -> p (a b) d", p=P), "x")
            load(x_mem, a["mem"].rearrange("a (b p) d -> p (a b) d", p=P), "mem")
            load(ident[:, :], a["ident"], "ident")
            load(gains[:, :, :], a["gains"], "gains")
            load(pt[:, 0:3, :], a["s5_prm"], "prm")
            load(b_raw, a["s5_b"], "b")
            load(ln_v, a["sgu_ln"].rearrange("(o a) d -> o a d", o=1).to_broadcast([P, 2, D]), "lnv")
            load(sguT[:, :, :], a["sgu_w"], "sgu")
            load(s5d[:, :], a["s5_d"], "s5d")
            load(bgate[:, :, :], a["b_gate"], "bgate")
            load(sink[:, :, :], a["sink"].rearrange("(o a) d -> o a d", o=1).to_broadcast([P, 2, 8]), "sink")

            stds = [0]

            def std():
                stds[0] += 1
                act.wait_ge(var_ready, stds[0])
                nc.scalar.activation(sd[:, :], ve[:, :], ACT.Sqrt).then_inc(std_ready, 1)

            def copy_T(u0, dst, gain=None):
                for u in range(4):
                    take_unit(act, (u0, u))
                    for j in range(2):
                        src = bank((u0, u))[:, j * TOK:(j + 1) * TOK]
                        k = 2 * u + j
                        if gain is None:
                            last = nc.scalar.activation(dst[:, k, :], src, ACT.Copy)
                        else:
                            last = nc.scalar.activation(dst[:, k, :], src, ACT.Identity,
                                                        scale=gains[:, gain, k:k + 1])
                    free_unit(last, (u0, u))

            def out_of(u, dst, func):
                take_unit(act, u)
                free_unit(nc.scalar.activation(dst, halves(bank(u)), func), u)

            def attention(name, heads, direct, dst_of, rows_of, dblocks, sink_of=None):
                g0 = head0[name]
                for i in range(heads + 2):
                    if i < heads:
                        g = g0 + i
                        act.wait_ge(negm_ready, g + 1)
                        if sink_of is not None:
                            nc.scalar.activation(esink[:, g % 2, :], negm[:, g % 2, :], ACT.Exp, bias=sink_of(i))
                        for b in range(TB):
                            src = bank((name + "_s", i))[:, b * 256:(b + 1) * 256] if direct else logit[:, g % 2, b, :]
                            last = nc.scalar.activation(prob[:, g % 2, b, :], src, ACT.Exp,
                                                        bias=negm[:, g % 2, b:b + 1],
                                                        scale=XSCALE if direct else 1.0,
                                                        accum_out=ssum[:, g % 2, b:b + 1])
                        last.then_inc(exp_ready, 1)
                    if 0 <= i - 1 < heads:
                        u, g = (name + "_t", i - 1), g0 + i - 1
                        take_unit(act, u)
                        last = nc.scalar.activation(probT[:, g % 2, :, :], halves(bank(u)), ACT.Copy)
                        free_unit(last, u)
                    if 0 <= i - 2 < heads:
                        u = (name + "_o", i - 2)
                        take_unit(act, u)
                        r0, rn = rows_of(i - 2)
                        src = bank(u)[r0:r0 + rn, 0:dblocks * TOK]
                        last = nc.scalar.activation(dst_of(i - 2), src if dblocks == 1 else halves(src), ACT.Copy)
                        free_unit(last, u)

            def ffn_silu(name, steps):
                f0 = ff0[name]
                for s in range(steps):
                    act.wait_ge(g_full, f0 + s + 1)
                    if s >= 2:
                        act.wait_ge(hT_ready, f0 + s - 1)
                    nc.scalar.activation(silu[:, s % 2, :], psum[:, 2 * (s % 2), :], ACT.Silu).then_inc(silu_ready, 1)

            std()
            act.wait_ge(loads["gains"], 16)
            copy_T("t_x", xT, 0)
            std()
            copy_T("t_mem", memT, 1)
            for i in range(2):
                out_of(("xa", i), uT[:, 2 * i:2 * i + 2, :], ACT.Copy)
            act.wait_ge(prm_exp, 1)
            nc.scalar.activation(pt[:, 20, :], pt[:, 12, :], ACT.Sin)
            nc.scalar.activation(pt[:, 21, :], pt[:, 12, :], ACT.Sin, scale=0.5).then_inc(sin_ready, 1)
            for i in range(4):
                out_of(("zv", i), zv[:, :, i * 256:(i + 1) * 256], ACT.Gelu_apprx_tanh)
            std()
            for u in range(4):
                take_unit(act, ("t_b", u))
                last = nc.scalar.activation(bT[:, 4 * u:4 * u + 4, :],
                                            bank(("t_b", u)).rearrange("p (n m) -> p n m", m=P), ACT.Copy)
                free_unit(last, ("t_b", u))
            for blk in range(0, BLK, 2):
                take_unit(act, ("bu", blk))
                dst = states[:, :, :, blk] if blk < PAIRS else states[:, ::-1, :, blk]
                last = nc.scalar.activation(dst.rearrange("p t r -> p r t"), halves(bank(("bu", blk))), ACT.Copy)
                free_unit(last, ("bu", blk))
            for i in range(4):
                out_of(("zu", i), zuT[:, 2 * i:2 * i + 2, :], ACT.Gelu_apprx_tanh)
            for i in range(4):
                out_of(("ga", i), gaT[:, 2 * i:2 * i + 2, :], ACT.Sigmoid)
            for i in range(4):
                out_of(("gb", i), gbT[:, 2 * i:2 * i + 2, :], ACT.Sigmoid)
            act.dma_start(cw, a["s5_c"]).then_inc(loads["cw"], 16)
            act.wait_ge(zvn_ready, 1)
            for i in range(4):
                out_of(("k", i), kT[:, 2 * i:2 * i + 2, :], ACT.Copy)
            for i in range(4):
                out_of(("v", i), v_t[:, :, i * 256:(i + 1) * 256], ACT.Copy)
            act.dma_start(sbias[0:1, :], a["sgu_bias"]).then_inc(loads["sbias"], 16)
            for q in range(4):
                evacuated(act, ("y", q))
                nc.scalar.activation(ygT[:, q, :], ygT[:, q, :], ACT.Gelu_apprx_tanh).then_inc(yg_ready, 1)
            for i in range(2):
                take_unit(act, ("glu", i))
                last = nc.scalar.activation(yaT[:, 2 * i:2 * i + 2, :], halves(bank(("glu", i))), ACT.Sigmoid)
                free_unit(last, ("glu", i))
            std()
            copy_T("t_xattn", xT, 2)
            for i in range(4):
                out_of(("q", i), qT[:, 2 * i:2 * i + 2, :], ACT.Copy)
            attention("x", 4, True, lambda i: oT[:, 2 * i:2 * i + 2, :], lambda i: (0, P), 2)
            std()
            copy_T("t_ffn", xT, 3)
            ffn_silu("ffn", FF_STEPS)
            std()
            std()
            act.wait_ge(loads["bgate"], 16)
            for m in range(2):
                copy_T(f"t_in{m}", xT)
                for i in range(2):
                    out_of((f"projb{m}", i), v_na[:, :, i * 256:(i + 1) * 256], ACT.Copy)
                for i in range(2):
                    out_of((f"projb{m}", 2 + i), qk_t[:, :, i * 256:(i + 1) * 256], ACT.Copy)
                u = (f"projb{m}", 4)
                take_unit(act, u)
                nc.scalar.activation(qk_t[:, :, 512:640], halves(bank(u))[:, :, 0:128], ACT.Copy)
                last = nc.scalar.activation(v_sw, halves(bank(u))[:, :, 128:256], ACT.Copy)
                free_unit(last, u)
                for i in range(2):
                    out_of((f"qk{m}", i), qnT[:, 2 * i:2 * i + 2, :], ACT.Copy)
                for i in range(2):
                    out_of((f"qk{m}", 2 + i), knT[:, 2 * i:2 * i + 2, :], ACT.Copy)

                def gates(name, dst, col0):
                    for i in range(4):
                        take_unit(act, (name, i))
                        for j in range(2):
                            k = 2 * i + j
                            last = nc.scalar.activation(dst[:, k, :], bank((name, i))[:, j * TOK:(j + 1) * TOK],
                                                        ACT.Sigmoid, bias=bgate[:, m, col0 + k:col0 + k + 1])
                        free_unit(last, (name, i))

                gates(f"ga{m}", gaT, 0)
                for u in range(3):
                    take_unit(act, (f"t_sw{m}", u))
                    if u < 2:
                        last = nc.scalar.activation(qsT[:, 2 * u:2 * u + 2, :], halves(bank((f"t_sw{m}", u))), ACT.Copy)
                    else:
                        last = nc.scalar.activation(ksT, bank((f"t_sw{m}", u))[:, 0:TOK], ACT.Copy)
                    free_unit(last, (f"t_sw{m}", u))
                gates(f"gb{m}", gbT, 8)
                attention(f"na{m}", 8, False, lambda i: onT[64 * (i % 2):64 * (i % 2) + 64, i // 2, :],
                          lambda i: (64 * (i % 2), 64), 1)
                attention(f"sw{m}", 8, False, lambda i: osT[64 * (i % 2):64 * (i % 2) + 64, i // 2, :],
                          lambda i: (64 * (i % 2), 64), 1, lambda i: sink_col(m, i))
                std()
                copy_T(f"t_mid{m}", xT)
                if m == 0:
                    ffn_silu("dense", FF_STEPS)
                    std()
            act.wait_ge(rexp_in, 1)
            nc.scalar.activation(rt[:, 8, :, 0], rt[:, 7, :, 0], ACT.Exp).then_inc(rexp_out, 1)
            f0 = ff0["moe"]

            def move_xe(n):
                act.wait_ge(gathered, n)
                nc.scalar.activation(xe_h[:, :, :].rearrange("p (b k) m -> p b (k m)", b=2), psum[:, 6:8, :],
                                     ACT.Copy).then_inc(xe_high, 1)

            def move_pickT(n):
                act.wait_ge(pickT_full, n)
                nc.scalar.activation(pickT[:, :, :], halves(psum[:, 3, 0:TOK]), ACT.Copy).then_inc(pickT_ready, 1)

            def high_part(p, n):
                act.wait_ge(slot_full[n % SLOTS], p * (16 * MOE_CHUNKS // SLOTS)
                            + 16 * (MOE_C0 // SLOTS + n // SLOTS + 1))
                nc.scalar.activation(w_h[:, n % SPLITS, :], ring[:, n % SLOTS, :], ACT.Copy).then_inc(w_high, 1)

            chunks, after = moe_events()
            act.wait_ge(h_high, 1)
            for n in range(AHEAD):
                high_part(0, n)
            move_xe(1)
            move_pickT(1)
            act.wait_ge(table_ready, 1)
            n_pass = act.value_load(table[0:1, 0:1], min_val=MOE_E, max_val=MOE_E + OVER)
            with act.Fori(0, n_pass) as p:
                for n in range(-1, len(chunks)):
                    if n >= 0:
                        for what, s in after.get(n, []):
                            if what == "prod":
                                act.wait_ge(u_full, p * MOE_PER + (f0 + s + 1))
                                nc.scalar.activation(e_silu[:, s % 2, :], psum[:, s % 2, 0:256], ACT.Silu
                                                     ).then_inc(silu_ready, 1)
                            else:
                                act.wait_ge(hT_full, p * MOE_PER + (s + 1))
                                nc.scalar.activation(eT_h[:, s % 2, :, :],
                                                     halves(psum[:, 2, 256 * (s % 2):256 * (s % 2) + 256]),
                                                     ACT.Copy).then_inc(hT_high, 1)
                    if n == len(chunks) - 2:
                        move_xe(p + 2)
                    if n + SPLITS < len(chunks) + AHEAD:
                        act.wait_ge(w_used, p * MOE_CHUNKS + (n + 2))
                        high_part(p, n + SPLITS)
                act.wait_ge(oe_full, p + 1)
                nc.scalar.activation(o_h[:, :, :], psum[:, 4:6, :], ACT.Copy).then_inc(oe_high, 1)
                act.wait_ge(scattered, p * 4 + 4)
                move_pickT(p + 2)
            std()
            act.wait_ge(out_ready, 1)
            act.dma_start(out.rearrange("a (b p) d -> p (a b) d", p=P), ysum[:, :, :]).then_inc(stored, 16)
            act.wait_ge(stored, 16)

        @block.vector
        def _(dve):
            V = nc.vector
            steps = [0]

            def link(ins):
                steps[0] += 1
                ins.then_inc(dve_step, 1)
                dve.wait_ge(dve_step, steps[0])

            norms = [0]

            def stats(src, rms, eps):
                norms[0] += 1
                for b in range(TB):
                    for c in range(2):
                        last = V.bn_stats(st[:, b, c, :], src[:, b, c * 512:(c + 1) * 512])
                link(last)
                for b in range(TB):
                    last = V.bn_aggr(mv[:, b, :], st[:, b, :, :])
                link(last)
                if rms:
                    link(V.tensor_tensor(msq[:, :], mv[:, :, 0], mv[:, :, 0], ALU.mult))
                    link(V.tensor_tensor(msq[:, :], msq[:, :], mv[:, :, 1], ALU.add))
                    V.tensor_scalar(ve[:, :], msq[:, :], eps, None, ALU.add).then_inc(var_ready, 1)
                else:
                    V.tensor_scalar(ve[:, :], mv[:, :, 1], eps, None, ALU.add).then_inc(var_ready, 1)
                dve.wait_ge(std_ready, norms[0])
                link(V.reciprocal(rstd[:, :], sd[:, :]))

            def scaled(dst, src, ready):
                for b in range(TB):
                    last = V.tensor_scalar(dst[:, b, :], src[:, b, :], rstd[:, b:b + 1], None, ALU.mult)
                last.then_inc(ready, 1)

            def layer_norm(x, g, b_, eps):
                stats(x, False, eps)
                for b in range(TB):
                    last = V.tensor_scalar(x[:, b, :], x[:, b, :], mv[:, b, 0:1], rstd[:, b:b + 1],
                                           ALU.subtract, ALU.mult)
                link(last)
                for b in range(TB):
                    last = V.tensor_tensor(x[:, b, :], x[:, b, :], g, ALU.mult)
                link(last)
                for b in range(TB):
                    last = V.tensor_tensor(x[:, b, :], x[:, b, :], b_, ALU.add)
                return last

            def residual(unit, i, alpha=None):
                take_unit(dve, unit)
                hs = h[:, :, i * 256:(i + 1) * 256]
                if alpha is None:
                    last = V.tensor_tensor(hs, hs, halves(bank(unit)), ALU.add)
                else:
                    last = V.scalar_tensor_tensor(hs, hs, alpha, halves(bank(unit)), ALU.mult, ALU.add)
                free_unit(last, unit)
                return last

            def attention(name, heads, bias_of, sink_of):
                g0 = head0[name]
                for i in range(heads + 1):
                    if i < heads:
                        g = g0 + i
                        u = (name + "_s", i)
                        take_unit(dve, u)
                        if bias_of is None:
                            link(V.reduce_max(mx[:, g % 2, :], halves(bank(u)), AX_X))
                            V.tensor_scalar(negm[:, g % 2, :], mx[:, g % 2, :], -XSCALE, None,
                                            ALU.mult).then_inc(negm_ready, 1)
                        else:
                            last = V.scalar_tensor_tensor(logit[:, g % 2, :, :], halves(bank(u)), HSCALE,
                                                          bias_of(i), ALU.mult, ALU.add)
                            free_unit(last, u)
                            evacuated(dve, u)
                            link(V.reduce_max(mx[:, g % 2, :], logit[:, g % 2, :, :], AX_X))
                            if sink_of is not None:
                                link(V.tensor_scalar(mx[:, g % 2, :], mx[:, g % 2, :], sink_of(i), None, ALU.max))
                            V.tensor_scalar(negm[:, g % 2, :], mx[:, g % 2, :], -1.0, None,
                                            ALU.mult).then_inc(negm_ready, 1)
                    if i >= 1:
                        g = g0 + i - 1
                        dve.wait_ge(exp_ready, g + 1)
                        if sink_of is not None:
                            link(V.tensor_tensor(ssum[:, g % 2, :], ssum[:, g % 2, :], esink[:, g % 2, :], ALU.add))
                        link(V.reciprocal(rsum[:, g % 2, :], ssum[:, g % 2, :]))
                        for b in range(TB):
                            last = V.tensor_scalar(prob[:, g % 2, b, :], prob[:, g % 2, b, :],
                                                   rsum[:, g % 2, b:b + 1], None, ALU.mult)
                            if b == 0 and bias_of is None:
                                free_unit(last, (name + "_s", i - 1))
                        last.then_inc(prob_ready, 1)

            def ffn_mul(name, steps_):
                f0 = ff0[name]
                for s in range(steps_):
                    dve.wait_ge(silu_ready, f0 + s + 1)
                    dve.wait_ge(u_full, f0 + s + 1)
                    if s >= 2:
                        dve.wait_ge(down_done, f0 + s - 1)
                    V.tensor_tensor(hT[:, s % 2, :, :], halves(silu[:, s % 2, :]), halves(psum[:, 2 * (s % 2) + 1, :]),
                                    ALU.mult).then_inc(hT_ready, 1)

            def add_sums(n, alpha=None):
                dve.wait_ge(down_done, FF_STEPS * n)
                for b in range(TB):
                    for c in range(2):
                        hs = h[:, b, c * 512:(c + 1) * 512]
                        acc = psum[:, 4 + 2 * b + c, :]
                        if alpha is None:
                            last = V.tensor_tensor(hs, hs, acc, ALU.add)
                        else:
                            last = V.scalar_tensor_tensor(hs, hs, alpha, acc, ALU.mult, ALU.add)
                last.then_inc(acc_free, 1)
                dve.wait_ge(acc_free, n)

            V.memset(ones[:, :], 1.0).then_inc(ones_ready, 1)
            dve.wait_ge(loads["x"], 16)
            stats(h, True, EPS)
            scaled(xn, h, xn_ready)
            dve.wait_ge(loads["mem"], 16)
            stats(x_mem, True, EPS)
            scaled(n_mem, x_mem, memn_ready)

            row = lambda n: pt[:, n, :]
            LR, LI, LS, STEP, X, KF, R, H, KI, ER = range(10)
            ANG, KA, MAG, NR, ARE, AIM, CRE, CIM, T1, T2 = 12, 10, 11, 13, 14, 15, 16, 17, 18, 19
            SN, SH = 20, 21
            magic = 1.5 * 2.0 ** 23

            def exp_of(dst, src):
                link(V.tensor_scalar(row(X), row(src), -87.0, 88.0, ALU.max, ALU.min))
                link(V.tensor_scalar(row(KF), row(X), 1.4426950408889634, magic, ALU.mult, ALU.add))
                link(V.tensor_scalar(row(KF), row(KF), magic, None, ALU.subtract))
                link(V.scalar_tensor_tensor(row(R), row(KF), -0.693359375, row(X), ALU.mult, ALU.add))
                link(V.scalar_tensor_tensor(row(R), row(KF), 2.12194440e-4, row(R), ALU.mult, ALU.add))
                link(V.tensor_scalar(row(H), row(R), 1.0 / 5040, None, ALU.mult))
                for c in (1.0 / 720, 1.0 / 120, 1.0 / 24, 1.0 / 6, 0.5, 1.0):
                    link(V.scalar_tensor_tensor(row(H), row(H), c, row(R), ALU.add, ALU.mult))
                link(V.tensor_scalar(row(KI).bitcast(I32), row(KF), 127.0, 2.0 ** 23, ALU.add, ALU.mult))
                link(V.scalar_tensor_tensor(row(dst), row(H), 1.0, row(KI), ALU.add, ALU.mult))

            dve.wait_ge(loads["prm"], 16)
            exp_of(STEP, LS)
            link(V.tensor_tensor(row(MAG), row(LR), row(STEP), ALU.mult))
            exp_of(ER, MAG)
            link(V.tensor_tensor(row(ANG), row(LI), row(STEP), ALU.mult))
            link(V.tensor_scalar(row(KA), row(ANG), 1.0 / (2 * np.pi), magic, ALU.mult, ALU.add))
            link(V.tensor_scalar(row(KA), row(KA), magic, None, ALU.subtract))
            c1 = 6.28125
            c2 = float(np.float32(np.floor((2 * np.pi - c1) * 2 ** 21) / 2 ** 21))
            c3 = float(2 * np.pi - c1 - c2)
            for c in (c1, c2, c3):
                link(V.scalar_tensor_tensor(row(ANG), row(KA), -c, row(ANG), ALU.mult, ALU.add))
            V.tensor_scalar(row(ANG), row(ANG), -3.1415925, 3.1415925, ALU.max, ALU.min).then_inc(prm_exp, 1)
            link(V.memset(b_wide_f[:, :], 0.0))
            dve.wait_ge(sin_ready, 1)
            link(V.tensor_tensor(row(SH), row(SH), row(SH), ALU.mult))
            link(V.tensor_scalar(row(SH), row(SH), -2.0, 1.0, ALU.mult, ALU.add))
            V.tensor_tensor(row(ARE), row(ER), row(SH), ALU.mult)
            link(V.tensor_tensor(row(AIM), row(ER), row(SN), ALU.mult))
            for r in range(2):
                V.tensor_copy(lam_a[:, 0, r, :], row(ARE))
            V.tensor_scalar(lam_a[:, 1, 1, :], row(AIM), -1.0, None, ALU.mult)
            V.tensor_copy(lam_a[:, 1, 0, :], row(AIM))
            link(V.tensor_scalar(row(NR), row(ARE), -1.0, None, ALU.add))
            V.tensor_tensor(row(T1), row(LR), row(LR), ALU.mult)
            link(V.tensor_tensor(row(T2), row(LI), row(LI), ALU.mult))
            link(V.tensor_tensor(row(MAG), row(T1), row(T2), ALU.add))
            link(V.reciprocal(row(MAG), row(MAG)))
            V.tensor_tensor(row(T1), row(NR), row(LR), ALU.mult)
            V.tensor_tensor(row(T2), row(AIM), row(LI), ALU.mult)
            V.tensor_tensor(row(CRE), row(AIM), row(LR), ALU.mult)
            link(V.tensor_tensor(row(CIM), row(NR), row(LI), ALU.mult))
            V.tensor_tensor(row(T1), row(T1), row(T2), ALU.add)
            link(V.tensor_tensor(row(CIM), row(CRE), row(CIM), ALU.subtract))
            V.tensor_tensor(row(CRE), row(T1), row(MAG), ALU.mult)
            link(V.tensor_tensor(row(CIM), row(CIM), row(MAG), ALU.mult))
            dve.wait_ge(loads["b"], 16)
            cre = row(CRE).unsqueeze(2).to_broadcast([P, BLK, S5_C])
            cim = row(CIM).unsqueeze(2).to_broadcast([P, BLK, S5_C])
            for out_r, (r0, r1, op) in enumerate(((0, 1, ALU.subtract), (1, 0, ALU.add))):
                V.tensor_tensor(b_tmp[:, 0], b_raw[:, r0], cre, ALU.mult)
                link(V.tensor_tensor(b_tmp[:, 1], b_raw[:, r1], cim, ALU.mult))
                for g in range(2):
                    rows = slice(64 * g, 64 * g + 64)
                    last = V.tensor_tensor(b_wide[rows, out_r, :, g, :], b_tmp[rows, 0], b_tmp[rows, 1], op)
                link(last)
            V.memset(msq[:, :], 0.0).then_inc(bwide_ready, 1)

            evacuated(dve, ("zv", 3))
            stats(zv, False, EPS)
            dve.wait_ge(loads["lnv"], 16)
            for b in range(TB):
                last = V.tensor_scalar(zv[:, b, :], zv[:, b, :], mv[:, b, 0:1], rstd[:, b:b + 1],
                                       ALU.subtract, ALU.mult)
            link(last)
            for b in range(TB):
                last = V.tensor_tensor(zv[:, b, :], zv[:, b, :], ln_v[:, 0, :], ALU.mult)
            link(last)
            for b in range(TB):
                last = V.tensor_tensor(zv[:, b, :], zv[:, b, :], ln_v[:, 1, :], ALU.add)
            last.then_inc(zvn_ready, 1)

            for blk in range(1, BLK, 2):
                take_unit(dve, ("bu", blk))
                dst = states[:, :, :, blk] if blk < PAIRS else states[:, ::-1, :, blk]
                last = V.tensor_copy(dst.rearrange("p t r -> p r t"), halves(bank(("bu", blk))))
                free_unit(last, ("bu", blk))
            evacuated(dve, ("bu", BLK - 1))
            evacuated(dve, ("bu", BLK - 2))
            per = 5
            ops = 4
            with dve.Fori(0, (TOK - 1) // per) as t:
                for j in range(per):
                    def at(o):
                        return states[:, bass.ds(t * per + (j + o), 1), :, :].rearrange("p a r k -> p (a r) k")
                    prev, cur = at(0), at(1)
                    done = t * (ops * per) + ops * j
                    V.tensor_tensor(scan_t[:, 0], prev, lam_a[:, 0], ALU.mult).then_inc(scan_step, 1)
                    V.tensor_tensor(scan_t[:, 1, ::-1, :], prev, lam_a[:, 1], ALU.mult).then_inc(scan_step, 1)
                    dve.wait_ge(scan_step, done + 1)
                    V.tensor_tensor(scan_t[:, 2], scan_t[:, 0], cur, ALU.add).then_inc(scan_step, 1)
                    dve.wait_ge(scan_step, done + 3)
                    V.tensor_tensor(cur, scan_t[:, 2], scan_t[:, 1], ALU.add).then_inc(scan_step, 1)
                    dve.wait_ge(scan_step, done + 4)
            V.memset(msq[:, :], 0.0).then_inc(scan_done, 1)
            dve.wait_ge(loads["cw"], 16)
            V.tensor_scalar(cw[:, 1], cw[:, 1], -1.0, None, ALU.mult).then_inc(cneg_ready, 1)

            evacuated(dve, ("zu", 3))
            for u in range(4):
                take_unit(dve, ("sgu", u))
                zs = zuT[:, 2 * u:2 * u + 2, :]
                last = V.tensor_tensor(zs, zs, halves(bank(("sgu", u))), ALU.mult)
                free_unit(last, ("sgu", u))
            evacuated(dve, ("gb", 3))
            for i in range(4):
                take_unit(dve, ("pb", i))
                gs = gbT[:, 2 * i:2 * i + 2, :]
                last = V.tensor_tensor(gs, gs, halves(bank(("pb", i))), ALU.mult)
                free_unit(last, ("pb", i))
            dve.wait_ge(loads["s5d"], 16)
            for q in range(4):
                take_unit(dve, ("y", q))
                last = V.scalar_tensor_tensor(ygT[:, q, :], uT[:, q, :], s5d[:, q:q + 1],
                                              bank(("y", q))[:, 0:TOK], ALU.mult, ALU.add)
                free_unit(last, ("y", q))
            for i in range(2):
                evacuated(dve, ("glu", i))
                ys = yaT[:, 2 * i:2 * i + 2, :]
                V.tensor_tensor(ys, ys, ygT[:, 2 * i:2 * i + 2, :], ALU.mult).then_inc(ya_ready, 1)

            def merge(name, first):
                for i in range(4):
                    take_unit(dve, (name, i))
                    gs = gaT[:, 2 * i:2 * i + 2, :]
                    last = V.tensor_tensor(gs, gs, halves(bank((name, i))), ALU.mult)
                    free_unit(last, (name, i))
                    evacuated(dve, (name, i))
                    V.tensor_tensor(gs, gs, gbT[:, 2 * i:2 * i + 2, :], ALU.add).then_inc(m_ready, 1)

            merge("pa", True)
            for i in range(4):
                residual(("out", i), i)
            evacuated(dve, ("out", 3))
            stats(h, True, EPS)
            scaled(xn, h, xn_ready)
            attention("x", 4, None, None)
            for i in range(4):
                residual(("xo", i), i)
            evacuated(dve, ("xo", 3))
            stats(h, True, EPS)
            scaled(xn, h, xn_ready)
            ffn_mul("ffn", FF_STEPS)
            add_sums(1)
            dve.wait_ge(loads["bc0"], 16 * 7)
            stats(h, True, EPS)
            for b in range(TB):
                last = V.scalar_tensor_tensor(h[:, b, :], h[:, b, :], rstd[:, b:b + 1], bc[:, 0, :],
                                              ALU.mult, ALU.mult)
            link(last)
            layer_norm(h, bc[:, 1, :], bc[:, 2, :], LN_EPS).then_inc(xn_ready, 1)
            dve.wait_ge(xn_ready, 4)
            dve.wait_ge(loads["nab"], 32)
            dve.wait_ge(loads["consts"], 80)
            dve.wait_ge(loads["sink"], 16)
            for m in range(2):
                evacuated(dve, (f"projb{m}", 4))
                heads = qk_t[:, :, 0:640].rearrange("p b (h d) -> p b h d", d=64)
                tmp = rtmp[:, :, :, 0:80]
                for b in range(TB):
                    x1, x2 = heads[:, b, :, 0:8], heads[:, b, :, 8:16]
                    cos = rope[:, b, 0, :].unsqueeze(1).to_broadcast([P, 10, 8])
                    sin = rope[:, b, 1, :].unsqueeze(1).to_broadcast([P, 10, 8])
                    t = [rtmp[:, n, b, 0:80].rearrange("p (h f) -> p h f", f=8) for n in range(4)]
                    V.tensor_tensor(t[0], x1, cos, ALU.mult)
                    V.tensor_tensor(t[1], x2, sin, ALU.mult)
                    V.tensor_tensor(t[2], x2, cos, ALU.mult)
                    link(V.tensor_tensor(t[3], x1, sin, ALU.mult))
                    V.tensor_tensor(x1, t[0], t[1], ALU.subtract)
                    last = V.tensor_tensor(x2, t[2], t[3], ALU.add)
                last.then_inc(qk_roped, 1)
                attention(f"na{m}", 8, lambda i: nabias[m][:, i, :, :], None)
                attention(f"sw{m}", 8, lambda i: swmask, lambda i: sink_col(m, i))
                evacuated(dve, (f"gb{m}", 3))
                for i in range(4):
                    take_unit(dve, (f"bna{m}", i))
                    gs = gaT[:, 2 * i:2 * i + 2, :]
                    last = V.tensor_tensor(gs, gs, halves(bank((f"bna{m}", i))), ALU.mult)
                    free_unit(last, (f"bna{m}", i))
                for i in range(4):
                    take_unit(dve, (f"bsw{m}", i))
                    gs = gbT[:, 2 * i:2 * i + 2, :]
                    last = V.tensor_tensor(gs, gs, halves(bank((f"bsw{m}", i))), ALU.mult)
                    free_unit(last, (f"bsw{m}", i))
                    evacuated(dve, (f"bsw{m}", i))
                    ms = gaT[:, 2 * i:2 * i + 2, :]
                    V.tensor_tensor(ms, ms, gs, ALU.add).then_inc(m_ready, 1)
                for i in range(4):
                    residual((f"out{m}", i), i, ALPHA)
                evacuated(dve, (f"out{m}", 3))
                if m == 1:
                    dve.wait_ge(loads["bcn"], 16 * 4)
                layer_norm(h, bc[:, 3, :], bc[:, 4, :], LN_EPS).then_inc(xn_ready, 1)
                dve.wait_ge(xn_ready, 5 + 2 * m)
                if m == 0:
                    ffn_mul("dense", FF_STEPS)
                    add_sums(2, ALPHA)
                    layer_norm(h, bc[:, 5, :], bc[:, 6, :], LN_EPS).then_inc(xn_ready, 1)
                    dve.wait_ge(xn_ready, 6)

            lg, m1, c1_, f1, l2, m2, f2 = (rt[:, n, :, :] for n in range(7))
            v1, v2 = rt[:, 9, :, 0:1], rt[:, 9, :, 1:2]
            take_unit(dve, ("router", 0))
            last = V.tensor_copy(lg, bank(("router", 0))[:, 0:16].rearrange("p (b e) -> p b e", e=8))
            free_unit(last, ("router", 0))
            evacuated(dve, ("router", 0))

            def first_max(val, src, dst, tmp, top):
                link(V.reduce_max(top, src, AX_X))
                link(V.tensor_tensor(tmp, src, top.to_broadcast([P, TB, 8]), ALU.is_equal))
                for b in range(TB):
                    last = V.tensor_tensor_scan(c1_[:, b, :], ones[:, 0:8], tmp[:, b, :], 0.0, ALU.mult, ALU.add)
                link(last)
                link(V.tensor_scalar(c1_, c1_, 1.0, None, ALU.is_le))
                link(V.tensor_tensor(dst, tmp, c1_, ALU.mult))

            first_max(None, lg, f1, m1, v1)
            link(V.scalar_tensor_tensor(l2, f1, -3.0e38, lg, ALU.mult, ALU.add))
            first_max(None, l2, f2, m2, v2)
            V.tensor_tensor(rt[:, 7, :, 0:1], v2, v1, ALU.subtract).then_inc(rexp_in, 1)
            dve.wait_ge(rexp_out, 1)
            ex, den, w1, w2 = rt[:, 8, :, 0:1], rt[:, 10, :, 0:1], rt[:, 10, :, 1:2], rt[:, 10, :, 2:3]
            link(V.tensor_scalar(den, ex, 1.0, None, ALU.add))
            link(V.reciprocal(w1, den))
            link(V.tensor_tensor(w2, ex, w1, ALU.mult))
            V.tensor_tensor(mask, f1, f2, ALU.add).then_inc(mask_ready, 1)
            V.tensor_tensor(f1, f1, w1.to_broadcast([P, TB, 8]), ALU.mult)
            link(V.tensor_tensor(f2, f2, w2.to_broadcast([P, TB, 8]), ALU.mult))
            link(V.tensor_tensor(pass_w[:, :, 0:8], f1, f2, ALU.add))
            take_unit(dve, ("pos", 0))
            pos = bank(("pos", 0))
            V.scalar_tensor_tensor(l2, pos[:, 0:16].rearrange("p (b e) -> p b e", e=8), 1.0, mask, ALU.add, ALU.mult)
            last = V.tensor_copy(m2[:, 0, :], pos[:, 16:24])
            free_unit(last, ("pos", 0))
            evacuated(dve, ("pos", 0))
            V.tensor_scalar(pass_pos[:, :, 0:8], l2, -1.0, None, ALU.add)
            link(V.tensor_scalar(m2[:, 0, :], m2[:, 0, :], float(CAP), None, ALU.is_gt))
            link(V.tensor_tensor_scan(m2[:, 1, :], ones[:, 0:8], m2[:, 0, :], 0.0, ALU.mult, ALU.add))
            n_x = PASSES - MOE_E
            sel, prod = over[:, 0, :, :], over[:, 1, :, :]
            for j in range(n_x):
                last = V.scalar_tensor_tensor(sel[:, j, :], m2[:, 1, :], float(j + 1), m2[:, 0, :],
                                              ALU.is_equal, ALU.mult)
            link(last)
            link(V.tensor_scalar(c1_, l2, -float(CAP), None, ALU.add))
            red = over[:, 3, 0, 0:n_x]
            for b in range(TB):
                link(V.tensor_tensor(prod, sel, c1_[:, b, :].unsqueeze(1).to_broadcast([P, n_x, 8]), ALU.mult))
                link(V.tensor_reduce(red, prod, AX_X, ALU.add))
                link(V.tensor_scalar(pass_pos[:, b, MOE_E:], red, -1.0, None, ALU.add))
                link(V.tensor_tensor(prod, sel, pass_w[:, b, 0:8].unsqueeze(1).to_broadcast([P, n_x, 8]), ALU.mult))
                link(V.tensor_reduce(pass_w[:, b, MOE_E:], prod, AX_X, ALU.add))
            link(V.tensor_tensor(prod, sel, iota[:, 0:8].unsqueeze(1).to_broadcast([P, n_x, 8]), ALU.mult))
            link(V.tensor_reduce(red, prod, AX_X, ALU.add))
            V.tensor_copy(table[:, 2:2 + n_x], red)
            V.tensor_scalar(table[:, 0:1], m2[:, 1, 7:8], float(MOE_E), None, ALU.add)
            V.tensor_copy(table[:, 1:2], m2[:, 1, 7:8]).then_inc(table_ready, 1)

            def build_pick(n, col):
                for b in range(TB):
                    last = V.tensor_scalar(pick[:, b, :], iota, col(b), None, ALU.is_equal)
                last.then_inc(pick_ready, 1)

            def move_xe(n):
                dve.wait_ge(xe_high, n)
                V.tensor_tensor(xe_l[:, :, :].rearrange("p (b k) m -> p b (k m)", b=2), psum[:, 6:8, :],
                                xe_h[:, :, :].rearrange("p (b k) m -> p b (k m)", b=2).bitcast(F32),
                                ALU.subtract).then_inc(xe_split, 1)

            V.tensor_copy(h_h[:, :, :], h[:, :, :]).then_inc(h_high, 1)
            dve.wait_ge(h_high, 1)
            V.tensor_tensor(h_l[:, :, :], h[:, :, :], h_h[:, :, :].bitcast(F32), ALU.subtract).then_inc(h_split, 1)

            def low_part(p, n):
                dve.wait_ge(w_high, p * MOE_CHUNKS + (n + 1))
                V.tensor_tensor(w_l[:, n % SPLITS, :], ring[:, n % SLOTS, :], w_h[:, n % SPLITS, :].bitcast(F32),
                                ALU.subtract).then_inc(w_split, 1)

            build_pick(0, lambda b: pass_pos[:, b, 0:1])
            for b in range(TB):
                for c in range(2):
                    V.tensor_scalar(ysum[:, b, c * 512:(c + 1) * 512], h[:, b, c * 512:(c + 1) * 512], ALPHA, None,
                                    ALU.mult).then_inc(y_added, 1)
            for n in range(AHEAD):
                low_part(0, n)
            move_xe(1)
            f0 = ff0["moe"]
            chunks, after = moe_events()
            dve.wait_ge(table_ready, 1)
            n_pass = dve.value_load(table[0:1, 0:1], min_val=MOE_E, max_val=MOE_E + OVER)
            with dve.Fori(0, n_pass) as p:
                for n in range(-1, len(chunks)):
                    for what, s in after.get(n, []):
                        if what == "prod":
                            dve.wait_ge(silu_ready, p * MOE_PER + (f0 + s + 1))
                            V.tensor_tensor(e_h[:, s % 2, :], e_silu[:, s % 2, :], psum[:, s % 2, 256:512],
                                            ALU.mult).then_inc(hT_ready, 1)
                            if s == 2:
                                dve.wait_ge(gathered, p + 1)
                                dve.wait_ge(pickT_full, p + 1)
                                build_pick(p, lambda b: pass_pos[:, b, bass.ds(p + 1, 1)])
                        else:
                            dve.wait_ge(hT_high, p * MOE_PER + (s + 1))
                            V.tensor_tensor(eT_l[:, s % 2, :, :],
                                            halves(psum[:, 2, 256 * (s % 2):256 * (s % 2) + 256]),
                                            eT_h[:, s % 2, :, :].bitcast(F32), ALU.subtract).then_inc(hT_moved, 1)
                    if n == len(chunks) - 2:
                        move_xe(p + 2)
                    if n + SPLITS < len(chunks) + AHEAD:
                        low_part(p, n + SPLITS)
                dve.wait_ge(oe_high, p + 1)
                V.tensor_tensor(o_l[:, :, :], psum[:, 4:6, :], o_h[:, :, :].bitcast(F32),
                                ALU.subtract).then_inc(oe_split, 1)
                for b in range(TB):
                    for c in range(2):
                        dve.wait_ge(scattered, p * 4 + (2 * b + c + 1))
                        ys = ysum[:, b, c * 512:(c + 1) * 512]
                        V.scalar_tensor_tensor(ys, psum[:, 4 * b + c, :], pass_w[:, b, bass.ds(p, 1)], ys,
                                               ALU.mult, ALU.add).then_inc(y_added, 1)
            dve.wait_ge(loads["bcn"], 16 * 4)
            dve.wait_ge(y_added, n_pass * 4 + 4)
            layer_norm(ysum, bc[:, 5, :], bc[:, 6, :], LN_EPS).then_inc(out_ready, 1)


def weight_stream(w):
    out = np.empty((len(CHUNKS), P, CHUNK_F), np.float32)
    for n, (kind, name, i) in enumerate(CHUNKS):
        m = w[name]
        if m.ndim == 3:
            per = MOE_PER
            m, i = m[i // per], i % per
        if kind == "k2":
            out[n] = m[256 * i:256 * i + 256].reshape(2, P, D).transpose(1, 0, 2).reshape(P, CHUNK_F)
        else:
            k, cols = (KD, 256) if kind == "k8" else (4, 512)
            part = m[:, cols * i:cols * (i + 1)]
            out[n] = part.reshape(k, P, cols).transpose(1, 0, 2).reshape(P, CHUNK_F)
    return out


def pair_heads():
    return np.concatenate([np.arange(64) + 64 * hd for i in range(4) for hd in (i, i + 4)])


def na_bias_layout(rpb):
    q, k = np.arange(TOK)[:, None], np.arange(TOK)[None, :]
    qr, qc, kr, kc = q // 64, q % 64, k // 64, k % 64
    start = np.clip(qc - 8, 0, 48)
    valid = (kc >= start) & (kc < start + 16)
    dr, dc = kr - qr + 7, np.clip(kc - qc + 15, 0, 30)
    out = np.where(valid[None], rpb[:, dr, dc], np.float32(-1e30))
    return out.reshape(8, TB, P, TOK).transpose(2, 0, 1, 3)


def layout(i):
    f = {k: np.asarray(v) for k, v in i.items()}
    per = pair_heads()
    w = {"w_in": np.concatenate([f["w_in"][0][:, :512], f["w_in"][0][:, 1536:2560],
                                 f["w_in"][0][:, 512:1536], f["w_in"][0][:, 2560:]], 1)}
    for n in ("w_k", "w_v", "w_q", "w_xo", "w_out", "w_proj_a", "w_proj_b", "s5_w_glu"):
        w[n] = f[n][0]
    w["ffn_gate"], w["ffn_up"], w["ffn_down"] = f["w_gate"][0], f["w_up"][0], f["w_down"][0]
    w["dense_gate"], w["dense_up"], w["dense_down"] = (f[f"ffn_w_{n}_2"][0] for n in ("gate", "up", "down"))
    w["moe_gate"], w["moe_up"], w["moe_down"] = (f[f"moe_w_{n}_2"][0] for n in ("gate", "up", "down"))
    for m in range(2):
        x = f["w_in_2"][m]
        w[f"w_in_{m}"] = np.concatenate([x[:, 1024:1536], x[:, 1536:2048][:, per], x[:, 2048:2304],
                                         x[:, 0:1024], x[:, 2304:]], 1)
        w[f"w_na_{m}"] = f["w_branch_na_2"][m]
        w[f"w_sw_{m}"] = f["w_branch_sw_2"][m][per]
        w[f"w_out_{m}"] = f["w_out_2"][m]

    def col(v):
        return v.reshape(-1, P).T

    def states(v):
        v = v.reshape(2, PAIRS, 2, S5_P, *v.shape[3:])
        return np.moveaxis(v, (2, 3), (0, 1)).reshape(P, BLK, *v.shape[4:])

    step = np.broadcast_to(f["s5_log_step"][0][:, :, None], (2, S5_G, S5_P))
    s5_c = np.zeros((P, 2, BLK, 2, S5_C), np.float32)
    for r, n in enumerate(("s5_c_re", "s5_c_im")):
        c = states(f[n][0].transpose(0, 1, 3, 2))
        for g in range(2):
            s5_c[64 * g:64 * g + 64, r, :, g, :] = c[64 * g:64 * g + 64]
    pos = np.arange(TOK, dtype=np.float32)
    inv = (1.0 / (500000.0 ** (np.arange(0, 16, 2, dtype=np.float32) / 16))).astype(np.float32)
    ang = pos[:, None] * inv[None, :]
    rope = np.stack([np.cos(ang), np.sin(ang)], 1).astype(np.float32).reshape(TB, P, 2, 8).transpose(1, 0, 2, 3)
    q, k = np.arange(TOK)[:, None], np.arange(TOK)[None, :]
    band = np.where(np.abs(q - k) <= 128, 0.0, -1e30).astype(np.float32).reshape(TB, P, TOK).transpose(1, 0, 2)
    return {
        "x": f["x"], "mem": f["mem"], "stream": weight_stream(w),
        "ident": np.eye(P, dtype=np.float32),
        "gains": np.stack([col(f["mix_norm_g"][0]), col(f["mem_norm_g"]), col(f["xattn_norm_g"][0]),
                           col(f["ffn_norm_g"][0])], 1),
        "s5_prm": np.stack([states(f["s5_lam_re"][0]), states(f["s5_lam_im"][0]), states(step)], 1),
        "s5_b": np.stack([states(f["s5_b_re"][0]), states(f["s5_b_im"][0])], 1),
        "s5_c": s5_c.reshape(P, 2, BLK, 32),
        "s5_d": col(f["s5_d"][0]),
        "sgu_ln": np.concatenate([f["sgu_ln_g"], f["sgu_ln_b"]], 0),
        "sgu_w": f["sgu_w"][0].transpose(2, 0, 1),
        "sgu_bias": f["sgu_bias"][0].reshape(1, -1),
        "b_gate": np.stack([col(f["b_gate_2"][m]) for m in range(2)], 1),
        "sink": f["sw_sink_2"],
        "na_bias": np.stack([na_bias_layout(f["na_rpb_2"][m]) for m in range(2)]),
        "sw_mask": band, "rope": rope,
        "before": np.triu(np.ones((P, P), np.float32), 1),
        "iota": np.broadcast_to(np.arange(P, dtype=np.float32), (P, P)),
        "router": f["moe_router_2"][0].reshape(KD, P, 8).transpose(1, 0, 2),
        "bc": np.stack([f["final_norm_g"], f["emb_ln_g_2"], f["emb_ln_b_2"]]
                       + [f[n][m] for m in range(2) for n in ("ln1_g_2", "ln1_b_2", "ln2_g_2", "ln2_b_2")]),
    }


def kernel(**inputs):
    import concourse.bacc as _bacc
    from concourse.bass_utils import run_bass_kernel_spmd as _run

    nc = _bacc.Bacc("TRN2", target_bir_lowering=False, num_devices=1)
    arrays, aps = {}, {}
    for name, v in layout(inputs).items():
        arrays["in_" + name] = np.ascontiguousarray(v)
        aps[name] = nc.dram_tensor("in_" + name, v.shape, mybir.dt.from_np(v.dtype), kind="ExternalInput").ap()
    out = nc.dram_tensor("out_dram", (1, TOK, D), F32, kind="ExternalOutput").ap()
    build(nc, aps, out)
    r = _run(nc, [arrays], core_ids=[0])
    return r.results[0]["out_dram"]
```

```python
from contextlib import ExitStack

import numpy as np

import concourse.bass as bass
from concourse import mybir

P = 128
TOK = 256
TB = TOK // P
D = 1024
KD = D // P
SLOTS = 7
CHUNK_F = 2048
BANKS = 8
BF = 512

ALU = mybir.AluOpType
ACT = mybir.ActivationFunctionType
F32 = mybir.dt.float32
F32R = mybir.dt.float32r
I32 = mybir.dt.int32
AX_X = mybir.AxisListType.X

S5_G, S5_P, S5_C = 32, 64, 16
PAIRS = S5_G // 2
BLK = 2 * PAIRS
SPAN = 2
SCAN = TOK // SPAN
FF_STEPS = 2816 // 256
FF_CHUNKS = 3 * FF_STEPS
MOE_E = 8
MOE_PER = 3584 // 256
MOE_CHUNKS = 3 * MOE_PER
CAP = P
OVER = (2 * TOK) // (CAP + 1)
PASSES = MOE_E + OVER + 1
SPLITS = 3
AHEAD = 2
ALPHA = 4.0 ** 0.25
EPS = 1e-6
LN_EPS = 1e-5
XSCALE = 256.0 ** -0.5
HSCALE = 64.0 ** -0.5
NORMS = ("x", "mem", "zv", "xattn", "ffn", "final", "emb", "ln1_0", "ln2_0", "ln1_1", "ln2_1")


def ffn_order(steps):
    out = [("gate", 0), ("up", 0)]
    for s in range(1, steps):
        out += [("gate", s), ("up", s), ("down", s - 1)]
    return out + [("down", steps - 1)]


FF_ORDER = ffn_order(FF_STEPS)


def ffn_chunks(name):
    return [("k2" if part == "down" else "k8", f"{name}_{part}", s) for part, s in FF_ORDER]


def moe_chunks(e):
    out = []
    for s in range(MOE_PER + 2):
        if s < MOE_PER:
            out += [("k8", "moe_gate", e * MOE_PER + s), ("k8", "moe_up", e * MOE_PER + s)]
        if s >= 2:
            out.append(("k2", "moe_down", e * MOE_PER + s - 2))
    return out


def moe_events():
    chunks, after = [], {}
    for s in range(MOE_PER + 2):
        if s < MOE_PER:
            chunks += [("gate", s), ("up", s)]
            after[len(chunks) - 1] = [("prod", s)]
        if s >= 2:
            chunks.append(("down", s - 2))
        if 1 <= s <= MOE_PER:
            after.setdefault(len(chunks) - 1, []).append(("move", s - 1))
    return chunks, after


def plan_chunks():
    c = [("k8", "w_in", i) for i in range(18)]
    c += [("k8", "w_k", i) for i in range(4)] + [("k8", "w_v", i) for i in range(4)]
    c += [("k8", "w_proj_b", i) for i in range(4)]
    c += [("k4", "s5_w_glu", 0)] + [("k4", "w_proj_a", i) for i in range(2)]
    c += [("k8", w, i) for w in ("w_out", "w_q", "w_xo") for i in range(4)]
    c += ffn_chunks("ffn")
    for layer in range(2):
        c += [("k8", f"w_in_{layer}", i) for i in range(17)]
        c += [("k4", f"w_na_{layer}", i) for i in range(2)] + [("k4", f"w_sw_{layer}", i) for i in range(2)]
        c += [("k8", f"w_out_{layer}", i) for i in range(4)]
        if layer == 0:
            c += ffn_chunks("dense")
    for e in range(MOE_E):
        c += moe_chunks(e)
    return c


def split_plan():
    out = [((("k8", "w_" + n, i)), (n, i)) for n in ("out", "q", "xo") for i in range(4)]
    for m in range(2):
        units = [(f"projb{m}", i) for i in range(5)] + [(f"{n}{m}", i) for n in ("qk", "ga", "gb") for i in range(4)]
        out += [(("k8", f"w_in_{m}", i), unit) for i, unit in enumerate(units)]
        out += [(("k8", f"w_out_{m}", i), (f"out{m}", i)) for i in range(4)]
    return out


def bu_block(u):
    return 8 * (u // 4) + u % 4


def plan_units():
    u = []

    def add(name, n):
        u.extend((name, i) for i in range(n))

    add("t_x", 4)
    add("t_mem", 4)
    add("xa", 2)
    add("zv", 4)
    add("t_b", 8)
    add("bu", BLK // 2)
    add("kmat", 1)
    add("zu", 4)
    add("ga", 4)
    add("gb", 4)
    add("k", 4)
    add("v", 4)
    add("sgu", 4)
    add("pb", 4)
    add("y", 4)
    add("glu", 2)
    add("pa", 4)
    add("out", 4)
    add("t_xattn", 4)
    add("q", 4)
    attention_units(u, "x", 4)
    add("xo", 4)
    add("t_ffn", 4)
    for m in range(2):
        add(f"t_in{m}", 4)
        add(f"projb{m}", 5)
        add(f"qk{m}", 4)
        add(f"ga{m}", 4)
        add(f"t_sw{m}", 3)
        attention_units(u, f"at{m}", 16, f"gb{m}")
        add(f"bna{m}", 4)
        add(f"bsw{m}", 4)
        add(f"out{m}", 4)
        add(f"t_mid{m}", 4)
    add("router", 1)
    add("pos", 1)
    return u


def attention_units(u, name, heads, gate=None):
    for i in range(-1, heads + 2):
        if i + 1 < heads:
            u.append((name + "_s", i + 1))
        if 0 <= i - 1 < heads:
            u.append((name + "_t", i - 1))
        if 0 <= i - 2 < heads:
            u.append((name + "_o", i - 2))
        if gate is not None and 0 <= i < 16 and i % 4 == 1:
            u.append((gate, i // 4))


CHUNKS = plan_chunks()
CHUNK_AT = {c: n for n, c in enumerate(CHUNKS)}
UNITS = plan_units()
SPLIT = split_plan()
SPLIT_AT = {c: n for n, (c, _) in enumerate(SPLIT)}
XF_USES = ["out", "t_xattn", "x_o", "t_ffn", "t_in0", "out0", "t_mid0", "t_in1", "out1"]
UNIT_AT = {u: n for n, u in enumerate(UNITS)}
MOE_C0 = CHUNK_AT[("k8", "moe_gate", 0)]
assert len(CHUNKS) % SLOTS == 0 and MOE_C0 % SLOTS == 0 and MOE_CHUNKS % SLOTS == 0
assert len(CHUNK_AT) == len(CHUNKS) and len(UNIT_AT) == len(UNITS)


def build(nc, a, out):
    with ExitStack() as ctx:
        def sb(name, shape, dt=F32):
            return ctx.enter_context(nc.sbuf_tensor(name, shape, dt))

        def sem(name):
            return ctx.enter_context(nc.semaphore(name))

        ring = sb("ring", [P, SLOTS, CHUNK_F])
        h = sb("h", [P, TB, D])
        ident = sb("ident", [P, P])
        gains = sb("gains", [P, 4, KD])
        s5d = sb("s5d", [P, 4])
        bgate = sb("bgate", [P, 2, 16])
        sink = sb("sink", [P, 2, 8])
        st = sb("st", [P, TB, 2, 6])
        mv = sb("mv", [P, TB, 2])
        ve = sb("ve", [P, TB])
        sd = sb("sd", [P, TB])
        rstd = sb("rstd", [P, TB])
        msq = sb("msq", [P, TB])
        lam_a = sb("lam_a", [P, 2, 2, BLK])
        scan_t = sb("scan_t", [P, 3, 2, BLK])
        kmat = sb("kmat", [P, 2, 4, 32])
        mx = sb("mx", [P, 2, TB])
        negm = sb("negm", [P, 2, TB])
        ssum = sb("ssum", [P, 2, TB])
        rsum = sb("rsum", [P, 2, TB])
        esink = sb("esink", [P, 2, TB])
        rt = sb("rt", [P, 12, TB, 8])
        mask = rt[:, 11, :, :]
        ones = sb("ones", [P, P])
        pass_pos = sb("pass_pos", [P, TB, PASSES])
        pass_w = sb("pass_w", [P, TB, PASSES])
        over = sb("over", [P, 4, PASSES - MOE_E, 8])
        table = sb("table", [P, 8], I32)
        silu = sb("silu", [P, 512])
        psum = ctx.enter_context(nc.psum_tensor("psum", [P, BANKS, BF], F32))
        with ExitStack() as early:
            def region(name, shape, dt=F32):
                return early.enter_context(nc.sbuf_tensor(name, shape, dt))

            sguT = region("sguT", [P, 8, P])
            big = region("big", [P, 16384])
            xT = region("xT", [P, KD, TOK])
            memT = region("memT", [P, KD, TOK])
            r_zu = region("r_zu", [P, 2048])
            r_zv = region("r_zv", [P, 2048])
            r_ga = region("r_ga", [P, 2048])
            r_k = region("r_k", [P, 2048])
            r_v = region("r_v", [P, 2048])
            r_gb = region("r_gb", [P, 2048])
            uT = region("uT", [P, 4, TOK])
        with ExitStack() as dense:
            def operand(name, shape):
                return dense.enter_context(nc.sbuf_tensor(name, shape, F32R))

            wp_h = operand("wp_h", [P, 2, CHUNK_F])
            wp_l = operand("wp_l", [P, 2, CHUNK_F])
            hf_l = operand("hf_l", [P, 2, 2, TOK])
            dense.enter_context(nc.sbuf_tensor("constants_stay_1", [P, 8192], F32))
            xf_h = operand("xf_h", [P, KD, TOK])
            xf_l = operand("xf_l", [P, KD, TOK])
            wf_h = operand("wf_h", [P, SPLITS, CHUNK_F])
            wf_l = operand("wf_l", [P, SPLITS, CHUNK_F])
            hf_h = operand("hf_h", [P, 2, 2, TOK])
        w_l = sb("w_l", [P, SPLITS, CHUNK_F], F32R)
        h_l = sb("h_l", [P, TB, D], F32R)
        sb("constants_stay_2", [P, 9216])
        ysum = sb("ysum", [P, TB, D])
        w_h = sb("w_h", [P, SPLITS, CHUNK_F], F32R)
        h_h = sb("h_h", [P, TB, D], F32R)
        xe_h = sb("xe_h", [P, KD, P], F32R)
        xe_l = sb("xe_l", [P, KD, P], F32R)
        o_h = sb("o_h", [P, 2, BF], F32R)
        o_l = sb("o_l", [P, 2, BF], F32R)
        pick = sb("pick", [P, TB, P], F32R)
        pickT = sb("pickT", [P, TB, P], F32R)
        e_silu = sb("e_silu", [P, 2, 256])
        e_h = sb("e_h", [P, 2, 256])
        eT_h = sb("eT_h", [P, 2, 2, P], F32R)
        eT_l = sb("eT_l", [P, 2, 2, P], F32R)

        def view(region, lo, size, pat, **kw):
            return region[:, lo:lo + size].rearrange(pat, **kw)

        x_mem = view(big, 0, 2048, "p (b d) -> p b d", b=TB)
        n_mem = view(big, 2048, 2048, "p (b d) -> p b d", b=TB)
        states = view(big, 0, SCAN * 2 * BLK, "p (t r k) -> p t r k", r=2, k=BLK)
        xn = view(r_gb, 0, 2048, "p (b d) -> p b d", b=TB)
        ln_v = view(r_k, 0, 2048, "p (a d) -> p a d", a=2)
        b_raw = view(r_zu, 0, 1024, "p (r k c) -> p r k c", r=2, k=BLK)
        pt = view(r_zu, 1024, 1024, "p (n k) -> p n k", k=BLK)
        b_tmp = view(r_v, 0, 1024, "p (r k c) -> p r k c", r=2, k=BLK)
        b_wide_f = [r_ga[:, :], big[:, 8192:10240]]
        b_wide = [w.rearrange("p (r k g c) -> p r k g c", r=2, k=BLK, g=2) for w in b_wide_f]
        bT = [w.rearrange("p (n m) -> p n m", m=P) for w in (r_v[:, :], big[:, 10240:12288])]
        cw = view(big, 12288, 2048, "p (r k m) -> p r k m", r=2, k=BLK)
        cw_lam = view(big, 14336, 2048, "p (r k m) -> p r k m", r=2, k=BLK)
        c_tmp = view(r_zu, 0, 1024, "p (k m) -> p k m", k=BLK)
        zuT = view(r_zu, 0, 2048, "p (k t) -> p k t", t=TOK)
        zv = view(r_zv, 0, 2048, "p (b d) -> p b d", b=TB)
        gaT = view(r_ga, 0, 2048, "p (k t) -> p k t", t=TOK)
        gbT = view(r_gb, 0, 2048, "p (k t) -> p k t", t=TOK)
        kT = view(r_k, 0, 2048, "p (k t) -> p k t", t=TOK)
        v_t = view(r_v, 0, 2048, "p (b d) -> p b d", b=TB)
        ygT = memT[:, 0:4, :]
        yaT = memT[:, 4:8, :]
        sbias = yaT.rearrange("p a t -> p (a t)")
        prob = view(r_zv, 0, 1024, "p (n b m) -> p n b m", n=2, b=TB)
        probT = view(r_zv, 1024, 1024, "p (n b l) -> p n b l", n=2, b=TB)
        logit = uT[:, :, :].rearrange("p a t -> p (a t)").rearrange("p (n b m) -> p n b m", n=2, b=TB)
        qT = zuT
        nabias = view(big, 7168, 4096, "p (h b m) -> p h b m", h=8, b=TB)
        bc = view(big, 11264, 4096, "p (n d) -> p n d", d=D)
        swmask = big[:, 15360:15872].rearrange("p (b m) -> p b m", b=TB)
        rope = big[:, 15872:15904].rearrange("p (b c f) -> p b c f", b=TB, c=2)
        wr = big[:, 15904:15968].rearrange("p (k e) -> p k e", e=8)
        before = big[:, 15968:16096]
        iota = big[:, 16096:16224]
        qk_t = view(r_gb, 0, 1536, "p (b d) -> p b d", b=TB)
        rtmp = view(r_zv, 0, 2048, "p (n b m) -> p n b m", n=8, b=TB)
        qnT = view(r_zu, 0, 1024, "p (k t) -> p k t", t=TOK)
        knT = view(r_zu, 1024, 1024, "p (k t) -> p k t", t=TOK)
        v_na = view(r_v, 0, 1024, "p (b d) -> p b d", b=TB)
        onT = view(r_v, 1024, 1024, "p (k t) -> p k t", t=TOK)
        qsT = view(r_k, 0, 1024, "p (k t) -> p k t", t=TOK)
        ksT = r_k[:, 1024:1280]
        v_sw = view(r_k, 1280, 256, "p (b d) -> p b d", b=TB)
        osT = view(r_zu, 0, 1024, "p (k t) -> p k t", t=TOK)

        slot_full = [sem(f"slot_full{i}") for i in range(SLOTS)]
        chunk_used = sem("chunk_used")
        bank_full = [sem(f"bank_full{i}") for i in range(BANKS)]
        bank_free = [sem(f"bank_free{i}") for i in range(BANKS)]
        loads = {n: sem("ld_" + n) for n in (
            "x", "mem", "ident", "gains", "prm", "b", "lnv", "sgu", "sbias", "s5d", "cw", "bgate", "sink",
            "nab", "bc0", "ln1", "ln2", "consts")}
        dve_step = sem("dve_step")
        scan_step = sem("scan_step")
        var_ready = sem("var_ready")
        std_ready = sem("std_ready")
        xn_ready = sem("xn_ready")
        memn_ready = sem("memn_ready")
        bwide_ready = sem("bwide_ready")
        angle_ready = sem("angle_ready")
        sin_ready = sem("sin_ready")
        zvn_ready = sem("zvn_ready")
        scan_done = sem("scan_done")
        cneg_ready = sem("cneg_ready")
        yg_ready = sem("yg_ready")
        ya_ready = sem("ya_ready")
        m_ready = sem("m_ready")
        negm_ready = sem("negm_ready")
        exp_ready = sem("exp_ready")
        prob_ready = sem("prob_ready")
        g_full = sem("gate_full")
        u_full = sem("up_full")
        silu_ready = sem("silu_ready")
        hT_ready = sem("hT_ready")
        down_done = sem("down_done")
        xf_high = sem("xf_high")
        wf_high = sem("wf_high")
        wf_split = sem("wf_split")
        product_ready = sem("product_ready")
        wp_high = sem("wp_high")
        wp_split = sem("wp_split")
        m_split = sem("m_split")
        hf_high = sem("hf_high")
        acc_free = sem("acc_free")
        qk_roped = sem("qk_roped")
        rexp_in = sem("rexp_in")
        rexp_out = sem("rexp_out")
        mask_ready = sem("mask_ready")
        table_ready = sem("table_ready")
        pick_ready = sem("pick_ready")
        gathered = sem("gathered")
        w_high = sem("w_high")
        w_split = sem("w_split")
        w_used = sem("w_used")
        h_high = sem("h_high")
        h_split = sem("h_split")
        xe_high = sem("xe_high")
        xe_split = sem("xe_split")
        hT_high = sem("hT_high")
        hT_full = sem("hT_full")
        hT_moved = sem("hT_moved")
        oe_full = sem("oe_full")
        oe_high = sem("oe_high")
        oe_split = sem("oe_split")
        pickT_full = sem("pickT_full")
        pickT_ready = sem("pickT_ready")
        scattered = sem("scattered")
        y_added = sem("y_added")
        ones_ready = sem("ones_ready")
        out_ready = sem("out_ready")
        stored = sem("stored")

        def bank(u):
            return psum[:, UNIT_AT[u] % BANKS, :]

        def open_unit(pe, u):
            n = UNIT_AT[u]
            if n >= BANKS:
                pe.wait_ge(bank_free[n % BANKS], n // BANKS)

        def close_unit(last, u):
            last.then_inc(bank_full[UNIT_AT[u] % BANKS], 1)

        def take_unit(eng, u):
            n = UNIT_AT[u]
            eng.wait_ge(bank_full[n % BANKS], n // BANKS + 1)

        def free_unit(last, u):
            last.then_inc(bank_free[UNIT_AT[u] % BANKS], 1)

        def evacuated(eng, u):
            n = UNIT_AT[u]
            eng.wait_ge(bank_free[n % BANKS], n // BANKS + 1)

        def halves(ap):
            return ap.rearrange("p (b c) -> p b c", b=2)

        passes = [("x", 4), ("at0", 16), ("at1", 16)]
        head0 = {}
        n = 0
        for name, heads in passes:
            head0[name] = n
            n += heads
        ff0 = {"ffn": 0, "dense": FF_STEPS, "moe": 2 * FF_STEPS}
        wf0 = {"ffn": 0, "dense": FF_CHUNKS}

        def sink_col(m, i):
            head = i // 2 + 4 * (i % 2)
            return sink[:, m, head:head + 1]

        block = ctx.enter_context(nc.Block())

        @block.sync
        def _(sp):
            sp.dma_start(h[:, :, :], a["x"].rearrange("a (b p) d -> p (a b) d", p=P)).then_inc(loads["x"], 16)
            for j in range(SLOTS):
                sp.dma_start(ring[:, j, :], a["stream"][j, :, :]).then_inc(slot_full[j], 16)
            with sp.Fori(1, MOE_C0 // SLOTS + 1) as r:
                for j in range(SLOTS):
                    sp.wait_ge(chunk_used, r * SLOTS - SLOTS + j + 1)
                    sp.dma_start(ring[:, j, :], a["stream"][bass.ds(r * SLOTS + j, 1), :, :]
                                 .rearrange("a p f -> (a p) f")).then_inc(slot_full[j], 16)
            with sp.Fori(MOE_C0 // SLOTS + 1, len(CHUNKS) // SLOTS) as r:
                for j in range(SLOTS):
                    sp.wait_ge(w_split, r * SLOTS + (j + 1 - SLOTS - MOE_C0))
                    sp.dma_start(ring[:, j, :], a["stream"][bass.ds(r * SLOTS + j, 1), :, :]
                                 .rearrange("a p f -> (a p) f")).then_inc(slot_full[j], 16)
            sp.wait_ge(table_ready, 1)
            n_over = sp.value_load(table[0:1, 1:2], min_val=0, max_val=OVER)
            with sp.If(n_over > 0):
                with sp.Fori(0, n_over) as p:
                    e = sp.value_load(table[0:1, bass.ds(p + 2, 1)], min_val=0, max_val=MOE_E - 1)
                    with sp.Fori(0, MOE_CHUNKS // SLOTS) as r:
                        for j in range(SLOTS):
                            sp.wait_ge(w_split, p * MOE_CHUNKS + r * SLOTS + (len(CHUNKS) - MOE_C0 - SLOTS + j + 1))
                            sp.dma_start(ring[:, j, :], a["stream"][bass.ds(e * MOE_CHUNKS + r * SLOTS + (MOE_C0 + j), 1), :, :]
                                         .rearrange("a p f -> (a p) f")).then_inc(slot_full[j], 16)
            for j in range(AHEAD):
                sp.wait_ge(w_split, n_over * MOE_CHUNKS + (len(CHUNKS) - MOE_C0 - SLOTS + j + 1))
                sp.dma_start(ring[:, j, :], a["stream"][MOE_C0 + j, :, :]).then_inc(slot_full[j], 16)

        @block.gpsimd
        def _(pool):
            for q in range(4):
                take_unit(pool, ("y", q))
            for slot, n in ((0, 0), (2, 1), (3, 2)):
                pool.dma_start(bc[:, slot, :], a["bc"][n:n + 1, :].to_broadcast([P, D])).then_inc(loads["bc0"], 16)
            pool.dma_start(swmask, a["sw_mask"]).then_inc(loads["consts"], 16)
            pool.dma_start(rope, a["rope"]).then_inc(loads["consts"], 16)
            pool.dma_start(wr, a["router"]).then_inc(loads["consts"], 16)
            pool.dma_start(before, a["before"]).then_inc(loads["consts"], 16)
            pool.dma_start(iota, a["iota"]).then_inc(loads["consts"], 16)

            def norm_load(m, which, used):
                pool.wait_ge(xn_ready, used)
                for n in range(2):
                    at = 3 + 4 * m + 2 * which + n
                    pool.dma_start(bc[:, 2 * which + n, :], a["bc"][at:at + 1, :].to_broadcast([P, D])
                                   ).then_inc(loads[("ln1", "ln2")[which]], 16)

            pool.wait_ge(down_done, FF_STEPS)
            pool.dma_start(nabias, a["na_bias"][0]).then_inc(loads["nab"], 16)
            norm_load(0, 0, 4)
            norm_load(0, 1, 4)
            norm_load(1, 0, 5)
            pool.wait_ge(down_done, 2 * FF_STEPS)
            pool.dma_start(nabias, a["na_bias"][1]).then_inc(loads["nab"], 16)
            norm_load(1, 1, 6)

        @block.tensor
        def _(pe):
            def weights(c):
                n = CHUNK_AT[c]
                pe.wait_ge(slot_full[n % SLOTS], 16 * (n // SLOTS + 1))
                k = {"k8": KD, "k4": 4, "k2": 2}[c[0]]
                return ring[:, n % SLOTS, :].rearrange("p (k c) -> p k c", k=k)

            def release(first, chunk):
                if CHUNK_AT[chunk] > 0:
                    first.then_inc(chunk_used, 1)

            def transposes(u0, src, n_units=4):
                for u in range(n_units):
                    open_unit(pe, (u0, u))
                    for j in range(2):
                        for b in range(TB):
                            last = nc.tensor.transpose(
                                bank((u0, u))[:, (2 * j + b) * P:(2 * j + b + 1) * P],
                                src[:, b, (2 * u + j) * P:(2 * u + j + 1) * P], ident[:, :])
                    close_unit(last, (u0, u))

            def form_a(unit, chunk, act_T):
                open_unit(pe, unit)
                w = weights(chunk)
                for j in range(2):
                    for k in range(KD):
                        last = nc.tensor.matmul(bank(unit)[:, j * TOK:(j + 1) * TOK], w[:, k, j * P:(j + 1) * P],
                                                act_T[:, k, :], start=(k == 0), stop=(k == KD - 1))
                        if j == k == 0:
                            release(last, chunk)
                close_unit(last, unit)

            def form_a4(name, chunk, act_T, u0):
                w = weights(chunk)
                for u in range(2):
                    open_unit(pe, (name, u0 + u))
                    for j in range(2):
                        for k in range(4):
                            last = nc.tensor.matmul(
                                bank((name, u0 + u))[:, j * TOK:(j + 1) * TOK],
                                w[:, k, (2 * u + j) * P:(2 * u + j + 1) * P],
                                act_T[:, k, :], start=(k == 0), stop=(k == 3))
                            if u == j == k == 0:
                                release(last, chunk)
                    close_unit(last, (name, u0 + u))

            def form_b(unit, chunk, act_T):
                open_unit(pe, unit)
                w = weights(chunk)
                for b in range(TB):
                    for k in range(KD):
                        last = nc.tensor.matmul(bank(unit)[:, b * 256:(b + 1) * 256],
                                                act_T[:, k, b * P:(b + 1) * P], w[:, k, :],
                                                start=(k == 0), stop=(k == KD - 1))
                        if b == k == 0:
                            release(last, chunk)
                close_unit(last, unit)

            def split_chunk(chunk):
                n = SPLIT_AT[chunk]
                pe.wait_ge(wp_split, n + 1)
                return [w[:, n % 2, :].rearrange("p (k c) -> p k c", k=KD) for w in (wp_h, wp_l)]

            def split_a(unit, chunk, tiles=(0, 1)):
                if 0 in tiles:
                    open_unit(pe, unit)
                wh, wl = split_chunk(chunk)
                for j in tiles:
                    for k in range(KD):
                        for i, (w, x) in enumerate(((wh, xf_h), (wh, xf_l), (wl, xf_h))):
                            last = nc.tensor.matmul(bank(unit)[:, j * TOK:(j + 1) * TOK], w[:, k, j * P:(j + 1) * P],
                                                    x[:, k, :], start=(k == i == 0), stop=(k == KD - 1 and i == 2))
                            if i == j == k == 0:
                                release(last, chunk)
                if 1 in tiles:
                    close_unit(last, unit)

            def split_b(unit, chunk):
                open_unit(pe, unit)
                wh, wl = split_chunk(chunk)
                for b in range(TB):
                    for k in range(KD):
                        for i, (x, w) in enumerate(((xf_h, wh), (xf_h, wl), (xf_l, wh))):
                            last = nc.tensor.matmul(bank(unit)[:, b * 256:(b + 1) * 256],
                                                    x[:, k, b * P:(b + 1) * P], w[:, k, :],
                                                    start=(k == i == 0), stop=(k == KD - 1 and i == 2))
                            if i == b == k == 0:
                                release(last, chunk)
                close_unit(last, unit)

            def attention(name, heads, kd, q_of, k_of, v_of, o_rows, dblocks, between=None):
                g0 = head0[name]
                for i in range(-1, heads + 2):
                    if i + 1 < heads:
                        u = (name + "_s", i + 1)
                        open_unit(pe, u)
                        for b in range(TB):
                            for k in range(kd):
                                last = nc.tensor.matmul(bank(u)[:, b * 256:(b + 1) * 256],
                                                        q_of(i + 1, k)[:, b * P:(b + 1) * P], k_of(i + 1, k),
                                                        start=(k == 0), stop=(k == kd - 1))
                        close_unit(last, u)
                    if 0 <= i - 1 < heads:
                        u = (name + "_t", i - 1)
                        g = g0 + i - 1
                        pe.wait_ge(prob_ready, g + 1)
                        open_unit(pe, u)
                        for m in range(TB):
                            for b in range(TB):
                                last = nc.tensor.transpose(
                                    bank(u)[:, (2 * m + b) * P:(2 * m + b + 1) * P],
                                    prob[:, g % 2, b, m * P:(m + 1) * P], ident[:, :])
                        close_unit(last, u)
                    if 0 <= i - 2 < heads:
                        u = (name + "_o", i - 2)
                        g = g0 + i - 2
                        evacuated(pe, (name + "_t", i - 2))
                        open_unit(pe, u)
                        r0, rn = o_rows(i - 2)
                        for j in range(dblocks):
                            for m in range(TB):
                                last = nc.tensor.matmul(bank(u)[r0:r0 + rn, j * TOK:(j + 1) * TOK],
                                                        v_of(i - 2, j, m), probT[:, g % 2, m, :],
                                                        start=(m == 0), stop=(m == TB - 1))
                        close_unit(last, u)
                    if between is not None:
                        between(i)

            def split_weights(name, n, k):
                pe.wait_ge(wf_split, wf0[name] + n + 1)
                return [w[:, n % SPLITS, :].rearrange("p (k c) -> p k c", k=k) for w in (wf_h, wf_l)]

            def half_step(name, n, b, full):
                wh, wl = split_weights(name, n, KD)
                for j in range(2):
                    for k in range(KD):
                        for i, (w, x) in enumerate(((wh, xf_h), (wh, xf_l), (wl, xf_h))):
                            last = nc.tensor.matmul(psum[:, b, j * TOK:(j + 1) * TOK], w[:, k, j * P:(j + 1) * P],
                                                    x[:, k, :], start=(k == i == 0), stop=(k == KD - 1 and i == 2))
                            if i == j == k == 0:
                                last.then_inc(chunk_used, 1)
                last.then_inc(full, 1)

            def down(name, n, s, first, final):
                wh, wl = split_weights(name, n, 2)
                for k in range(2):
                    for b in range(TB):
                        for i, (x, w) in enumerate(((hf_h, wh), (hf_h, wl), (hf_l, wh))):
                            for c in range(2):
                                last = nc.tensor.matmul(psum[:, 4 + 2 * b + c, :], x[:, s % 2, k, b * P:(b + 1) * P],
                                                        w[:, k, c * 512:(c + 1) * 512],
                                                        start=(first and k == i == 0),
                                                        stop=(final and k == 1 and i == 2), skip_group_check=True)
                                if i == k == b == c == 0:
                                    last.then_inc(chunk_used, 1)
                last.then_inc(down_done, 1)

            def all_banks_free(next_unit):
                n = next_unit
                for b in range(BANKS):
                    used = (n - b + BANKS - 1) // BANKS
                    if used > 0:
                        pe.wait_ge(bank_free[b], used)

            def ffn(name, next_unit):
                f0 = ff0[name]
                all_banks_free(next_unit)
                for n, (part, s) in enumerate(FF_ORDER):
                    if part == "gate" and s >= 2:
                        pe.wait_ge(hT_ready, f0 + s - 1)
                    if part == "down":
                        pe.wait_ge(hT_ready, f0 + s + 1)
                        down(name, n, s, s == 0, s == FF_STEPS - 1)
                    else:
                        half_step(name, n, 2 * (s % 2) + (part == "up"), g_full if part == "gate" else u_full)

            pe.wait_ge(loads["ident"], 16)
            pe.wait_ge(xn_ready, 1)
            transposes("t_x", xn)
            pe.wait_ge(memn_ready, 1)
            transposes("t_mem", n_mem)
            evacuated(pe, ("t_x", 3))
            for i in range(2):
                form_a(("xa", i), ("k8", "w_in", i), xT)
            for i in range(4):
                form_b(("zv", i), ("k8", "w_in", 2 + i), xT)
            pe.wait_ge(bwide_ready, 1)
            for u in range(8):
                open_unit(pe, ("t_b", u))
                for j in range(4):
                    n = 4 * (u % 4) + j
                    last = nc.tensor.transpose(bank(("t_b", u))[:, j * P:(j + 1) * P],
                                               b_wide_f[u // 4][:, n * P:(n + 1) * P], ident[:, :])
                close_unit(last, ("t_b", u))
            evacuated(pe, ("t_b", 7))
            evacuated(pe, ("xa", 1))
            for u in range(BLK // 2):
                open_unit(pe, ("bu", u))
                for j in range(2):
                    blk = bu_block(u) + 4 * j
                    pair = blk % PAIRS
                    r0 = 32 * (pair % 4)
                    ch = uT[r0:r0 + 32, pair // 4, :]
                    earlier, later = (ch[:, 0::2], ch[:, 1::2]) if blk < PAIRS else (ch[:, ::-2], ch[:, 254::-2])
                    for r in range(2):
                        o = bank(("bu", u))[:, (2 * j + r) * SCAN:(2 * j + r + 1) * SCAN]
                        nc.tensor.matmul(o, bT[1][r0:r0 + 32, r * 8 + blk // 4, :], earlier, start=True, stop=False)
                        last = nc.tensor.matmul(o, bT[0][r0:r0 + 32, r * 8 + blk // 4, :], later,
                                                start=False, stop=True)
                close_unit(last, ("bu", u))
            pe.wait_ge(cneg_ready, 1)
            open_unit(pe, ("kmat", 0))
            for d in range(2):
                for pair in range(PAIRS):
                    i, q = pair % 4, pair // 4
                    for r in range(2):
                        last = nc.tensor.matmul(bank(("kmat", 0))[32 * i:32 * i + 32, (4 * d + q) * 32:(4 * d + q + 1) * 32],
                                                b_wide[0][:, r, d * PAIRS + pair, :, :].rearrange("p g c -> p (g c)"),
                                                cw[:, r, d * PAIRS + pair, :], start=(r == 0), stop=(r == 1))
            close_unit(last, ("kmat", 0))
            for i in range(4):
                form_a(("zu", i), ("k8", "w_in", 6 + i), xT)
            for i in range(4):
                form_a(("ga", i), ("k8", "w_in", 10 + i), xT)
            for i in range(4):
                form_a(("gb", i), ("k8", "w_in", 14 + i), xT)
            evacuated(pe, ("t_mem", 3))
            for i in range(4):
                form_a(("k", i), ("k8", "w_k", i), memT)
            for i in range(4):
                form_b(("v", i), ("k8", "w_v", i), memT)
            pe.wait_ge(zvn_ready, 1)
            pe.wait_ge(loads["sgu"], 16)
            pe.wait_ge(loads["sbias"], 16)
            pe.wait_ge(ones_ready, 1)
            for u in range(4):
                open_unit(pe, ("sgu", u))
                for j in range(2):
                    hd = 2 * u + j
                    for b in range(TB):
                        o = bank(("sgu", u))[:, j * TOK + b * P:j * TOK + (b + 1) * P]
                        nc.tensor.matmul(o, zv[:, b, hd * P:(hd + 1) * P], sguT[:, hd, :], start=True, stop=False)
                        last = nc.tensor.matmul(o, ones[0:1, :], sbias[0:1, hd * P:(hd + 1) * P],
                                                start=False, stop=True)
                close_unit(last, ("sgu", u))
            evacuated(pe, ("sgu", 3))
            for i in range(4):
                form_a(("pb", i), ("k8", "w_proj_b", i), zuT)
            pe.wait_ge(scan_done, 1)
            evacuated(pe, ("kmat", 0))
            for q in range(4):
                open_unit(pe, ("y", q))
                for i in range(4):
                    fwd, bwd = 4 * q + i, PAIRS + 4 * q + i
                    rows = slice(32 * i, 32 * i + 32)
                    for odd in range(2):
                        o = bank(("y", q))[rows, odd * SCAN:(odd + 1) * SCAN]
                        nc.tensor.matmul(o, kmat[rows, odd, q, :], uT[rows, q, odd::2], start=True, stop=False)
                        for r in range(2):
                            if odd:
                                nc.tensor.matmul(o, cw[:, r, fwd, :], states[:, :, r, fwd], start=False, stop=False)
                                last = nc.tensor.matmul(o[:, 0:SCAN - 1], cw_lam[:, r, bwd, :],
                                                        states[:, SCAN - 2::-1, r, bwd], start=False, stop=(r == 1))
                            else:
                                nc.tensor.matmul(o, cw[:, r, bwd, :], states[:, ::-1, r, bwd], start=False, stop=False)
                                last = nc.tensor.matmul(o[:, 1:SCAN], cw_lam[:, r, fwd, :],
                                                        states[:, 0:SCAN - 1, r, fwd], start=False, stop=(r == 1))
                close_unit(last, ("y", q))
            pe.wait_ge(yg_ready, 4)
            form_a4("glu", ("k4", "s5_w_glu", 0), ygT, 0)
            pe.wait_ge(ya_ready, 2)
            for c in range(2):
                form_a4("pa", ("k4", "w_proj_a", c), yaT, 2 * c)
            pe.wait_ge(m_split, 4)
            for i in range(4):
                split_b(("out", i), ("k8", "w_out", i))
            pe.wait_ge(xn_ready, 2)
            transposes("t_xattn", xn)
            evacuated(pe, ("t_xattn", 3))
            for i in range(4):
                split_a(("q", i), ("k8", "w_q", i))
            evacuated(pe, ("q", 3))
            evacuated(pe, ("v", 3))
            attention("x", 4, 2, lambda i, k: qT[:, 2 * i + k, :], lambda i, k: kT[:, 2 * i + k, :],
                      lambda i, j, m: v_t[:, m, (2 * i + j) * P:(2 * i + j + 1) * P], lambda i: (0, P), 2)
            evacuated(pe, ("x_o", 3))
            for i in range(4):
                split_b(("xo", i), ("k8", "w_xo", i))
            pe.wait_ge(xn_ready, 3)
            transposes("t_ffn", xn)
            evacuated(pe, ("t_ffn", 3))
            ffn("ffn", UNIT_AT[("t_in0", 0)])

            for m in range(2):
                pe.wait_ge(acc_free, 1 + m)
                pe.wait_ge(xn_ready, 4 + 2 * m)
                transposes(f"t_in{m}", h)
                evacuated(pe, (f"t_in{m}", 3))
                for i in range(5):
                    split_b((f"projb{m}", i), ("k8", f"w_in_{m}", i))
                for i in range(4):
                    split_a((f"qk{m}", i), ("k8", f"w_in_{m}", 5 + i))
                for i in range(4):
                    split_a((f"ga{m}", i), ("k8", f"w_in_{m}", 9 + i))
                pe.wait_ge(qk_roped, m + 1)
                for u in range(3):
                    open_unit(pe, (f"t_sw{m}", u))
                    for j in range(2 if u < 2 else 1):
                        for b in range(TB):
                            last = nc.tensor.transpose(
                                bank((f"t_sw{m}", u))[:, (2 * j + b) * P:(2 * j + b + 1) * P],
                                qk_t[:, b, (2 * u + j) * P:(2 * u + j + 1) * P], ident[:, :])
                    close_unit(last, (f"t_sw{m}", u))

                def half_gate(i):
                    if 0 <= i < 16 and i % 2:
                        split_a((f"gb{m}", i // 4), ("k8", f"w_in_{m}", 13 + i // 4), (i // 2 % 2,))

                evacuated(pe, (f"qk{m}", 3))
                evacuated(pe, (f"t_sw{m}", 2))
                attention(f"at{m}", 16, 1,
                          lambda i, k: (qnT if i < 8 else qsT)[64 * (i % 2):64 * (i % 2) + 64, i % 8 // 2, :],
                          lambda i, k: (knT[64 * (i % 2):64 * (i % 2) + 64, i // 2, :] if i < 8 else
                                        ksT[64 * (i % 2):64 * (i % 2) + 64, :]),
                          lambda i, j, mb: (v_na[:, mb, i * 64:(i + 1) * 64] if i < 8 else
                                            v_sw[:, mb, (i % 2) * 64:(i % 2) * 64 + 64]),
                          lambda i: (64 * (i % 2), 64), 1, half_gate)
                for c in range(2):
                    form_a4(f"bna{m}", ("k4", f"w_na_{m}", c), onT, 2 * c)
                evacuated(pe, (f"at{m}_o", 15))
                for c in range(2):
                    form_a4(f"bsw{m}", ("k4", f"w_sw_{m}", c), osT, 2 * c)
                pe.wait_ge(m_split, 4 + 4 * (m + 1))
                for i in range(4):
                    split_b((f"out{m}", i), ("k8", f"w_out_{m}", i))
                pe.wait_ge(xn_ready, 5 + 2 * m)
                transposes(f"t_mid{m}", h)
                evacuated(pe, (f"t_mid{m}", 3))
                if m == 0:
                    ffn("dense", UNIT_AT[("t_in1", 0)])

            pe.wait_ge(loads["consts"], 80)
            open_unit(pe, ("router", 0))
            for b in range(TB):
                for k in range(KD):
                    last = nc.tensor.matmul(bank(("router", 0))[:, b * 8:(b + 1) * 8], xT[:, k, b * P:(b + 1) * P],
                                            wr[:, k, :], start=(k == 0), stop=(k == KD - 1))
                    if b == k == 0:
                        last.then_inc(chunk_used, 1)
            close_unit(last, ("router", 0))
            pe.wait_ge(mask_ready, 1)
            open_unit(pe, ("pos", 0))
            pos = bank(("pos", 0))
            nc.tensor.matmul(pos[:, 0:8], before, mask[:, 0, :], start=True, stop=True)
            nc.tensor.matmul(pos[:, 8:16], ones[:, :], mask[:, 0, :], start=True, stop=False)
            nc.tensor.matmul(pos[:, 8:16], before, mask[:, 1, :], start=False, stop=True)
            nc.tensor.matmul(pos[:, 16:24], ones[:, :], mask[:, 0, :], start=True, stop=False)
            close_unit(nc.tensor.matmul(pos[:, 16:24], ones[:, :], mask[:, 1, :], start=False, stop=True),
                       ("pos", 0))
            all_banks_free(len(UNITS))

            def gather():
                for k in range(KD):
                    for b in range(TB):
                        for part in (h_h, h_l):
                            last = nc.tensor.matmul(psum[:, 6 + k // 4, (k % 4) * P:(k % 4 + 1) * P],
                                                    part[:, b, k * P:(k + 1) * P], pick[:, b, :],
                                                    start=(b == 0 and part is h_h), stop=(b == 1 and part is h_l))
                last.then_inc(gathered, 1)

            def transpose_pick():
                for b in range(TB):
                    last = nc.tensor.transpose(psum[:, 3, b * P:(b + 1) * P], pick[:, b, :].bitcast(F32), ident[:, :])
                last.then_inc(pickT_full, 1)

            pe.wait_ge(h_split, 1)
            pe.wait_ge(pick_ready, 1)
            gather()
            transpose_pick()
            f0 = ff0["moe"]
            pe.wait_ge(table_ready, 1)
            n_pass = pe.value_load(table[0:1, 0:1], min_val=MOE_E, max_val=MOE_E + OVER)
            with pe.Fori(0, n_pass) as p:
                chunk = [0]

                def next_chunk(k):
                    n = chunk[0]
                    chunk[0] += 1
                    pe.wait_ge(w_split, p * MOE_CHUNKS + (n + 1))
                    return [w[:, n % SPLITS, :].rearrange("p (k c) -> p k c", k=k) for w in (w_h, w_l)]

                def half_product(s, o):
                    wh, wl = next_chunk(KD)
                    out = psum[:, s % 2, o * 256:(o + 1) * 256]
                    for k in range(KD):
                        first = nc.tensor.matmul(out, xe_h[:, k, :], wh[:, k, :], start=(k == 0), stop=False)
                        if k == 0:
                            first.then_inc(w_used, 1)
                        nc.tensor.matmul(out, xe_h[:, k, :], wl[:, k, :], start=False, stop=False)
                        last = nc.tensor.matmul(out, xe_l[:, k, :], wh[:, k, :], start=False, stop=(k == KD - 1))
                    if o == 1:
                        last.then_inc(u_full, 1)

                def transpose_h(s):
                    pe.wait_ge(hT_ready, p * MOE_PER + (f0 + s + 1))
                    for k in range(2):
                        last = nc.tensor.transpose(psum[:, 2, (2 * (s % 2) + k) * P:(2 * (s % 2) + k + 1) * P],
                                                   e_h[:, s % 2, k * P:(k + 1) * P], ident[:, :])
                    last.then_inc(hT_full, 1)

                def expert_down(s):
                    pe.wait_ge(hT_moved, p * MOE_PER + (s + 1))
                    wh, wl = next_chunk(2)
                    for k in range(2):
                        for n, (x, w) in enumerate(((eT_h, wh), (eT_h, wl), (eT_l, wh))):
                            for c in range(2):
                                last = nc.tensor.matmul(psum[:, 4 + c, :], x[:, s % 2, k, :],
                                                        w[:, k, c * 512:(c + 1) * 512],
                                                        start=(s == 0 and k == n == 0),
                                                        stop=(s == MOE_PER - 1 and k == 1 and n == 2),
                                                        skip_group_check=True)
                                if k == n == c == 0:
                                    last.then_inc(w_used, 1)
                    if s == MOE_PER - 1:
                        last.then_inc(oe_full, 1)

                pe.wait_ge(xe_split, p + 1)
                for s in range(MOE_PER):
                    if s < 2:
                        pe.wait_ge(y_added, p * 4 + (s + 1))
                    pe.wait_ge(hT_ready, p * MOE_PER + (f0 + s - 1))
                    half_product(s, 0)
                    half_product(s, 1)
                    if s == 2:
                        pe.wait_ge(y_added, p * 4 + 4)
                    if s >= 2:
                        expert_down(s - 2)
                    if s >= 1:
                        transpose_h(s - 1)
                expert_down(MOE_PER - 2)
                transpose_h(MOE_PER - 1)
                pe.wait_ge(pick_ready, p + 2)
                gather()
                expert_down(MOE_PER - 1)
                transpose_pick()
                pe.wait_ge(oe_split, p + 1)
                pe.wait_ge(pickT_ready, p + 1)
                for b in range(TB):
                    for c in range(2):
                        nc.tensor.matmul(psum[:, 4 * b + c, :], pickT[:, b, :], o_h[:, c, :], start=True, stop=False)
                        nc.tensor.matmul(psum[:, 4 * b + c, :], pickT[:, b, :], o_l[:, c, :],
                                         start=False, stop=True).then_inc(scattered, 1)

        @block.scalar
        def _(act):
            def load(dst, src, name):
                act.dma_start(dst, src).then_inc(loads[name], 16)

            load(x_mem, a["mem"].rearrange("a (b p) d -> p (a b) d", p=P), "mem")
            load(ident[:, :], a["ident"], "ident")
            load(gains[:, :, :], a["gains"], "gains")
            load(pt[:, 0:3, :], a["s5_prm"], "prm")
            load(b_raw, a["s5_b"], "b")
            load(ln_v, a["sgu_ln"].rearrange("(o a) d -> o a d", o=1).to_broadcast([P, 2, D]), "lnv")
            load(sguT[:, :, :], a["sgu_w"], "sgu")
            load(cw, a["s5_c"], "cw")
            load(s5d[:, :], a["s5_d"], "s5d")
            load(bgate[:, :, :], a["b_gate"], "bgate")
            load(sink[:, :, :], a["sink"].rearrange("(o a) d -> o a d", o=1).to_broadcast([P, 2, 8]), "sink")

            stds = [0]

            def std():
                stds[0] += 1
                act.wait_ge(var_ready, stds[0])
                nc.scalar.activation(sd[:, :], ve[:, :], ACT.Sqrt).then_inc(std_ready, 1)

            def copy_T(u0, dst, gain=None):
                for u in range(4):
                    take_unit(act, (u0, u))
                    for j in range(2):
                        src = bank((u0, u))[:, j * TOK:(j + 1) * TOK]
                        k = 2 * u + j
                        if gain is None:
                            last = nc.scalar.activation(dst[:, k, :], src, ACT.Copy)
                        else:
                            last = nc.scalar.activation(dst[:, k, :], src, ACT.Identity,
                                                        scale=gains[:, gain, k:k + 1])
                    free_unit(last, (u0, u))

            def out_of(u, dst, func):
                take_unit(act, u)
                free_unit(nc.scalar.activation(dst, halves(bank(u)), func), u)

            def attention(name, heads, direct, dst_of, rows_of, dblocks, sink_of=None, between=None):
                g0 = head0[name]
                for i in range(heads + 2):
                    if i < heads:
                        g = g0 + i
                        act.wait_ge(negm_ready, g + 1)
                        if sink_of is not None and sink_of(i) is not None:
                            nc.scalar.activation(esink[:, g % 2, :], negm[:, g % 2, :], ACT.Exp, bias=sink_of(i))
                        for b in range(TB):
                            src = bank((name + "_s", i))[:, b * 256:(b + 1) * 256] if direct else logit[:, g % 2, b, :]
                            last = nc.scalar.activation(prob[:, g % 2, b, :], src, ACT.Exp,
                                                        bias=negm[:, g % 2, b:b + 1],
                                                        scale=XSCALE if direct else 1.0,
                                                        accum_out=ssum[:, g % 2, b:b + 1])
                        last.then_inc(exp_ready, 1)
                    if between is not None:
                        between(i)
                    if 0 <= i - 1 < heads:
                        u, g = (name + "_t", i - 1), g0 + i - 1
                        take_unit(act, u)
                        last = nc.scalar.activation(probT[:, g % 2, :, :], halves(bank(u)), ACT.Copy)
                        free_unit(last, u)
                    if 0 <= i - 2 < heads:
                        u = (name + "_o", i - 2)
                        take_unit(act, u)
                        r0, rn = rows_of(i - 2)
                        src = bank(u)[r0:r0 + rn, 0:dblocks * TOK]
                        last = nc.scalar.activation(dst_of(i - 2), src if dblocks == 1 else halves(src), ACT.Copy)
                        if direct:
                            last.then_inc(xf_high, 1)
                        else:
                            free_unit(last, u)

            def wf_part(name, n):
                at = CHUNK_AT[ffn_chunks(name)[n]]
                act.wait_ge(slot_full[at % SLOTS], 16 * (at // SLOTS + 1))
                if n >= SPLITS:
                    act.wait_ge(chunk_used, at - SPLITS + 1)
                nc.scalar.activation(wf_h[:, n % SPLITS, :], ring[:, at % SLOTS, :], ACT.Copy).then_inc(wf_high, 1)

            def high_part(p, n):
                act.wait_ge(slot_full[n % SLOTS], p * (16 * MOE_CHUNKS // SLOTS)
                            + 16 * (MOE_C0 // SLOTS + n // SLOTS + 1))
                nc.scalar.activation(w_h[:, n % SPLITS, :], ring[:, n % SLOTS, :], ACT.Copy).then_inc(w_high, 1)

            parts = [0]

            def wp_part():
                n = parts[0]
                parts[0] += 1
                at = CHUNK_AT[SPLIT[n][0]]
                act.wait_ge(slot_full[at % SLOTS], 16 * (at // SLOTS + 1))
                if n >= 2:
                    take_unit(act, SPLIT[n - 2][1])
                nc.scalar.activation(wp_h[:, n % 2, :], ring[:, at % SLOTS, :], ACT.Copy).then_inc(wp_high, 1)

            def merged_high(m0):
                for i in range(4):
                    act.wait_ge(m_ready, m0 + i + 1)
                    nc.scalar.activation(xf_h[:, 2 * i:2 * i + 2, :], gaT[:, 2 * i:2 * i + 2, :], ACT.Copy
                                         ).then_inc(xf_high, 1)

            def copy_xf(u0, gain=None):
                for u in range(4):
                    take_unit(act, (u0, u))
                    for j in range(2):
                        k = 2 * u + j
                        src = bank((u0, u))[:, j * TOK:(j + 1) * TOK]
                        if gain is None:
                            last = nc.scalar.activation(xf_h[:, k, :], src, ACT.Copy)
                        else:
                            last = nc.scalar.activation(xf_h[:, k, :], src, ACT.Identity,
                                                        scale=gains[:, gain, k:k + 1])
                    last.then_inc(xf_high, 1)

            def ffn(name):
                f0 = ff0[name]
                for n, (part, s) in enumerate(FF_ORDER):
                    if part == "gate":
                        act.wait_ge(g_full, f0 + s + 1)
                        if s >= 1:
                            act.wait_ge(hT_ready, f0 + s)
                        nc.scalar.activation(silu[:, :], psum[:, 2 * (s % 2), :], ACT.Silu).then_inc(silu_ready, 1)
                    if n + SPLITS < FF_CHUNKS:
                        wf_part(name, n + SPLITS)
                    elif n < FF_CHUNKS - 1:
                        wp_part()
                    if part == "up":
                        act.wait_ge(product_ready, wf0[name] // 3 + s + 1)
                        if s >= 2:
                            act.wait_ge(down_done, f0 + s - 1)
                        nc.scalar.activation(hf_h[:, s % 2, :, :], halves(silu[:, :]), ACT.Copy).then_inc(hf_high, 1)

            std()
            act.wait_ge(loads["gains"], 16)
            copy_T("t_x", xT, 0)
            std()
            copy_T("t_mem", memT, 1)
            for i in range(2):
                out_of(("xa", i), uT[:, 2 * i:2 * i + 2, :], ACT.Copy)
            act.wait_ge(angle_ready, 1)
            nc.scalar.activation(pt[:, 20, :], pt[:, 12, :], ACT.Sin)
            nc.scalar.activation(pt[:, 21, :], pt[:, 12, :], ACT.Sin, scale=0.5).then_inc(sin_ready, 1)
            for i in range(4):
                out_of(("zv", i), zv[:, :, i * 256:(i + 1) * 256], ACT.Gelu_apprx_tanh)
            std()
            for u in range(8):
                take_unit(act, ("t_b", u))
                n = 4 * (u % 4)
                last = nc.scalar.activation(bT[u // 4][:, n:n + 4, :],
                                            bank(("t_b", u)).rearrange("p (n m) -> p n m", m=P), ACT.Copy)
                free_unit(last, ("t_b", u))
            for u in range(0, BLK // 2, 2):
                take_unit(act, ("bu", u))
                last = nc.scalar.activation(states[:, :, :, bu_block(u):bu_block(u) + 5:4].rearrange("p t r k -> p k r t"),
                                            bank(("bu", u)).rearrange("p (k r t) -> p k r t", k=2, r=2), ACT.Copy)
                free_unit(last, ("bu", u))
            take_unit(act, ("kmat", 0))
            last = nc.scalar.activation(kmat[:, :, :, :].rearrange("p d q m -> p (d q m)"),
                                        bank(("kmat", 0))[:, 0:256], ACT.Copy)
            free_unit(last, ("kmat", 0))
            for i in range(4):
                out_of(("zu", i), zuT[:, 2 * i:2 * i + 2, :], ACT.Gelu_apprx_tanh)
            for i in range(4):
                out_of(("ga", i), gaT[:, 2 * i:2 * i + 2, :], ACT.Sigmoid)
            for i in range(4):
                out_of(("gb", i), gbT[:, 2 * i:2 * i + 2, :], ACT.Sigmoid)
            act.wait_ge(zvn_ready, 1)
            for i in range(4):
                out_of(("k", i), kT[:, 2 * i:2 * i + 2, :], ACT.Copy)
            for i in range(4):
                out_of(("v", i), v_t[:, :, i * 256:(i + 1) * 256], ACT.Copy)
            act.dma_start(sbias[0:1, :], a["sgu_bias"]).then_inc(loads["sbias"], 16)
            for q in range(4):
                evacuated(act, ("y", q))
                nc.scalar.activation(ygT[:, q, :], ygT[:, q, :], ACT.Gelu_apprx_tanh).then_inc(yg_ready, 1)
            for i in range(2):
                take_unit(act, ("glu", i))
                last = nc.scalar.activation(yaT[:, 2 * i:2 * i + 2, :], halves(bank(("glu", i))), ACT.Sigmoid)
                free_unit(last, ("glu", i))
            for _ in range(2):
                wp_part()
            merged_high(0)
            for _ in range(4):
                wp_part()
            std()
            copy_xf("t_xattn", 2)
            for i in range(4):
                if i < 3:
                    wp_part()
                out_of(("q", i), qT[:, 2 * i:2 * i + 2, :], ACT.Copy)
            attention("x", 4, True, lambda i: xf_h[:, 2 * i:2 * i + 2, :], lambda i: (0, P), 2)
            for _ in range(3):
                wp_part()
            for n in range(SPLITS - 1):
                wf_part("ffn", n)
            std()
            copy_xf("t_ffn", 3)
            wf_part("ffn", SPLITS - 1)
            ffn("ffn")
            std()
            std()
            act.wait_ge(loads["bgate"], 16)
            for m in range(2):
                copy_xf(f"t_in{m}")
                for i in range(2):
                    wp_part()
                    out_of((f"projb{m}", i), v_na[:, :, i * 256:(i + 1) * 256], ACT.Copy)
                for i in range(2):
                    wp_part()
                    out_of((f"projb{m}", 2 + i), qk_t[:, :, i * 256:(i + 1) * 256], ACT.Copy)
                u = (f"projb{m}", 4)
                wp_part()
                take_unit(act, u)
                nc.scalar.activation(qk_t[:, :, 512:640], halves(bank(u))[:, :, 0:128], ACT.Copy)
                last = nc.scalar.activation(v_sw, halves(bank(u))[:, :, 128:256], ACT.Copy)
                free_unit(last, u)
                for i in range(2):
                    wp_part()
                    out_of((f"qk{m}", i), qnT[:, 2 * i:2 * i + 2, :], ACT.Copy)
                for i in range(2):
                    wp_part()
                    out_of((f"qk{m}", 2 + i), knT[:, 2 * i:2 * i + 2, :], ACT.Copy)

                def gate(name, i, dst, col0):
                    take_unit(act, (name, i))
                    for j in range(2):
                        k = 2 * i + j
                        last = nc.scalar.activation(dst[:, k, :], bank((name, i))[:, j * TOK:(j + 1) * TOK],
                                                    ACT.Sigmoid, bias=bgate[:, m, col0 + k:col0 + k + 1])
                    free_unit(last, (name, i))

                for i in range(4):
                    wp_part()
                    gate(f"ga{m}", i, gaT, 0)
                for u in range(3):
                    take_unit(act, (f"t_sw{m}", u))
                    if u < 2:
                        last = nc.scalar.activation(qsT[:, 2 * u:2 * u + 2, :], halves(bank((f"t_sw{m}", u))), ACT.Copy)
                    else:
                        last = nc.scalar.activation(ksT, bank((f"t_sw{m}", u))[:, 0:TOK], ACT.Copy)
                    free_unit(last, (f"t_sw{m}", u))

                def gate_b(i):
                    if i > 0 and i % 4 == 0:
                        gate(f"gb{m}", i // 4 - 1, gbT, 8)
                        wp_part()

                attention(f"at{m}", 16, False,
                          lambda i: (onT if i < 8 else osT)[64 * (i % 2):64 * (i % 2) + 64, i % 8 // 2, :],
                          lambda i: (64 * (i % 2), 64), 1, lambda i: sink_col(m, i - 8) if i >= 8 else None, gate_b)
                merged_high(4 + 4 * m)
                for _ in range(2):
                    wp_part()
                if m == 0:
                    for n in range(SPLITS - 1):
                        wf_part("dense", n)
                    std()
                    copy_xf(f"t_mid{m}")
                    wf_part("dense", SPLITS - 1)
                    ffn("dense")
                    std()
                else:
                    std()
                    copy_T(f"t_mid{m}", xT)
            for n in range(AHEAD):
                high_part(0, n)
            act.wait_ge(rexp_in, 1)
            nc.scalar.activation(rt[:, 8, :, 0], rt[:, 7, :, 0], ACT.Exp).then_inc(rexp_out, 1)
            f0 = ff0["moe"]

            def move_xe(n):
                act.wait_ge(gathered, n)
                nc.scalar.activation(xe_h[:, :, :].rearrange("p (b k) m -> p b (k m)", b=2), psum[:, 6:8, :],
                                     ACT.Copy).then_inc(xe_high, 1)

            def move_pickT(n):
                act.wait_ge(pickT_full, n)
                nc.scalar.activation(pickT[:, :, :], halves(psum[:, 3, 0:TOK]), ACT.Copy).then_inc(pickT_ready, 1)

            chunks, after = moe_events()
            move_xe(1)
            move_pickT(1)
            act.wait_ge(table_ready, 1)
            n_pass = act.value_load(table[0:1, 0:1], min_val=MOE_E, max_val=MOE_E + OVER)
            with act.Fori(0, n_pass) as p:
                for n in range(-1, len(chunks)):
                    if n >= 0:
                        for what, s in after.get(n, []):
                            if what == "prod":
                                act.wait_ge(u_full, p * MOE_PER + (f0 + s + 1))
                                nc.scalar.activation(e_silu[:, s % 2, :], psum[:, s % 2, 0:256], ACT.Silu
                                                     ).then_inc(silu_ready, 1)
                            else:
                                act.wait_ge(hT_full, p * MOE_PER + (s + 1))
                                nc.scalar.activation(eT_h[:, s % 2, :, :],
                                                     halves(psum[:, 2, 256 * (s % 2):256 * (s % 2) + 256]),
                                                     ACT.Copy).then_inc(hT_high, 1)
                    if n == len(chunks) - 2:
                        move_xe(p + 2)
                    if n + SPLITS < len(chunks) + AHEAD:
                        act.wait_ge(w_used, p * MOE_CHUNKS + (n + 2))
                        high_part(p, n + SPLITS)
                act.wait_ge(oe_full, p + 1)
                nc.scalar.activation(o_h[:, :, :], psum[:, 4:6, :], ACT.Copy).then_inc(oe_high, 1)
                act.wait_ge(scattered, p * 4 + 4)
                move_pickT(p + 2)
            std()
            act.wait_ge(out_ready, 1)
            act.dma_start(out.rearrange("a (b p) d -> p (a b) d", p=P), ysum[:, :, :]).then_inc(stored, 16)
            act.wait_ge(stored, 16)

        @block.vector
        def _(dve):
            V = nc.vector
            steps = [0]

            def link(ins):
                steps[0] += 1
                ins.then_inc(dve_step, 1)
                dve.wait_ge(dve_step, steps[0])

            norms = [0]

            def stats(src, rms, eps, meanwhile=None):
                norms[0] += 1
                for b in range(TB):
                    for c in range(2):
                        last = V.bn_stats(st[:, b, c, :], src[:, b, c * 512:(c + 1) * 512])
                link(last)
                for b in range(TB):
                    last = V.bn_aggr(mv[:, b, :], st[:, b, :, :])
                link(last)
                if rms:
                    link(V.tensor_tensor(msq[:, :], mv[:, :, 0], mv[:, :, 0], ALU.mult))
                    link(V.tensor_tensor(msq[:, :], msq[:, :], mv[:, :, 1], ALU.add))
                    V.tensor_scalar(ve[:, :], msq[:, :], eps, None, ALU.add).then_inc(var_ready, 1)
                else:
                    V.tensor_scalar(ve[:, :], mv[:, :, 1], eps, None, ALU.add).then_inc(var_ready, 1)
                if meanwhile is not None:
                    meanwhile()
                dve.wait_ge(std_ready, norms[0])
                link(V.reciprocal(rstd[:, :], sd[:, :]))

            def scaled(dst, src, ready):
                for b in range(TB):
                    last = V.tensor_scalar(dst[:, b, :], src[:, b, :], rstd[:, b:b + 1], None, ALU.mult)
                last.then_inc(ready, 1)

            def layer_norm(x, g, b_, eps):
                def times_gain():
                    for b in range(TB):
                        V.scalar_tensor_tensor(x[:, b, :], x[:, b, :], mv[:, b, 0:1], g, ALU.subtract, ALU.mult)

                stats(x, False, eps, times_gain)
                for b in range(TB):
                    last = V.scalar_tensor_tensor(x[:, b, :], x[:, b, :], rstd[:, b:b + 1], b_, ALU.mult, ALU.add)
                return last

            def residual(unit, i, alpha=None):
                take_unit(dve, unit)
                hs = h[:, :, i * 256:(i + 1) * 256]
                if alpha is None:
                    last = V.tensor_tensor(hs, hs, halves(bank(unit)), ALU.add)
                else:
                    last = V.scalar_tensor_tensor(hs, hs, alpha, halves(bank(unit)), ALU.mult, ALU.add)
                free_unit(last, unit)
                return last

            def attention(name, heads, bias_of, sink_of):
                g0 = head0[name]
                for i in range(heads + (2 if bias_of is None else 1)):
                    if i < heads:
                        g = g0 + i
                        u = (name + "_s", i)
                        take_unit(dve, u)
                        if bias_of is None:
                            link(V.reduce_max(mx[:, g % 2, :], halves(bank(u)), AX_X))
                            V.tensor_scalar(negm[:, g % 2, :], mx[:, g % 2, :], -XSCALE, None,
                                            ALU.mult).then_inc(negm_ready, 1)
                        else:
                            last = V.scalar_tensor_tensor(logit[:, g % 2, :, :], halves(bank(u)), HSCALE,
                                                          bias_of(i), ALU.mult, ALU.add)
                            free_unit(last, u)
                            evacuated(dve, u)
                            link(V.reduce_max(mx[:, g % 2, :], logit[:, g % 2, :, :], AX_X))
                            if sink_of(i) is not None:
                                link(V.tensor_scalar(mx[:, g % 2, :], mx[:, g % 2, :], sink_of(i), None, ALU.max))
                            V.tensor_scalar(negm[:, g % 2, :], mx[:, g % 2, :], -1.0, None,
                                            ALU.mult).then_inc(negm_ready, 1)
                    if 0 <= i - 1 < heads:
                        g = g0 + i - 1
                        dve.wait_ge(exp_ready, g + 1)
                        if sink_of is not None and sink_of(i - 1) is not None:
                            link(V.tensor_tensor(ssum[:, g % 2, :], ssum[:, g % 2, :], esink[:, g % 2, :], ALU.add))
                        link(V.reciprocal(rsum[:, g % 2, :], ssum[:, g % 2, :]))
                        for b in range(TB):
                            last = V.tensor_scalar(prob[:, g % 2, b, :], prob[:, g % 2, b, :],
                                                   rsum[:, g % 2, b:b + 1], None, ALU.mult)
                            if b == 0 and bias_of is None:
                                free_unit(last, (name + "_s", i - 1))
                        last.then_inc(prob_ready, 1)
                    if bias_of is None and i >= 2:
                        xf_rest_of((name + "_o", i - 2), "x_o", i - 2)
                    if bias_of is not None and i in (5, 9, 13):
                        wp_rest()

            rests = [0]

            def wp_rest():
                n = rests[0]
                rests[0] += 1
                dve.wait_ge(wp_high, n + 1)
                V.tensor_tensor(wp_l[:, n % 2, :], ring[:, CHUNK_AT[SPLIT[n][0]] % SLOTS, :],
                                wp_h[:, n % 2, :].bitcast(F32), ALU.subtract).then_inc(wp_split, 1)

            def merged_rest(use, i):
                dve.wait_ge(xf_high, 4 * XF_USES.index(use) + i + 1)
                V.tensor_tensor(xf_l[:, 2 * i:2 * i + 2, :], gaT[:, 2 * i:2 * i + 2, :],
                                xf_h[:, 2 * i:2 * i + 2, :].bitcast(F32), ALU.subtract).then_inc(m_split, 1)

            def xf_rest_of(unit, use, i, gain=None):
                take_unit(dve, unit)
                dve.wait_ge(xf_high, 4 * XF_USES.index(use) + i + 1)
                high = xf_h[:, 2 * i:2 * i + 2, :].bitcast(F32)
                if gain is None:
                    last = V.tensor_tensor(xf_l[:, 2 * i:2 * i + 2, :], halves(bank(unit)), high, ALU.subtract)
                else:
                    for j in range(2):
                        k = 2 * i + j
                        last = V.scalar_tensor_tensor(xf_l[:, k, :], bank(unit)[:, j * TOK:(j + 1) * TOK],
                                                      gains[:, gain, k:k + 1], high[:, j, :], ALU.mult, ALU.subtract)
                free_unit(last, unit)

            def wf_rest(name, n):
                at = CHUNK_AT[ffn_chunks(name)[n]]
                dve.wait_ge(wf_high, wf0[name] + n + 1)
                V.tensor_tensor(wf_l[:, n % SPLITS, :], ring[:, at % SLOTS, :], wf_h[:, n % SPLITS, :].bitcast(F32),
                                ALU.subtract).then_inc(wf_split, 1)

            def xf_rest(u0, gain=None):
                for u in range(4):
                    xf_rest_of((u0, u), u0, u, gain)

            def ffn(name):
                f0 = ff0[name]
                for n, (part, s) in enumerate(FF_ORDER):
                    if part == "up":
                        dve.wait_ge(silu_ready, f0 + s + 1)
                        dve.wait_ge(u_full, f0 + s + 1)
                        V.tensor_tensor(silu[:, :], silu[:, :], psum[:, 2 * (s % 2) + 1, :],
                                        ALU.mult).then_inc(product_ready, 1)
                    if n + SPLITS < FF_CHUNKS:
                        wf_rest(name, n + SPLITS)
                    elif n < FF_CHUNKS - 1:
                        wp_rest()
                    if part == "up":
                        dve.wait_ge(hf_high, wf0[name] // 3 + s + 1)
                        V.tensor_tensor(hf_l[:, s % 2, :, :], halves(silu[:, :]), hf_h[:, s % 2, :, :].bitcast(F32),
                                        ALU.subtract).then_inc(hT_ready, 1)

            def add_sums(n, alpha=None):
                dve.wait_ge(down_done, FF_STEPS * n)
                for b in range(TB):
                    for c in range(2):
                        hs = h[:, b, c * 512:(c + 1) * 512]
                        acc = psum[:, 4 + 2 * b + c, :]
                        if alpha is None:
                            last = V.tensor_tensor(hs, hs, acc, ALU.add)
                        else:
                            last = V.scalar_tensor_tensor(hs, hs, alpha, acc, ALU.mult, ALU.add)
                last.then_inc(acc_free, 1)
                dve.wait_ge(acc_free, n)

            V.memset(ones[:, :], 1.0).then_inc(ones_ready, 1)
            dve.wait_ge(loads["x"], 16)
            stats(h, True, EPS)
            scaled(xn, h, xn_ready)
            dve.wait_ge(loads["mem"], 16)
            stats(x_mem, True, EPS)
            scaled(n_mem, x_mem, memn_ready)

            row = lambda n: pt[:, n, :]
            LR, LI, LS, STEP, X, KF, R, H, KI, ER = range(10)
            ANG, KA, MAG, NR, ARE, AIM, CRE, CIM, T1, T2 = 12, 10, 11, 13, 14, 15, 16, 17, 18, 19
            SN, SH = 20, 21
            magic = 1.5 * 2.0 ** 23

            def exp_of(dst, src):
                link(V.tensor_scalar(row(X), row(src), -87.0, 88.0, ALU.max, ALU.min))
                link(V.tensor_scalar(row(KF), row(X), 1.4426950408889634, magic, ALU.mult, ALU.add))
                link(V.tensor_scalar(row(KF), row(KF), magic, None, ALU.subtract))
                link(V.scalar_tensor_tensor(row(R), row(KF), -0.693359375, row(X), ALU.mult, ALU.add))
                link(V.scalar_tensor_tensor(row(R), row(KF), 2.12194440e-4, row(R), ALU.mult, ALU.add))
                link(V.tensor_scalar(row(H), row(R), 1.0 / 5040, None, ALU.mult))
                for c in (1.0 / 720, 1.0 / 120, 1.0 / 24, 1.0 / 6, 0.5, 1.0):
                    link(V.scalar_tensor_tensor(row(H), row(H), c, row(R), ALU.add, ALU.mult))
                link(V.tensor_scalar(row(KI).bitcast(I32), row(KF), 127.0, 2.0 ** 23, ALU.add, ALU.mult))
                link(V.scalar_tensor_tensor(row(dst), row(H), 1.0, row(KI), ALU.add, ALU.mult))

            dve.wait_ge(loads["prm"], 16)
            exp_of(STEP, LS)
            link(V.tensor_tensor(row(MAG), row(LR), row(STEP), ALU.mult))
            exp_of(ER, MAG)
            link(V.tensor_tensor(row(ANG), row(LI), row(STEP), ALU.mult))
            link(V.tensor_scalar(row(KA), row(ANG), 1.0 / (2 * np.pi), magic, ALU.mult, ALU.add))
            link(V.tensor_scalar(row(KA), row(KA), magic, None, ALU.subtract))
            c1 = 6.28125
            c2 = float(np.float32(np.floor((2 * np.pi - c1) * 2 ** 21) / 2 ** 21))
            c3 = float(2 * np.pi - c1 - c2)
            for c in (c1, c2, c3):
                link(V.scalar_tensor_tensor(row(ANG), row(KA), -c, row(ANG), ALU.mult, ALU.add))
            V.tensor_scalar(row(ANG), row(ANG), -3.1415925, 3.1415925, ALU.max, ALU.min).then_inc(angle_ready, 1)
            for w in b_wide_f:
                last = V.memset(w, 0.0)
            link(last)
            dve.wait_ge(sin_ready, 1)
            link(V.tensor_tensor(row(SH), row(SH), row(SH), ALU.mult))
            link(V.tensor_scalar(row(SH), row(SH), -2.0, 1.0, ALU.mult, ALU.add))
            V.tensor_tensor(row(ARE), row(ER), row(SH), ALU.mult)
            link(V.tensor_tensor(row(AIM), row(ER), row(SN), ALU.mult))
            V.tensor_tensor(row(T1), row(ARE), row(ARE), ALU.mult)
            link(V.tensor_tensor(row(T2), row(AIM), row(AIM), ALU.mult))
            for r in range(2):
                V.tensor_tensor(lam_a[:, 0, r, :], row(T1), row(T2), ALU.subtract)
            V.scalar_tensor_tensor(lam_a[:, 1, 0, :], row(ARE), 2.0, row(AIM), ALU.mult, ALU.mult)
            V.scalar_tensor_tensor(lam_a[:, 1, 1, :], row(ARE), -2.0, row(AIM), ALU.mult, ALU.mult)
            link(V.tensor_scalar(row(NR), row(ARE), -1.0, None, ALU.add))
            V.tensor_tensor(row(T1), row(LR), row(LR), ALU.mult)
            link(V.tensor_tensor(row(T2), row(LI), row(LI), ALU.mult))
            link(V.tensor_tensor(row(MAG), row(T1), row(T2), ALU.add))
            link(V.reciprocal(row(MAG), row(MAG)))
            V.tensor_tensor(row(T1), row(NR), row(LR), ALU.mult)
            V.tensor_tensor(row(T2), row(AIM), row(LI), ALU.mult)
            V.tensor_tensor(row(CRE), row(AIM), row(LR), ALU.mult)
            link(V.tensor_tensor(row(CIM), row(NR), row(LI), ALU.mult))
            V.tensor_tensor(row(T1), row(T1), row(T2), ALU.add)
            link(V.tensor_tensor(row(CIM), row(CRE), row(CIM), ALU.subtract))
            V.tensor_tensor(row(CRE), row(T1), row(MAG), ALU.mult)
            link(V.tensor_tensor(row(CIM), row(CIM), row(MAG), ALU.mult))
            dve.wait_ge(loads["b"], 16)
            cre = row(CRE).unsqueeze(2).to_broadcast([P, BLK, S5_C])
            cim = row(CIM).unsqueeze(2).to_broadcast([P, BLK, S5_C])
            for n in range(2):
                for out_r, (r0, r1, op) in enumerate(((0, 1, ALU.subtract), (1, 0, ALU.add))):
                    V.tensor_tensor(b_tmp[:, 0], b_raw[:, r0], cre, ALU.mult)
                    link(V.tensor_tensor(b_tmp[:, 1], b_raw[:, r1], cim, ALU.mult))
                    for g in range(2):
                        rows = slice(64 * g, 64 * g + 64)
                        last = V.tensor_tensor(b_wide[n][rows, out_r, :, g, :], b_tmp[rows, 0], b_tmp[rows, 1], op)
                    link(last)
                if n == 0:
                    V.tensor_tensor(row(T1), row(CRE), row(ARE), ALU.mult)
                    V.tensor_tensor(row(T2), row(CIM), row(AIM), ALU.mult)
                    V.tensor_tensor(row(MAG), row(CRE), row(AIM), ALU.mult)
                    link(V.tensor_tensor(row(CIM), row(CIM), row(ARE), ALU.mult))
                    V.tensor_tensor(row(CRE), row(T1), row(T2), ALU.subtract)
                    link(V.tensor_tensor(row(CIM), row(CIM), row(MAG), ALU.add))
            V.memset(msq[:, :], 0.0).then_inc(bwide_ready, 1)
            dve.wait_ge(loads["cw"], 16)
            link(V.tensor_scalar(cw[:, 1], cw[:, 1], -1.0, None, ALU.mult))
            lam_re = row(ARE).unsqueeze(2).to_broadcast([P, BLK, 32])
            lam_im = row(AIM).unsqueeze(2).to_broadcast([P, BLK, 32])
            for r, (one, other, op) in enumerate(((0, 1, ALU.add), (1, 0, ALU.subtract))):
                V.tensor_tensor(cw_lam[:, r], cw[:, one], lam_re, ALU.mult)
                link(V.tensor_tensor(c_tmp, cw[:, other], lam_im, ALU.mult))
                link(V.tensor_tensor(cw_lam[:, r], cw_lam[:, r], c_tmp, op))
            V.memset(msq[:, :], 0.0).then_inc(cneg_ready, 1)

            evacuated(dve, ("zv", 3))
            dve.wait_ge(loads["lnv"], 16)
            layer_norm(zv, ln_v[:, 0, :], ln_v[:, 1, :], EPS).then_inc(zvn_ready, 1)

            for u in range(1, BLK // 2, 2):
                take_unit(dve, ("bu", u))
                last = V.tensor_copy(states[:, :, :, bu_block(u):bu_block(u) + 5:4].rearrange("p t r k -> p k r t"),
                                     bank(("bu", u)).rearrange("p (k r t) -> p k r t", k=2, r=2))
                free_unit(last, ("bu", u))
            evacuated(dve, ("bu", BLK // 2 - 1))
            evacuated(dve, ("bu", BLK // 2 - 2))
            ops = 3

            def scan_at(prev, cur, done):
                V.tensor_tensor(scan_t[:, 0:2, :, :], prev.to_broadcast([P, 2, 2, BLK]), lam_a[:, :, :, :],
                                ALU.mult).then_inc(scan_step, 1)
                dve.wait_ge(scan_step, done + 1)
                V.tensor_tensor(scan_t[:, 2], scan_t[:, 0], scan_t[:, 1, ::-1, :], ALU.add).then_inc(scan_step, 1)
                dve.wait_ge(scan_step, done + 2)
                cur = cur.rearrange("p a r k -> p (a r) k")
                V.tensor_tensor(cur, scan_t[:, 2], cur, ALU.add).then_inc(scan_step, 1)
                dve.wait_ge(scan_step, done + 3)

            per = 6
            turns = (SCAN - 1) // per
            with dve.Fori(0, turns) as t:
                for j in range(per):
                    scan_at(states[:, bass.ds(t * per + j, 1), :, :], states[:, bass.ds(t * per + (j + 1), 1), :, :],
                            t * (ops * per) + ops * j)
            for m in range(turns * per + 1, SCAN):
                scan_at(states[:, m - 1:m, :, :], states[:, m:m + 1, :, :], ops * (m - 1))
            V.memset(msq[:, :], 0.0).then_inc(scan_done, 1)

            evacuated(dve, ("zu", 3))
            for u in range(4):
                take_unit(dve, ("sgu", u))
                zs = zuT[:, 2 * u:2 * u + 2, :]
                last = V.tensor_tensor(zs, zs, halves(bank(("sgu", u))), ALU.mult)
                free_unit(last, ("sgu", u))
            evacuated(dve, ("gb", 3))
            for i in range(4):
                take_unit(dve, ("pb", i))
                gs = gbT[:, 2 * i:2 * i + 2, :]
                last = V.tensor_tensor(gs, gs, halves(bank(("pb", i))), ALU.mult)
                free_unit(last, ("pb", i))
            dve.wait_ge(loads["s5d"], 16)
            for q in range(4):
                take_unit(dve, ("y", q))
                last = V.scalar_tensor_tensor(ygT[:, q, :].rearrange("p (j e) -> p j e", e=2),
                                              uT[:, q, :].rearrange("p (j e) -> p j e", e=2), s5d[:, q:q + 1],
                                              bank(("y", q))[:, 0:TOK].rearrange("p (e j) -> p j e", e=2),
                                              ALU.mult, ALU.add)
                free_unit(last, ("y", q))
            for i in range(2):
                evacuated(dve, ("glu", i))
                ys = yaT[:, 2 * i:2 * i + 2, :]
                V.tensor_tensor(ys, ys, ygT[:, 2 * i:2 * i + 2, :], ALU.mult).then_inc(ya_ready, 1)

            for _ in range(2):
                wp_rest()
            for i in range(4):
                take_unit(dve, ("pa", i))
                gs = gaT[:, 2 * i:2 * i + 2, :]
                last = V.tensor_tensor(gs, gs, halves(bank(("pa", i))), ALU.mult)
                free_unit(last, ("pa", i))
                evacuated(dve, ("pa", i))
                V.tensor_tensor(gs, gs, gbT[:, 2 * i:2 * i + 2, :], ALU.add).then_inc(m_ready, 1)
                if i >= 1:
                    merged_rest("out", i - 1)
            merged_rest("out", 3)
            for i in range(4):
                if i < 2:
                    wp_rest()
                residual(("out", i), i)
                if i == 2:
                    wp_rest()
            evacuated(dve, ("out", 3))
            stats(h, True, EPS)
            scaled(xn, h, xn_ready)
            wp_rest()
            xf_rest("t_xattn", 2)
            for _ in range(3):
                wp_rest()
            attention("x", 4, None, None)
            for i in range(4):
                if i < 3:
                    wp_rest()
                residual(("xo", i), i)
                if i >= 1 and i < 3:
                    wf_rest("ffn", i - 1)
            evacuated(dve, ("xo", 3))
            stats(h, True, EPS)
            scaled(xn, h, xn_ready)
            xf_rest("t_ffn", 3)
            wf_rest("ffn", SPLITS - 1)
            ffn("ffn")
            add_sums(1)
            dve.wait_ge(loads["bc0"], 16 * 3)
            stats(h, True, EPS)
            for b in range(TB):
                last = V.scalar_tensor_tensor(h[:, b, :], h[:, b, :], rstd[:, b:b + 1], bc[:, 0, :],
                                              ALU.mult, ALU.mult)
            link(last)
            layer_norm(h, bc[:, 2, :], bc[:, 3, :], LN_EPS).then_inc(xn_ready, 1)
            dve.wait_ge(xn_ready, 4)
            dve.wait_ge(loads["consts"], 80)
            dve.wait_ge(loads["sink"], 16)
            for m in range(2):
                xf_rest(f"t_in{m}")
                for _ in range(6):
                    wp_rest()
                evacuated(dve, (f"projb{m}", 4))
                heads = qk_t[:, :, 0:640].rearrange("p b (h d) -> p b h d", d=64)
                for b in range(TB):
                    x1, x2 = heads[:, b, :, 0:8], heads[:, b, :, 8:16]
                    cos = rope[:, b, 0, :].unsqueeze(1).to_broadcast([P, 10, 8])
                    sin = rope[:, b, 1, :].unsqueeze(1).to_broadcast([P, 10, 8])
                    t = [rtmp[:, n, b, 0:80].rearrange("p (h f) -> p h f", f=8) for n in range(4)]
                    V.tensor_tensor(t[0], x1, cos, ALU.mult)
                    V.tensor_tensor(t[1], x2, sin, ALU.mult)
                    V.tensor_tensor(t[2], x2, cos, ALU.mult)
                    link(V.tensor_tensor(t[3], x1, sin, ALU.mult))
                    V.tensor_tensor(x1, t[0], t[1], ALU.subtract)
                    last = V.tensor_tensor(x2, t[2], t[3], ALU.add)
                last.then_inc(qk_roped, 1)
                for _ in range(7):
                    wp_rest()
                dve.wait_ge(loads["nab"], 16 * (m + 1))
                attention(f"at{m}", 16, lambda i: nabias[:, i, :, :] if i < 8 else swmask,
                          lambda i: sink_col(m, i - 8) if i >= 8 else None)
                wp_rest()
                evacuated(dve, (f"gb{m}", 3))
                for i in range(4):
                    take_unit(dve, (f"bna{m}", i))
                    gs = gaT[:, 2 * i:2 * i + 2, :]
                    last = V.tensor_tensor(gs, gs, halves(bank((f"bna{m}", i))), ALU.mult)
                    free_unit(last, (f"bna{m}", i))
                for i in range(4):
                    take_unit(dve, (f"bsw{m}", i))
                    gs = gbT[:, 2 * i:2 * i + 2, :]
                    last = V.tensor_tensor(gs, gs, halves(bank((f"bsw{m}", i))), ALU.mult)
                    free_unit(last, (f"bsw{m}", i))
                    evacuated(dve, (f"bsw{m}", i))
                    ms = gaT[:, 2 * i:2 * i + 2, :]
                    V.tensor_tensor(ms, ms, gs, ALU.add).then_inc(m_ready, 1)
                    if i >= 1:
                        merged_rest(f"out{m}", i - 1)
                merged_rest(f"out{m}", 3)
                for i in range(4):
                    if i < 2:
                        wp_rest()
                    residual((f"out{m}", i), i, ALPHA)
                    if m == 0 and 1 <= i < 3:
                        wf_rest("dense", i - 1)
                evacuated(dve, (f"out{m}", 3))
                dve.wait_ge(loads["ln1"], 32 * (m + 1))
                layer_norm(h, bc[:, 0, :], bc[:, 1, :], LN_EPS).then_inc(xn_ready, 1)
                dve.wait_ge(xn_ready, 5 + 2 * m)
                if m == 0:
                    xf_rest("t_mid0")
                    wf_rest("dense", SPLITS - 1)
                    ffn("dense")
                    add_sums(2, ALPHA)
                    dve.wait_ge(loads["ln2"], 32)
                    layer_norm(h, bc[:, 2, :], bc[:, 3, :], LN_EPS).then_inc(xn_ready, 1)
                    dve.wait_ge(xn_ready, 6)

            def low_part(p, n):
                dve.wait_ge(w_high, p * MOE_CHUNKS + (n + 1))
                V.tensor_tensor(w_l[:, n % SPLITS, :], ring[:, n % SLOTS, :], w_h[:, n % SPLITS, :].bitcast(F32),
                                ALU.subtract).then_inc(w_split, 1)

            V.tensor_copy(h_h[:, :, :], h[:, :, :]).then_inc(h_high, 1)
            dve.wait_ge(h_high, 1)
            V.tensor_tensor(h_l[:, :, :], h[:, :, :], h_h[:, :, :].bitcast(F32), ALU.subtract).then_inc(h_split, 1)
            for n in range(AHEAD):
                low_part(0, n)

            lg, m1, c1_, f1, l2, m2, f2 = (rt[:, n, :, :] for n in range(7))
            v1, v2 = rt[:, 9, :, 0:1], rt[:, 9, :, 1:2]
            take_unit(dve, ("router", 0))
            last = V.tensor_copy(lg, bank(("router", 0))[:, 0:16].rearrange("p (b e) -> p b e", e=8))
            free_unit(last, ("router", 0))
            evacuated(dve, ("router", 0))

            def first_max(src, dst, tmp, top):
                link(V.reduce_max(top, src, AX_X))
                link(V.tensor_tensor(tmp, src, top.to_broadcast([P, TB, 8]), ALU.is_equal))
                for b in range(TB):
                    last = V.tensor_tensor_scan(c1_[:, b, :], ones[:, 0:8], tmp[:, b, :], 0.0, ALU.mult, ALU.add)
                link(last)
                link(V.tensor_scalar(c1_, c1_, 1.0, None, ALU.is_le))
                link(V.tensor_tensor(dst, tmp, c1_, ALU.mult))

            first_max(lg, f1, m1, v1)
            link(V.scalar_tensor_tensor(l2, f1, -3.0e38, lg, ALU.mult, ALU.add))
            first_max(l2, f2, m2, v2)
            V.tensor_tensor(rt[:, 7, :, 0:1], v2, v1, ALU.subtract).then_inc(rexp_in, 1)
            dve.wait_ge(rexp_out, 1)
            ex, den, w1, w2 = rt[:, 8, :, 0:1], rt[:, 10, :, 0:1], rt[:, 10, :, 1:2], rt[:, 10, :, 2:3]
            link(V.tensor_scalar(den, ex, 1.0, None, ALU.add))
            link(V.reciprocal(w1, den))
            link(V.tensor_tensor(w2, ex, w1, ALU.mult))
            V.tensor_tensor(mask, f1, f2, ALU.add).then_inc(mask_ready, 1)
            V.tensor_tensor(f1, f1, w1.to_broadcast([P, TB, 8]), ALU.mult)
            link(V.tensor_tensor(f2, f2, w2.to_broadcast([P, TB, 8]), ALU.mult))
            link(V.tensor_tensor(pass_w[:, :, 0:8], f1, f2, ALU.add))
            take_unit(dve, ("pos", 0))
            pos = bank(("pos", 0))
            V.scalar_tensor_tensor(l2, pos[:, 0:16].rearrange("p (b e) -> p b e", e=8), 1.0, mask, ALU.add, ALU.mult)
            last = V.tensor_copy(m2[:, 0, :], pos[:, 16:24])
            free_unit(last, ("pos", 0))
            evacuated(dve, ("pos", 0))
            V.tensor_scalar(pass_pos[:, :, 0:8], l2, -1.0, None, ALU.add)
            link(V.tensor_scalar(m2[:, 0, :], m2[:, 0, :], float(CAP), None, ALU.is_gt))
            link(V.tensor_tensor_scan(m2[:, 1, :], ones[:, 0:8], m2[:, 0, :], 0.0, ALU.mult, ALU.add))
            n_x = PASSES - MOE_E
            sel, prod = over[:, 0, :, :], over[:, 1, :, :]
            for j in range(n_x):
                last = V.scalar_tensor_tensor(sel[:, j, :], m2[:, 1, :], float(j + 1), m2[:, 0, :],
                                              ALU.is_equal, ALU.mult)
            link(last)
            link(V.tensor_scalar(c1_, l2, -float(CAP), None, ALU.add))
            red = over[:, 3, 0, 0:n_x]
            for b in range(TB):
                link(V.tensor_tensor(prod, sel, c1_[:, b, :].unsqueeze(1).to_broadcast([P, n_x, 8]), ALU.mult))
                link(V.tensor_reduce(red, prod, AX_X, ALU.add))
                link(V.tensor_scalar(pass_pos[:, b, MOE_E:], red, -1.0, None, ALU.add))
                link(V.tensor_tensor(prod, sel, pass_w[:, b, 0:8].unsqueeze(1).to_broadcast([P, n_x, 8]), ALU.mult))
                link(V.tensor_reduce(pass_w[:, b, MOE_E:], prod, AX_X, ALU.add))
            link(V.tensor_tensor(prod, sel, iota[:, 0:8].unsqueeze(1).to_broadcast([P, n_x, 8]), ALU.mult))
            link(V.tensor_reduce(red, prod, AX_X, ALU.add))
            V.tensor_copy(table[:, 2:2 + n_x], red)
            V.tensor_scalar(table[:, 0:1], m2[:, 1, 7:8], float(MOE_E), None, ALU.add)
            V.tensor_copy(table[:, 1:2], m2[:, 1, 7:8]).then_inc(table_ready, 1)

            def build_pick(n, col):
                for b in range(TB):
                    last = V.tensor_scalar(pick[:, b, :], iota, col(b), None, ALU.is_equal)
                last.then_inc(pick_ready, 1)

            def move_xe(n):
                dve.wait_ge(xe_high, n)
                V.tensor_tensor(xe_l[:, :, :].rearrange("p (b k) m -> p b (k m)", b=2), psum[:, 6:8, :],
                                xe_h[:, :, :].rearrange("p (b k) m -> p b (k m)", b=2).bitcast(F32),
                                ALU.subtract).then_inc(xe_split, 1)

            build_pick(0, lambda b: pass_pos[:, b, 0:1])
            for b in range(TB):
                for c in range(2):
                    V.tensor_scalar(ysum[:, b, c * 512:(c + 1) * 512], h[:, b, c * 512:(c + 1) * 512], ALPHA, None,
                                    ALU.mult).then_inc(y_added, 1)
            move_xe(1)
            f0 = ff0["moe"]
            chunks, after = moe_events()
            dve.wait_ge(table_ready, 1)
            n_pass = dve.value_load(table[0:1, 0:1], min_val=MOE_E, max_val=MOE_E + OVER)
            with dve.Fori(0, n_pass) as p:
                for n in range(-1, len(chunks)):
                    for what, s in after.get(n, []):
                        if what == "prod":
                            dve.wait_ge(silu_ready, p * MOE_PER + (f0 + s + 1))
                            V.tensor_tensor(e_h[:, s % 2, :], e_silu[:, s % 2, :], psum[:, s % 2, 256:512],
                                            ALU.mult).then_inc(hT_ready, 1)
                            if s == 2:
                                dve.wait_ge(gathered, p + 1)
                                dve.wait_ge(pickT_full, p + 1)
                                build_pick(p, lambda b: pass_pos[:, b, bass.ds(p + 1, 1)])
                        else:
                            dve.wait_ge(hT_high, p * MOE_PER + (s + 1))
                            V.tensor_tensor(eT_l[:, s % 2, :, :],
                                            halves(psum[:, 2, 256 * (s % 2):256 * (s % 2) + 256]),
                                            eT_h[:, s % 2, :, :].bitcast(F32), ALU.subtract).then_inc(hT_moved, 1)
                    if n == len(chunks) - 2:
                        move_xe(p + 2)
                    if n + SPLITS < len(chunks) + AHEAD:
                        low_part(p, n + SPLITS)
                dve.wait_ge(oe_high, p + 1)
                V.tensor_tensor(o_l[:, :, :], psum[:, 4:6, :], o_h[:, :, :].bitcast(F32),
                                ALU.subtract).then_inc(oe_split, 1)
                for b in range(TB):
                    for c in range(2):
                        dve.wait_ge(scattered, p * 4 + (2 * b + c + 1))
                        ys = ysum[:, b, c * 512:(c + 1) * 512]
                        V.scalar_tensor_tensor(ys, psum[:, 4 * b + c, :], pass_w[:, b, bass.ds(p, 1)], ys,
                                               ALU.mult, ALU.add).then_inc(y_added, 1)
            dve.wait_ge(loads["ln2"], 64)
            dve.wait_ge(y_added, n_pass * 4 + 4)
            layer_norm(ysum, bc[:, 2, :], bc[:, 3, :], LN_EPS).then_inc(out_ready, 1)


def weight_stream(w):
    out = np.empty((len(CHUNKS), P, CHUNK_F), np.float32)
    for n, (kind, name, i) in enumerate(CHUNKS):
        m = w[name]
        if m.ndim == 3:
            per = MOE_PER
            m, i = m[i // per], i % per
        if kind == "k2":
            out[n] = m[256 * i:256 * i + 256].reshape(2, P, D).transpose(1, 0, 2).reshape(P, CHUNK_F)
        else:
            k, cols = (KD, 256) if kind == "k8" else (4, 512)
            part = m[:, cols * i:cols * (i + 1)]
            out[n] = part.reshape(k, P, cols).transpose(1, 0, 2).reshape(P, CHUNK_F)
    return out


def pair_heads():
    return np.concatenate([np.arange(64) + 64 * hd for i in range(4) for hd in (i, i + 4)])


def na_bias_layout(rpb):
    q, k = np.arange(TOK)[:, None], np.arange(TOK)[None, :]
    qr, qc, kr, kc = q // 64, q % 64, k // 64, k % 64
    start = np.clip(qc - 8, 0, 48)
    valid = (kc >= start) & (kc < start + 16)
    dr, dc = kr - qr + 7, np.clip(kc - qc + 15, 0, 30)
    out = np.where(valid[None], rpb[:, dr, dc], np.float32(-1e30))
    return out.reshape(8, TB, P, TOK).transpose(2, 0, 1, 3)


def layout(i):
    f = {k: np.asarray(v) for k, v in i.items()}
    per = pair_heads()
    w = {"w_in": np.concatenate([f["w_in"][0][:, :512], f["w_in"][0][:, 1536:2560],
                                 f["w_in"][0][:, 512:1536], f["w_in"][0][:, 2560:]], 1)}
    for n in ("w_k", "w_v", "w_q", "w_xo", "w_out", "w_proj_a", "w_proj_b", "s5_w_glu"):
        w[n] = f[n][0]
    w["ffn_gate"], w["ffn_up"], w["ffn_down"] = f["w_gate"][0], f["w_up"][0], f["w_down"][0]
    w["dense_gate"], w["dense_up"], w["dense_down"] = (f[f"ffn_w_{n}_2"][0] for n in ("gate", "up", "down"))
    w["moe_gate"], w["moe_up"], w["moe_down"] = (f[f"moe_w_{n}_2"][0] for n in ("gate", "up", "down"))
    for m in range(2):
        x = f["w_in_2"][m]
        w[f"w_in_{m}"] = np.concatenate([x[:, 1024:1536], x[:, 1536:2048][:, per], x[:, 2048:2304],
                                         x[:, 0:1024], x[:, 2304:]], 1)
        w[f"w_na_{m}"] = f["w_branch_na_2"][m]
        w[f"w_sw_{m}"] = f["w_branch_sw_2"][m][per]
        w[f"w_out_{m}"] = f["w_out_2"][m]

    def col(v):
        return v.reshape(-1, P).T

    def states(v):
        v = v.reshape(2, PAIRS, 2, S5_P, *v.shape[3:])
        return np.moveaxis(v, (2, 3), (0, 1)).reshape(P, BLK, *v.shape[4:])

    step = np.broadcast_to(f["s5_log_step"][0][:, :, None], (2, S5_G, S5_P))
    s5_c = np.zeros((P, 2, BLK, 2, S5_C), np.float32)
    for r, n in enumerate(("s5_c_re", "s5_c_im")):
        c = states(f[n][0].transpose(0, 1, 3, 2))
        for g in range(2):
            s5_c[64 * g:64 * g + 64, r, :, g, :] = c[64 * g:64 * g + 64]
    pos = np.arange(TOK, dtype=np.float32)
    inv = (1.0 / (500000.0 ** (np.arange(0, 16, 2, dtype=np.float32) / 16))).astype(np.float32)
    ang = pos[:, None] * inv[None, :]
    rope = np.stack([np.cos(ang), np.sin(ang)], 1).astype(np.float32).reshape(TB, P, 2, 8).transpose(1, 0, 2, 3)
    q, k = np.arange(TOK)[:, None], np.arange(TOK)[None, :]
    band = np.where(np.abs(q - k) <= 128, 0.0, -1e30).astype(np.float32).reshape(TB, P, TOK).transpose(1, 0, 2)
    return {
        "x": f["x"], "mem": f["mem"], "stream": weight_stream(w),
        "ident": np.eye(P, dtype=np.float32),
        "gains": np.stack([col(f["mix_norm_g"][0]), col(f["mem_norm_g"]), col(f["xattn_norm_g"][0]),
                           col(f["ffn_norm_g"][0])], 1),
        "s5_prm": np.stack([states(f["s5_lam_re"][0]), states(f["s5_lam_im"][0]), states(step)], 1),
        "s5_b": np.stack([states(f["s5_b_re"][0]), states(f["s5_b_im"][0])], 1),
        "s5_c": s5_c.reshape(P, 2, BLK, 32),
        "s5_d": col(f["s5_d"][0]),
        "sgu_ln": np.concatenate([f["sgu_ln_g"], f["sgu_ln_b"]], 0),
        "sgu_w": f["sgu_w"][0].transpose(2, 0, 1),
        "sgu_bias": f["sgu_bias"][0].reshape(1, -1),
        "b_gate": np.stack([col(f["b_gate_2"][m]) for m in range(2)], 1),
        "sink": f["sw_sink_2"],
        "na_bias": np.stack([na_bias_layout(f["na_rpb_2"][m]) for m in range(2)]),
        "sw_mask": band, "rope": rope,
        "before": np.triu(np.ones((P, P), np.float32), 1),
        "iota": np.broadcast_to(np.arange(P, dtype=np.float32), (P, P)),
        "router": f["moe_router_2"][0].reshape(KD, P, 8).transpose(1, 0, 2),
        "bc": np.stack([f["final_norm_g"], f["emb_ln_g_2"], f["emb_ln_b_2"]]
                       + [f[n][m] for m in range(2) for n in ("ln1_g_2", "ln1_b_2", "ln2_g_2", "ln2_b_2")]),
    }


def kernel(**inputs):
    import concourse.bacc as _bacc
    from concourse.bass_utils import run_bass_kernel_spmd as _run

    nc = _bacc.Bacc("TRN2", target_bir_lowering=False, num_devices=1)
    arrays, aps = {}, {}
    for name, v in layout(inputs).items():
        arrays["in_" + name] = np.ascontiguousarray(v)
        aps[name] = nc.dram_tensor("in_" + name, v.shape, mybir.dt.from_np(v.dtype), kind="ExternalInput").ap()
    out = nc.dram_tensor("out_dram", (1, TOK, D), F32, kind="ExternalOutput").ap()
    build(nc, aps, out)
    r = _run(nc, [arrays], core_ids=[0])
    return r.results[0]["out_dram"]
```
